# Optimizing a Trainium2 kernel written in Bass

```python
import math
import jax, jax.numpy as jnp
from jax import lax
import numpy as np

D_MODEL = 1024
BATCH = 1
SEQ = 512
DEPTH = 2

N_MEM = 256
NORM_EPS = 1e-6
NEG_INF = -1e30
ATTN_BLOCK = 128

LRU_WIDTH = 1024
LRU_BLOCKS = 16
LRU_BLOCK_DIM = LRU_WIDTH // LRU_BLOCKS
CONV_WIDTH = 4
LRU_C = 8.0
LRU_A_MIN = 0.9
LRU_A_MAX = 0.999

DIL_GROUPS = ((128, 1), (512, 4), (2048, 16))
DIL_HEADS = 4
DIL_HEAD_DIM = 128
DIL_WIDTH = DIL_HEADS * DIL_HEAD_DIM
DIL_QKV = len(DIL_GROUPS) * DIL_WIDTH

MEM_HEADS = 4
MEM_HEAD_DIM = 64
MEM_WIDTH = MEM_HEADS * MEM_HEAD_DIM

NSA_HEADS = 16
NSA_KV_GROUPS = 2
NSA_HEADS_PER_GROUP = NSA_HEADS // NSA_KV_GROUPS
NSA_HEAD_DIM = 64
NSA_WIDTH = NSA_HEADS * NSA_HEAD_DIM
NSA_KV = NSA_KV_GROUPS * NSA_HEAD_DIM
CMP_BLOCK = 32
CMP_STRIDE = 16
SLC_BLOCK = 64
SLC_TOP_N = 8
WIN_SIZE = 512
PHI_HIDDEN = 256
SEL_FORCE = 1e6

N_EVEN = (DEPTH + 1) // 2
N_ODD = DEPTH // 2

HAWK_IN_SPLITS = (LRU_WIDTH, LRU_WIDTH, DIL_QKV, DIL_QKV, DIL_QKV, DIL_WIDTH, MEM_WIDTH, MEM_WIDTH)
HAWK_IN = sum(HAWK_IN_SPLITS)
HAWK_OUT = LRU_WIDTH + DIL_WIDTH + MEM_WIDTH
NSA_IN_SPLITS = (NSA_WIDTH, 6 * NSA_KV, 3 * NSA_HEADS, NSA_WIDTH, MEM_WIDTH, MEM_WIDTH)
NSA_IN = sum(NSA_IN_SPLITS)
NSA_OUT = NSA_WIDTH + MEM_WIDTH


def rms_norm(x, g):
    xf = x.astype(jnp.float32)
    y = xf * lax.rsqrt(jnp.mean(xf * xf, axis=-1, keepdims=True) + NORM_EPS)
    return (y * g.astype(jnp.float32)).astype(x.dtype)

def split_cols(h, sizes):
    return jnp.split(h, np.cumsum(sizes)[:-1].tolist(), axis=-1)

def alibi_slopes(n):
    return np.exp2(-8.0 * np.arange(1, n + 1) / n).astype(np.float32)

def banded_attention(q, k, v, slopes, max_dist, pos_scale):
    n, g, r, length, hd = q.shape
    blk = ATTN_BLOCK
    nb = -(-length // blk)
    pad_end = nb * blk - length
    p = -(-max_dist // blk)
    width = (p + 1) * blk
    q = jnp.pad(q, ((0, 0), (0, 0), (0, 0), (0, pad_end), (0, 0)))
    k = jnp.pad(k, ((0, 0), (0, 0), (p * blk, pad_end), (0, 0))).reshape(n, g, nb + p, blk, hd)
    v = jnp.pad(v, ((0, 0), (0, 0), (p * blk, pad_end), (0, 0))).reshape(n, g, nb + p, blk, hd)
    k_win = jnp.concatenate([k[:, :, i:i + nb] for i in range(p + 1)], axis=3).transpose(2, 0, 1, 3, 4)
    v_win = jnp.concatenate([v[:, :, i:i + nb] for i in range(p + 1)], axis=3).transpose(2, 0, 1, 3, 4)
    q_blk = q.reshape(n, g, r, nb, blk, hd).transpose(3, 0, 1, 2, 4, 5)
    dist = p * blk + np.arange(blk)[:, None] - np.arange(width)[None, :]
    key_idx = (np.arange(nb)[:, None] - p) * blk + np.arange(width)[None, :]
    valid = (dist >= 0)[None] & (dist <= max_dist)[None] & (key_idx >= 0)[:, None, :]
    bias = -(slopes[:, :, None, None] * (dist * pos_scale).astype(np.float32)[None, None])
    scale = hd ** -0.5

    def one_block(args):
        qb, kb, vb, ok = args
        s = jnp.einsum('ngrqd,ngkd->ngrqk', qb, kb, preferred_element_type=jnp.float32) * scale + bias
        s = jnp.where(ok, s, NEG_INF)
        m = jnp.max(s, axis=-1, keepdims=True)
        e = jnp.exp(s - m)
        den = jnp.sum(e, axis=-1, keepdims=True)
        o = jnp.einsum('ngrqk,ngkd->ngrqd', (e / den).astype(vb.dtype), vb,
                       preferred_element_type=jnp.float32)
        return o.astype(qb.dtype), (m + jnp.log(den))[..., 0]

    o, lse = lax.map(one_block, (q_blk, k_win, v_win, jnp.asarray(valid)))
    o = o.transpose(1, 2, 3, 0, 4, 5).reshape(n, g, r, nb * blk, hd)[:, :, :, :length]
    lse = lse.transpose(1, 2, 3, 0, 4).reshape(n, g, r, nb * blk)[..., :length]
    return o, lse

def dilated_attention(q, k, v):
    b, s, _, hd = q.shape
    slopes_all = alibi_slopes(len(DIL_GROUPS) * DIL_HEADS).reshape(len(DIL_GROUPS), DIL_HEADS)
    outs, lses = [], []
    for gi, (window, dil) in enumerate(DIL_GROUPS):
        sub = s // dil

        def to_sub(t):
            t = t[:, :, gi * DIL_HEADS:(gi + 1) * DIL_HEADS]
            return t.reshape(b, sub, dil, DIL_HEADS, hd).transpose(0, 2, 3, 1, 4).reshape(
                b * dil, DIL_HEADS, sub, hd)

        o, lse = banded_attention(to_sub(q)[:, :, None], to_sub(k), to_sub(v),
                                  slopes_all[gi][:, None], window // dil, dil)
        outs.append(o[:, :, 0].reshape(b, dil, DIL_HEADS, sub, hd).transpose(0, 3, 1, 2, 4).reshape(
            b, s, DIL_HEADS, hd))
        lses.append(lse[:, :, 0].reshape(b, dil, DIL_HEADS, sub).transpose(0, 3, 1, 2).reshape(
            b, s, DIL_HEADS))
    w = jax.nn.softmax(jnp.stack(lses, axis=0), axis=0)
    o = jnp.einsum('gbsh,gbshd->bshd', w, jnp.stack(outs, axis=0).astype(jnp.float32))
    return o.astype(q.dtype)

def causal_depthwise_conv(x, w, bias):
    y = lax.conv_general_dilated(x, w[:, None, :], window_strides=(1,),
                                 padding=((CONV_WIDTH - 1, 0),),
                                 dimension_numbers=('NWC', 'WIO', 'NWC'),
                                 feature_group_count=x.shape[-1])
    return y + bias

def rg_lru(x, gate_a_w, gate_a_b, gate_x_w, gate_x_b, lam):
    b, s, w = x.shape
    xb = x.reshape(b, s, LRU_BLOCKS, LRU_BLOCK_DIM)
    r = jax.nn.sigmoid((jnp.einsum('bshi,hij->bshj', xb, gate_a_w) + gate_a_b).astype(jnp.float32)).reshape(b, s, w)
    i = jax.nn.sigmoid((jnp.einsum('bshi,hij->bshj', xb, gate_x_w) + gate_x_b).astype(jnp.float32)).reshape(b, s, w)
    log_a = -LRU_C * r * jax.nn.softplus(-lam.astype(jnp.float32))
    a = jnp.exp(log_a)
    mult = jnp.sqrt(-jnp.expm1(2.0 * log_a))
    mult = jnp.where((jnp.arange(s) == 0)[None, :, None], 1.0, mult)
    u = x.astype(jnp.float32) * i * mult

    def combine(c1, c2):
        a1, b1 = c1
        a2, b2 = c2
        return a1 * a2, a2 * b1 + b2

    _, h = lax.associative_scan(combine, (a, u), axis=1)
    return h.astype(x.dtype)

def memory_attention(q, mem_n, w_mem_kv):
    b, s, _ = q.shape
    k, v = jnp.split(mem_n @ w_mem_kv, 2, axis=-1)
    q = q.reshape(b, s, MEM_HEADS, MEM_HEAD_DIM)
    k = k.reshape(b, -1, MEM_HEADS, MEM_HEAD_DIM)
    v = v.reshape(b, -1, MEM_HEADS, MEM_HEAD_DIM)
    sc = jnp.einsum('bshd,bmhd->bhsm', q, k, preferred_element_type=jnp.float32) * MEM_HEAD_DIM ** -0.5
    p = jax.nn.softmax(sc, axis=-1)
    o = jnp.einsum('bhsm,bmhd->bshd', p.astype(v.dtype), v)
    return o.reshape(b, s, MEM_WIDTH)

def hawk_dilated_layer(x, mem, norm_g, w_in, conv_w, conv_b, ga_w, ga_b, gx_w, gx_b, lam,
                       mem_norm_g, w_mem_kv, w_out):
    b, s, _ = x.shape
    h = rms_norm(x, norm_g) @ w_in
    xa, za, q, k, v, zb, qm, zm = split_cols(h, HAWK_IN_SPLITS)
    ya = rg_lru(causal_depthwise_conv(xa, conv_w, conv_b), ga_w, ga_b, gx_w, gx_b, lam)
    nh = len(DIL_GROUPS) * DIL_HEADS
    shp = (b, s, nh, DIL_HEAD_DIM)
    yb = dilated_attention(q.reshape(shp), k.reshape(shp), v.reshape(shp)).reshape(b, s, DIL_WIDTH)
    ym = memory_attention(qm, rms_norm(mem, mem_norm_g), w_mem_kv)
    y = jnp.concatenate([ya * jax.nn.silu(za), yb * jax.nn.silu(zb), ym * jax.nn.silu(zm)], axis=-1)
    return x + (y.astype(x.dtype) @ w_out)

def compress_tokens(t, pe, w1, w2):
    s, hd = t.shape[2], t.shape[3]
    n_cmp = (s - CMP_BLOCK) // CMP_STRIDE + 1
    idx = np.arange(n_cmp)[:, None] * CMP_STRIDE + np.arange(CMP_BLOCK)[None, :]
    blocks = t[:, :, idx] + pe
    flat = blocks.reshape(blocks.shape[0], blocks.shape[1], n_cmp, CMP_BLOCK * hd)
    return jax.nn.silu(flat @ w1) @ w2

def compressed_attention(q, k, v, slopes):
    s, hd = q.shape[3], q.shape[4]
    n_cmp = k.shape[2]
    block_end = np.arange(n_cmp) * CMP_STRIDE + CMP_BLOCK - 1
    dist = (np.arange(s)[:, None] - block_end[None, :]).astype(np.float32)
    visible = dist >= 0
    bias = -jnp.asarray(slopes)[:, :, None, None] * jnp.asarray(dist)
    sc = jnp.einsum('bgrsd,bgnd->bgrsn', q, k, preferred_element_type=jnp.float32) * hd ** -0.5 + bias
    sc = jnp.where(visible, sc, NEG_INF)
    p = jax.nn.softmax(sc, axis=-1) * visible.any(axis=-1, keepdims=True).astype(np.float32)
    o = jnp.einsum('bgrsn,bgnd->bgrsd', p.astype(v.dtype), v)
    return o, p

def selected_attention(q, k, v, p_cmp, slopes):
    b, g, r, s, hd = q.shape
    n_slc = s // SLC_BLOCK
    top_n = min(SLC_TOP_N, n_slc)
    n_cmp = p_cmp.shape[-1]
    c_start = np.arange(n_cmp)[:, None] * CMP_STRIDE
    s_start = np.arange(n_slc)[None, :] * SLC_BLOCK
    overlap = ((c_start < s_start + SLC_BLOCK) & (c_start + CMP_BLOCK > s_start)).astype(np.float32)
    imp = jnp.einsum('bgrsn,nj->bgsj', p_cmp, overlap)
    cur = (np.arange(s) // SLC_BLOCK)[:, None]
    j = np.arange(n_slc)[None, :]
    forced = (j == 0) | (j == cur) | (j == cur - 1)
    imp = jnp.where(forced, SEL_FORCE, jnp.where(j > cur, -SEL_FORCE, imp))
    _, sel = lax.top_k(imp, top_n)
    nqb = s // ATTN_BLOCK
    k_blocks = k.reshape(b, g, n_slc, SLC_BLOCK, hd)
    v_blocks = v.reshape(b, g, n_slc, SLC_BLOCK, hd)
    q_blk = q.reshape(b, g, r, nqb, ATTN_BLOCK, hd).transpose(3, 0, 1, 2, 4, 5)
    sel_blk = sel.reshape(b, g, nqb, ATTN_BLOCK, top_n).transpose(2, 0, 1, 3, 4)
    qpos_blk = jnp.arange(s, dtype=jnp.int32).reshape(nqb, ATTN_BLOCK)
    bi = jnp.arange(b)[:, None, None]
    gi = jnp.arange(g)[None, :, None]
    slope_b = jnp.asarray(slopes)[None, :, :, None, None]
    n_keys = top_n * SLC_BLOCK

    def one_block(args):
        qb, ib, qpos = args
        flat = ib.reshape(b, g, ATTN_BLOCK * top_n)
        kg = k_blocks[bi, gi, flat].reshape(b, g, ATTN_BLOCK, n_keys, hd)
        vg = v_blocks[bi, gi, flat].reshape(b, g, ATTN_BLOCK, n_keys, hd)
        kpos = (ib[..., None] * SLC_BLOCK + jnp.arange(SLC_BLOCK)).reshape(b, g, ATTN_BLOCK, n_keys)
        dist = (qpos[None, None, :, None] - kpos)[:, :, None]
        sc = jnp.einsum('bgrqd,bgqkd->bgrqk', qb, kg, preferred_element_type=jnp.float32) * hd ** -0.5
        sc = jnp.where(dist >= 0, sc - slope_b * dist.astype(jnp.float32), NEG_INF)
        p = jax.nn.softmax(sc, axis=-1)
        return jnp.einsum('bgrqk,bgqkd->bgrqd', p.astype(vg.dtype), vg)

    o = lax.map(one_block, (q_blk, sel_blk, qpos_blk))
    return o.transpose(1, 2, 3, 0, 4, 5).reshape(b, g, r, s, hd)

def nsa_layer(x, mem, norm_g, w_in, pe_k, pe_v, phik_w1, phik_w2, phiv_w1, phiv_w2,
              mem_norm_g, w_mem_kv, w_out):
    b, s, _ = x.shape
    g, r, hd = NSA_KV_GROUPS, NSA_HEADS_PER_GROUP, NSA_HEAD_DIM
    h = rms_norm(x, norm_g) @ w_in
    q, kv, gate_logits, z, qm, zm = split_cols(h, NSA_IN_SPLITS)
    q = q.reshape(b, s, g, r, hd).transpose(0, 2, 3, 1, 4)
    kc, vc, ks, vs, kw, vw = [t.reshape(b, s, g, hd).transpose(0, 2, 1, 3)
                              for t in jnp.split(kv, 6, axis=-1)]
    slopes = alibi_slopes(NSA_HEADS).reshape(g, r)
    k_cmp = compress_tokens(kc, pe_k, phik_w1, phik_w2)
    v_cmp = compress_tokens(vc, pe_v, phiv_w1, phiv_w2)
    o_cmp, p_cmp = compressed_attention(q, k_cmp, v_cmp, slopes)
    o_slc = selected_attention(q, ks, vs, p_cmp, slopes)
    o_win, _ = banded_attention(q, kw, vw, slopes, WIN_SIZE - 1, 1)
    gates = jax.nn.sigmoid(gate_logits.astype(jnp.float32)).reshape(b, s, g, r, 3).transpose(0, 2, 3, 1, 4)
    o = gates[..., 0:1] * o_cmp + gates[..., 1:2] * o_slc + gates[..., 2:3] * o_win
    o = o.transpose(0, 3, 1, 2, 4).reshape(b, s, NSA_WIDTH).astype(x.dtype)
    ym = memory_attention(qm, rms_norm(mem, mem_norm_g), w_mem_kv)
    y = jnp.concatenate([o * jax.nn.silu(z), ym * jax.nn.silu(zm)], axis=-1)
    return x + (y.astype(x.dtype) @ w_out)

def first_inputs(seed: int = 0) -> dict:
    key = jax.random.key(seed)
    keys = iter(jax.random.split(key, 40))

    def nrm(shape, scale):
        return jax.random.normal(next(keys), shape, jnp.float32) * scale

    def gain(shape):
        return 1.0 + 0.02 * jax.random.normal(next(keys), shape, jnp.float32)

    x = nrm((BATCH, SEQ, D_MODEL), 1.0)
    mem = nrm((BATCH, N_MEM, D_MODEL), 1.0)
    u = jax.random.uniform(next(keys), (N_EVEN, LRU_WIDTH), jnp.float32, LRU_A_MIN, LRU_A_MAX)
    a_base = u ** (1.0 / LRU_C)
    hawk_lambda = jnp.log(a_base) - jnp.log1p(-a_base)
    phi_in = CMP_BLOCK * NSA_HEAD_DIM
    return {
        "x": x,
        "mem": mem,
        "hawk_norm": gain((N_EVEN, D_MODEL)),
        "hawk_w_in": nrm((N_EVEN, D_MODEL, HAWK_IN), D_MODEL ** -0.5),
        "hawk_conv_w": nrm((N_EVEN, CONV_WIDTH, LRU_WIDTH), CONV_WIDTH ** -0.5),
        "hawk_conv_b": nrm((N_EVEN, LRU_WIDTH), 0.02),
        "hawk_gate_a_w": nrm((N_EVEN, LRU_BLOCKS, LRU_BLOCK_DIM, LRU_BLOCK_DIM), LRU_BLOCK_DIM ** -0.5),
        "hawk_gate_a_b": nrm((N_EVEN, LRU_BLOCKS, LRU_BLOCK_DIM), 0.02),
        "hawk_gate_x_w": nrm((N_EVEN, LRU_BLOCKS, LRU_BLOCK_DIM, LRU_BLOCK_DIM), LRU_BLOCK_DIM ** -0.5),
        "hawk_gate_x_b": nrm((N_EVEN, LRU_BLOCKS, LRU_BLOCK_DIM), 0.02),
        "hawk_lambda": hawk_lambda,
        "hawk_mem_norm": gain((N_EVEN, D_MODEL)),
        "hawk_w_mem_kv": nrm((N_EVEN, D_MODEL, 2 * MEM_WIDTH), D_MODEL ** -0.5),
        "hawk_w_out": nrm((N_EVEN, HAWK_OUT, D_MODEL), HAWK_OUT ** -0.5),
        "nsa_norm": gain((N_ODD, D_MODEL)),
        "nsa_w_in": nrm((N_ODD, D_MODEL, NSA_IN), D_MODEL ** -0.5),
        "nsa_pe_k": nrm((N_ODD, CMP_BLOCK, NSA_HEAD_DIM), 0.1),
        "nsa_pe_v": nrm((N_ODD, CMP_BLOCK, NSA_HEAD_DIM), 0.1),
        "nsa_phi_k_w1": nrm((N_ODD, phi_in, PHI_HIDDEN), phi_in ** -0.5),
        "nsa_phi_k_w2": nrm((N_ODD, PHI_HIDDEN, NSA_HEAD_DIM), PHI_HIDDEN ** -0.5),
        "nsa_phi_v_w1": nrm((N_ODD, phi_in, PHI_HIDDEN), phi_in ** -0.5),
        "nsa_phi_v_w2": nrm((N_ODD, PHI_HIDDEN, NSA_HEAD_DIM), PHI_HIDDEN ** -0.5),
        "nsa_mem_norm": gain((N_ODD, D_MODEL)),
        "nsa_w_mem_kv": nrm((N_ODD, D_MODEL, 2 * MEM_WIDTH), D_MODEL ** -0.5),
        "nsa_w_out": nrm((N_ODD, NSA_OUT, D_MODEL), NSA_OUT ** -0.5),
        "final_norm": gain((D_MODEL,)),
    }

def first_block(x, mem, hawk_norm, hawk_w_in, hawk_conv_w, hawk_conv_b, hawk_gate_a_w, hawk_gate_a_b,
              hawk_gate_x_w, hawk_gate_x_b, hawk_lambda, hawk_mem_norm, hawk_w_mem_kv, hawk_w_out,
              nsa_norm, nsa_w_in, nsa_pe_k, nsa_pe_v, nsa_phi_k_w1, nsa_phi_k_w2, nsa_phi_v_w1,
              nsa_phi_v_w2, nsa_mem_norm, nsa_w_mem_kv, nsa_w_out, final_norm):
    for layer in range(DEPTH):
        i = layer // 2
        if layer % 2 == 0:
            x = hawk_dilated_layer(x, mem, hawk_norm[i], hawk_w_in[i], hawk_conv_w[i], hawk_conv_b[i],
                                   hawk_gate_a_w[i], hawk_gate_a_b[i], hawk_gate_x_w[i], hawk_gate_x_b[i],
                                   hawk_lambda[i], hawk_mem_norm[i], hawk_w_mem_kv[i], hawk_w_out[i])
        else:
            x = nsa_layer(x, mem, nsa_norm[i], nsa_w_in[i], nsa_pe_k[i], nsa_pe_v[i], nsa_phi_k_w1[i],
                          nsa_phi_k_w2[i], nsa_phi_v_w1[i], nsa_phi_v_w2[i], nsa_mem_norm[i],
                          nsa_w_mem_kv[i], nsa_w_out[i])
    return rms_norm(x, final_norm)


MEM_LEN = 256
DA_HEADS = 8
DA_HEAD_DIM = 64
DA_V_DIM = 2 * DA_HEAD_DIM
DA_WIDTH = DA_HEADS * DA_V_DIM
QK_WIDTH = DA_HEADS * 2 * DA_HEAD_DIM
LAMBDA_INIT_SCALE = 0.1
CONV_WIDTH_2 = 512
CONV_K = 3
MEM_HEAD_DIM_2 = 128
MEM_WIDTH_2 = MEM_HEADS * MEM_HEAD_DIM_2
N_BRANCH = 3
ROPE_THETA = 10000.0
Q_BLOCK = 128
N_EXPERTS = 16
N_GROUPS = 4
EXPERTS_PER_GROUP = N_EXPERTS // N_GROUPS
TOP_K = 2
D_FF_EXPERT = 512
EXPERT_BLOCK = 128
LN_EPS = 1e-5
RMS_EPS = 1e-5
DEEPNORM_ALPHA = (2 * DEPTH) ** 0.25
DEEPNORM_BETA = (8 * DEPTH) ** -0.25

IN_SIZES = (QK_WIDTH, QK_WIDTH, DA_WIDTH, CONV_WIDTH_2, CONV_WIDTH_2, CONV_WIDTH_2, MEM_WIDTH_2, N_BRANCH * D_MODEL)
IN_COLS = sum(IN_SIZES)
IN_SPLITS = tuple(sum(IN_SIZES[:i + 1]) for i in range(len(IN_SIZES) - 1))


def layer_norm(x, g, b):
    x32 = x.astype(jnp.float32)
    mu = jnp.mean(x32, axis=-1, keepdims=True)
    var = jnp.mean(jnp.square(x32 - mu), axis=-1, keepdims=True)
    y = (x32 - mu) * lax.rsqrt(var + LN_EPS) * g.astype(jnp.float32) + b.astype(jnp.float32)
    return y.astype(x.dtype)

def rope(t, cos, sin):
    half = t.shape[-1] // 2
    t1, t2 = t[..., :half], t[..., half:]
    cos = cos.astype(t.dtype)
    sin = sin.astype(t.dtype)
    return jnp.concatenate([t1 * cos - t2 * sin, t2 * cos + t1 * sin], axis=-1)

def diff_attention(q, k, v, lam, lam_init, subln_g):
    B, S = q.shape[0], q.shape[1]
    qh = jnp.transpose(q, (0, 2, 3, 1, 4))
    kh = jnp.transpose(k, (0, 2, 3, 1, 4))
    vh = jnp.transpose(v, (0, 2, 1, 3))
    scale = DA_HEAD_DIM ** -0.5
    outs = []
    for blk in range(S // Q_BLOCK):
        s0 = blk * Q_BLOCK
        end = s0 + Q_BLOCK
        qb = qh[:, :, :, s0:end]
        kb = kh[:, :, :, :end]
        sc = jnp.einsum('bhcqd,bhckd->bhcqk', qb, kb).astype(jnp.float32) * scale
        causal = jnp.arange(end)[None, :] <= (s0 + jnp.arange(Q_BLOCK))[:, None]
        sc = jnp.where(causal, sc, -jnp.inf)
        p = jax.nn.softmax(sc, axis=-1)
        a = p[:, :, 0] - lam * p[:, :, 1]
        outs.append(jnp.einsum('bhqk,bhkd->bhqd', a.astype(v.dtype), vh[:, :, :end]))
    o = jnp.concatenate(outs, axis=2).astype(jnp.float32)
    o = o * lax.rsqrt(jnp.mean(jnp.square(o), axis=-1, keepdims=True) + RMS_EPS)
    o = o * subln_g.astype(jnp.float32) * (1.0 - lam_init)
    o = jnp.transpose(o, (0, 2, 1, 3)).astype(v.dtype)
    return o.reshape(B, S, DA_WIDTH)

def short_gated_conv(bg, cg, u, w):
    z = cg * u
    S = z.shape[1]
    zp = jnp.pad(z, ((0, 0), (CONV_K - 1, 0), (0, 0)))
    y = w[0] * zp[:, 0:S]
    for tap in range(1, CONV_K):
        y = y + w[tap] * zp[:, tap:tap + S]
    return bg * y

def memory_attention_2(qm, mem, w_kv):
    B, S = qm.shape[0], qm.shape[1]
    M = mem.shape[1]
    kv = mem @ w_kv
    km = kv[..., :MEM_WIDTH_2].reshape(B, M, MEM_HEADS, MEM_HEAD_DIM_2)
    vm = kv[..., MEM_WIDTH_2:].reshape(B, M, MEM_HEADS, MEM_HEAD_DIM_2)
    q = qm.reshape(B, S, MEM_HEADS, MEM_HEAD_DIM_2)
    sc = jnp.einsum('bshd,bmhd->bhsm', q, km).astype(jnp.float32) * (MEM_HEAD_DIM_2 ** -0.5)
    p = jax.nn.softmax(sc, axis=-1)
    o = jnp.einsum('bhsm,bmhd->bshd', p.astype(vm.dtype), vm)
    return o.reshape(B, S, MEM_WIDTH_2)

def grouped_moe(x2d, w_router, router_bias, w_gate, w_up, w_down):
    T, D = x2d.shape
    logits = (x2d @ w_router).astype(jnp.float32) + router_bias.astype(jnp.float32)
    scores = jax.nn.softmax(logits, axis=-1)
    grouped = scores.reshape(T, N_GROUPS, EXPERTS_PER_GROUP)
    g_idx = jnp.argmax(jnp.max(grouped, axis=-1), axis=-1)
    in_group = jnp.take_along_axis(grouped, g_idx[:, None, None], axis=1)[:, 0]
    top_vals, top_idx = lax.top_k(in_group, TOP_K)
    experts = g_idx[:, None] * EXPERTS_PER_GROUP + top_idx
    weights = top_vals / jnp.sum(top_vals, axis=-1, keepdims=True)

    A = T * TOP_K
    e_flat = experts.reshape(A).astype(jnp.int32)
    tok_flat = jnp.repeat(jnp.arange(T, dtype=jnp.int32), TOP_K)
    gate_flat = weights.reshape(A).astype(x2d.dtype)
    order = jnp.argsort(e_flat)
    e_sorted = e_flat[order]
    counts = jnp.zeros((N_EXPERTS,), jnp.int32).at[e_flat].add(1)
    start = jnp.cumsum(counts) - counts
    padded = ((counts + EXPERT_BLOCK - 1) // EXPERT_BLOCK) * EXPERT_BLOCK
    pad_end = jnp.cumsum(padded)
    pad_start = pad_end - padded
    dest = pad_start[e_sorted] + (jnp.arange(A, dtype=jnp.int32) - start[e_sorted])
    P = ((A + EXPERT_BLOCK - 1) // EXPERT_BLOCK) * EXPERT_BLOCK + N_EXPERTS * EXPERT_BLOCK
    n_blocks = P // EXPERT_BLOCK
    buf_tok = jnp.full((P,), T, jnp.int32).at[dest].set(tok_flat[order])
    buf_gate = jnp.zeros((P,), x2d.dtype).at[dest].set(gate_flat[order])
    blk_start = jnp.arange(n_blocks, dtype=jnp.int32) * EXPERT_BLOCK
    blk_expert = jnp.minimum(jnp.searchsorted(pad_end, blk_start, side='right'), N_EXPERTS - 1).astype(jnp.int32)
    x_pad = jnp.concatenate([x2d, jnp.zeros((1, D), x2d.dtype)], axis=0)
    xb = x_pad[buf_tok].reshape(n_blocks, EXPERT_BLOCK, D)

    def expert_block(args):
        xblk, e = args
        h = jax.nn.silu(xblk @ w_gate[e]) * (xblk @ w_up[e])
        return h @ w_down[e]

    yb = lax.map(expert_block, (xb, blk_expert))
    y = yb.reshape(P, D) * buf_gate[:, None]
    return jax.ops.segment_sum(y, buf_tok, num_segments=T + 1)[:T]

def second_inputs(seed: int = 0) -> dict:
    key = jax.random.key(seed)
    ks = jax.random.split(key, 26)
    f32 = jnp.float32

    def nrm(k, shape, fan_in, scale=1.0):
        return jax.random.normal(k, shape, f32) * (scale * fan_in ** -0.5)

    x = jax.random.normal(ks[0], (BATCH, SEQ, D_MODEL), f32)
    mem = jax.random.normal(ks[1], (BATCH, MEM_LEN, D_MODEL), f32)
    positions = (jax.random.randint(ks[2], (BATCH, 1), 0, 4096, jnp.int32)
                 + jnp.arange(SEQ, dtype=jnp.int32)[None, :])
    col_scale = jnp.concatenate([
        jnp.ones((2 * QK_WIDTH,), f32),
        jnp.full((DA_WIDTH,), DEEPNORM_BETA, f32),
        jnp.ones((IN_COLS - 2 * QK_WIDTH - DA_WIDTH,), f32)])
    w_in = nrm(ks[3], (DEPTH, D_MODEL, IN_COLS), D_MODEL) * col_scale
    lambda_q1 = LAMBDA_INIT_SCALE * jax.random.normal(ks[4], (DEPTH, DA_HEAD_DIM), f32)
    lambda_k1 = LAMBDA_INIT_SCALE * jax.random.normal(ks[5], (DEPTH, DA_HEAD_DIM), f32)
    lambda_q2 = LAMBDA_INIT_SCALE * jax.random.normal(ks[6], (DEPTH, DA_HEAD_DIM), f32)
    lambda_k2 = LAMBDA_INIT_SCALE * jax.random.normal(ks[7], (DEPTH, DA_HEAD_DIM), f32)
    diff_subln_g = 1.0 + 0.02 * jax.random.normal(ks[8], (DEPTH, DA_V_DIM), f32)
    conv_w = nrm(ks[9], (DEPTH, CONV_K, CONV_WIDTH_2), CONV_K)
    w_mem_kv = nrm(ks[10], (DEPTH, D_MODEL, 2 * MEM_WIDTH_2), D_MODEL)
    w_br_attn = nrm(ks[11], (DEPTH, DA_WIDTH, D_MODEL), DA_WIDTH, DEEPNORM_BETA)
    w_br_conv = nrm(ks[12], (DEPTH, CONV_WIDTH_2, D_MODEL), CONV_WIDTH_2, DEEPNORM_BETA)
    w_br_mem = nrm(ks[13], (DEPTH, MEM_WIDTH_2, D_MODEL), MEM_WIDTH_2, DEEPNORM_BETA)
    w_out = nrm(ks[14], (DEPTH, D_MODEL, D_MODEL), D_MODEL, DEEPNORM_BETA)
    ln1_g = 1.0 + 0.02 * jax.random.normal(ks[15], (DEPTH, D_MODEL), f32)
    ln1_b = 0.02 * jax.random.normal(ks[16], (DEPTH, D_MODEL), f32)
    ln2_g = 1.0 + 0.02 * jax.random.normal(ks[17], (DEPTH, D_MODEL), f32)
    ln2_b = 0.02 * jax.random.normal(ks[18], (DEPTH, D_MODEL), f32)
    w_router = nrm(ks[19], (D_MODEL, N_EXPERTS), D_MODEL)
    router_bias = 0.01 * jax.random.normal(ks[20], (N_EXPERTS,), f32)
    w_exp_gate = nrm(ks[21], (DEPTH, N_EXPERTS, D_MODEL, D_FF_EXPERT), D_MODEL, DEEPNORM_BETA)
    w_exp_up = nrm(ks[22], (DEPTH, N_EXPERTS, D_MODEL, D_FF_EXPERT), D_MODEL, DEEPNORM_BETA)
    w_exp_down = nrm(ks[23], (DEPTH, N_EXPERTS, D_FF_EXPERT, D_MODEL), D_FF_EXPERT, DEEPNORM_BETA)
    return {'x': x, 'mem': mem, 'positions': positions, 'w_in': w_in,
            'lambda_q1': lambda_q1, 'lambda_k1': lambda_k1, 'lambda_q2': lambda_q2, 'lambda_k2': lambda_k2,
            'diff_subln_g': diff_subln_g, 'conv_w': conv_w, 'w_mem_kv': w_mem_kv,
            'w_br_attn': w_br_attn, 'w_br_conv': w_br_conv, 'w_br_mem': w_br_mem, 'w_out': w_out,
            'ln1_g': ln1_g, 'ln1_b': ln1_b, 'ln2_g': ln2_g, 'ln2_b': ln2_b,
            'w_router': w_router, 'router_bias': router_bias,
            'w_exp_gate': w_exp_gate, 'w_exp_up': w_exp_up, 'w_exp_down': w_exp_down}

def second_block(x, mem, positions, w_in, lambda_q1, lambda_k1, lambda_q2, lambda_k2, diff_subln_g,
              conv_w, w_mem_kv, w_br_attn, w_br_conv, w_br_mem, w_out,
              ln1_g, ln1_b, ln2_g, ln2_b, w_router, router_bias,
              w_exp_gate, w_exp_up, w_exp_down):
    B, S, D = x.shape
    inv_freq = ROPE_THETA ** (-jnp.arange(0, DA_HEAD_DIM, 2, dtype=jnp.float32) / DA_HEAD_DIM)
    ang = positions.astype(jnp.float32)[..., None] * inv_freq
    cos = jnp.cos(ang)[:, :, None, :]
    sin = jnp.sin(ang)[:, :, None, :]

    for l in range(DEPTH):
        lam_init = 0.8 - 0.6 * math.exp(-0.3 * l)
        proj = x @ w_in[l]
        q, k, v, cb, cc, cu, qm, gates = jnp.split(proj, IN_SIZES and IN_SPLITS, axis=-1)

        q = rope(q.reshape(B, S, DA_HEADS * 2, DA_HEAD_DIM), cos, sin).reshape(B, S, DA_HEADS, 2, DA_HEAD_DIM)
        k = rope(k.reshape(B, S, DA_HEADS * 2, DA_HEAD_DIM), cos, sin).reshape(B, S, DA_HEADS, 2, DA_HEAD_DIM)
        v = v.reshape(B, S, DA_HEADS, DA_V_DIM)
        lam = (jnp.exp(jnp.sum(lambda_q1[l].astype(jnp.float32) * lambda_k1[l].astype(jnp.float32)))
               - jnp.exp(jnp.sum(lambda_q2[l].astype(jnp.float32) * lambda_k2[l].astype(jnp.float32)))
               + lam_init)
        y_attn = diff_attention(q, k, v, lam, lam_init, diff_subln_g[l])

        y_conv = short_gated_conv(cb, cc, cu, conv_w[l])

        y_mem = memory_attention_2(qm, mem, w_mem_kv[l])

        g = jax.nn.sigmoid(gates.reshape(B, S, N_BRANCH, D))
        merged = (g[:, :, 0] * (y_attn @ w_br_attn[l])
                  + g[:, :, 1] * (y_conv @ w_br_conv[l])
                  + g[:, :, 2] * (y_mem @ w_br_mem[l]))
        mix = merged @ w_out[l]
        x = layer_norm(DEEPNORM_ALPHA * x + mix, ln1_g[l], ln1_b[l])

        f = grouped_moe(x.reshape(B * S, D), w_router, router_bias,
                        w_exp_gate[l], w_exp_up[l], w_exp_down[l]).reshape(B, S, D)
        x = layer_norm(DEEPNORM_ALPHA * x + f, ln2_g[l], ln2_b[l])
    return x


def setup_inputs(seed=0):
    out = dict(first_inputs(seed))
    for name, value in second_inputs(seed + 1).items():
        if name != "x":
            out[name + "_2"] = value
    return out


def reference(
    x, mem, hawk_norm, hawk_w_in, hawk_conv_w, hawk_conv_b, hawk_gate_a_w, hawk_gate_a_b,
    hawk_gate_x_w, hawk_gate_x_b, hawk_lambda, hawk_mem_norm, hawk_w_mem_kv, hawk_w_out,
    nsa_norm, nsa_w_in, nsa_pe_k, nsa_pe_v, nsa_phi_k_w1, nsa_phi_k_w2, nsa_phi_v_w1,
    nsa_phi_v_w2, nsa_mem_norm, nsa_w_mem_kv, nsa_w_out, final_norm, mem_2, positions_2, w_in_2,
    lambda_q1_2, lambda_k1_2, lambda_q2_2, lambda_k2_2, diff_subln_g_2, conv_w_2, w_mem_kv_2,
    w_br_attn_2, w_br_conv_2, w_br_mem_2, w_out_2, ln1_g_2, ln1_b_2, ln2_g_2, ln2_b_2,
    w_router_2, router_bias_2, w_exp_gate_2, w_exp_up_2, w_exp_down_2,
):
    x = first_block(
        x, mem, hawk_norm, hawk_w_in, hawk_conv_w, hawk_conv_b, hawk_gate_a_w, hawk_gate_a_b,
        hawk_gate_x_w, hawk_gate_x_b, hawk_lambda, hawk_mem_norm, hawk_w_mem_kv, hawk_w_out,
        nsa_norm, nsa_w_in, nsa_pe_k, nsa_pe_v, nsa_phi_k_w1, nsa_phi_k_w2, nsa_phi_v_w1,
        nsa_phi_v_w2, nsa_mem_norm, nsa_w_mem_kv, nsa_w_out, final_norm,
    )
    return second_block(
        x, mem_2, positions_2, w_in_2, lambda_q1_2, lambda_k1_2, lambda_q2_2, lambda_k2_2,
        diff_subln_g_2, conv_w_2, w_mem_kv_2, w_br_attn_2, w_br_conv_2, w_br_mem_2, w_out_2,
        ln1_g_2, ln1_b_2, ln2_g_2, ln2_b_2, w_router_2, router_bias_2, w_exp_gate_2, w_exp_up_2,
        w_exp_down_2,
    )


_drawn_inputs = setup_inputs


def setup_inputs(seed=0):
    import zlib

    import numpy as np

    out = dict(_drawn_inputs(seed))
    spreads = {}
    factors = {'hawk_norm': 5.693,
     'hawk_gate_a_b': 8.0,
     'hawk_gate_x_b': 8.0,
     'hawk_mem_norm': 8.0,
     'nsa_norm': 7.273,
     'nsa_pe_k': 8.0,
     'nsa_pe_v': 2.949,
     'nsa_mem_norm': 8.0,
     'mem_2': 3.609,
     'lambda_q1_2': 4.649,
     'lambda_k1_2': 4.924,
     'lambda_q2_2': 8.0,
     'lambda_k2_2': 6.804,
     'diff_subln_g_2': 38.924,
     'w_mem_kv_2': 3.529,
     'w_br_mem_2': 3.528,
     'router_bias_2': 6.895}
    for name, (base, spread) in spreads.items():
        noise = np.random.default_rng([zlib.crc32(name.encode()), seed]).standard_normal(out[name].shape)
        drawn = base * np.exp(spread * noise) if base else spread * noise
        out[name] = __import__('jax').numpy.asarray(drawn.astype(out[name].dtype))
    for name, factor in factors.items():
        out[name] = (out[name] * factor).astype(out[name].dtype)
    return out
```

```python
import itertools
from collections import namedtuple
from contextlib import ExitStack, contextmanager

import concourse.bass as bass
import numpy as np
from concourse import mybir

F32 = mybir.dt.float32
I32 = mybir.dt.int32
ALU = mybir.AluOpType
ACT = mybir.ActivationFunctionType
AX_X = mybir.AxisListType.X

P = 128
BANK = 512
SEQ = 512
TT = SEQ // P
D = 1024
DK = D // P
N_MEM = 256
MT = N_MEM // P
BIG = 1e30

LRU = 1024
CONV_W = 4
HAWK_COLS = dict(xa=0, za=1024, q=2048, k=3584, v=5120, zb=6656, qm=7168, zm=7424)
DIL_GROUPS, DIL_HEADS, DIL_HD = 3, 4, 128
MEM_HEADS, MEM_HD = 4, 64
HAWK_OUT = 1792
NORM_EPS = 1e-6

NSA_COLS = dict(q=0, kc=1024, vc=1152, ks=1280, vs=1408, kw=1536, vw=1664, gates=1792, z=1840, qm=2864, zm=3120)
NSA_HEADS, NSA_GROUPS, NSA_HD = 16, 2, 64
CMP_BLOCK, CMP_STRIDE = 32, 16
N_CMP = (SEQ - CMP_BLOCK) // CMP_STRIDE + 1
PHI = 256
NSA_OUT = 1280

IN2 = dict(q=0, k=1024, v=2048, cb=3072, cc=3584, cu=4096, qm=4608, gates=5120)
DA_HEADS, DA_V = 8, 128
MEM2_HEADS, MEM2_HD = 4, 128
CONV2 = 512
N_EXPERTS, N_EGROUPS, PER_GROUP, D_FF = 16, 4, 4, 512
MAX_BLOCKS = 24
LN_EPS = 1e-5
ALPHA = 4 ** 0.25


stages = itertools.count()
tensors_made = itertools.count()


def bag(**values):
    return namedtuple("Names", list(values))(**values)


class Chip:

    ps = ident = columns = w_slots = rotate = col = None


@contextmanager
def stage(nc, *names):
    sems, every, number = {}, [], next(stages)
    for name in names:
        base, _, n = name.partition("*")
        made = [nc.alloc_semaphore(f"{base}_{number}_{i}") for i in range(int(n or 1))]
        every += made
        sems[base] = made if n else made[0]
    with nc.Block() as block:
        yield block, bag(**sems)
    nc.clear_and_free_semaphores(every)
    nc.all_engine_barrier()


@contextmanager
def Tensors(nc):
    with ExitStack() as stack:
        def make(name, shape, dtype=F32):
            return stack.enter_context(nc.sbuf_tensor(f"{name}_{next(tensors_made)}", shape, dtype))
        yield make


def flat(ap):
    return ap.rearrange("p a b -> p (a b)")


def one(t, index, parts=slice(0, P)):
    return t[parts, bass.ds(index, 1), :].rearrange("p a b -> p (a b)")


def pairs(eng, n, first=0):
    if n // 2 > 1:
        with eng.Fori(0, n // 2) as i:
            for u in range(2):
                yield 2 * i + u, (first + u) % 2, i
    else:
        for c in range(2 * (n // 2)):
            yield c, (first + c) % 2, c // 2
    if n % 2:
        yield n - 1, first, n // 2




def projection(nc, m, xT, ktiles, jobs, ntok=SEQ):
    w_slots, ps = m.w_slots, m.ps

    def walk(eng):
        chunks, tiles, first = [0, 0], [0, 0], 0
        for job in jobs:
            n = job["chunks"]
            per = job["width"] // P if job["kind"] == "T" else ntok // P
            for c, slot, turn in pairs(eng, n, first):
                yield job, c, slot, chunks[slot] + turn, tiles[slot] + per * turn, per
            for slot in range(2):
                turns = n // 2 + (n % 2 if slot == first else 0)
                chunks[slot] += turns
                tiles[slot] += per * turns
            first = (first + n) % 2

    with stage(nc, "weights_loaded*2", "tile_ready*2", "tile_taken*2") as (block, s):

        @block.sync
        def _(sp):
            for job, c, slot, chunk, tile, per in walk(sp):
                sp.wait_ge(s.tile_ready[slot], tile + 1)
                w = job["width"]
                src = job["w"][:, bass.ds(c * w + job["col"], w)].rearrange("(k p) n -> p k n", p=P)
                sp.dma_start(w_slots[slot][:, 0:ktiles, 0:w], src).then_inc(s.weights_loaded[slot], 16)

        @block.tensor
        def _(pe):
            for slot in range(2):
                pe.sem_inc(s.tile_ready[slot], 1)
            for job, c, slot, chunk, tile, per in walk(pe):
                pe.wait_ge(s.weights_loaded[slot], 16 * chunk + 16)
                pe.wait_ge(s.tile_taken[slot], tile + 1)
                w = w_slots[slot]
                for j in range(per):
                    for k in range(ktiles):
                        if job["kind"] == "T":
                            out = ps[:, (4 * slot + j) * BANK:(4 * slot + j) * BANK + ntok]
                            mm = pe.matmul(out, w[:, k, j * P:(j + 1) * P], xT[:, k, 0:ntok],
                                           start=k == 0, stop=k == ktiles - 1)
                        else:
                            out = ps[:, (4 * slot + j) * BANK:(4 * slot + j) * BANK + job["width"]]
                            mm = pe.matmul(out, xT[:, k, j * P:(j + 1) * P], w[:, k, 0:job["width"]],
                                           start=k == 0, stop=k == ktiles - 1)
                    mm.then_inc(s.tile_ready[slot], 1)

        @block.scalar
        def _(act):
            for slot in range(2):
                act.sem_inc(s.tile_taken[slot], 1)
            for job, c, slot, chunk, tile, per in walk(act):
                n = ntok if job["kind"] == "T" else job["width"]
                for j in range(per):
                    act.wait_ge(s.tile_ready[slot], tile + (j + 2))
                    bank = ps[:, (4 * slot + j) * BANK:(4 * slot + j) * BANK + n]
                    job["take"](act, bank, c, j).then_inc(s.tile_taken[slot], 1)


def take_T(dst, func=ACT.Copy, first=0, per=4):
    return lambda act, bank, c, j: act.activation(one(dst, per * c + (first + j)), bank, func)


def take_N(dst, func=ACT.Copy, width=512):
    return lambda act, bank, c, j: act.activation(
        dst[:, j, bass.ds(c * width, width)], bank, func)


def memory_kv(nc, m, memT, w_kv, n_cols, KT, V):
    projection(nc, m, memT, DK, [
        dict(w=w_kv, col=0, chunks=1, width=n_cols, kind="T", take=take_T(KT)),
        dict(w=w_kv, col=n_cols, chunks=1, width=n_cols, kind="N", take=take_N(V, width=n_cols)),
    ], ntok=N_MEM)




def to_columns(nc, m, src, tiles, dstT, gain=None):
    n = src.shape[2] // P
    with stage(nc, "turned", "taken") as (block, s):

        @block.tensor
        def _(pe):
            for k in range(n):
                if k >= 8:
                    pe.wait_ge(s.taken, k - 7)
                for t in range(tiles):
                    mm = pe.transpose(m.ps[:, (k % 8) * BANK + t * P:(k % 8) * BANK + (t + 1) * P],
                                      src[:, t, k * P:(k + 1) * P], m.ident[:, :])
                mm.then_inc(s.turned, 1)

        @block.scalar
        def _(act):
            for k in range(n):
                act.wait_ge(s.turned, k + 1)
                bank = m.ps[:, (k % 8) * BANK:(k % 8) * BANK + tiles * P]
                if gain is None:
                    ins = act.activation(dstT[:, k, 0:tiles * P], bank, ACT.Copy)
                else:
                    ins = act.activation(dstT[:, k, 0:tiles * P], bank, ACT.Copy, scale=gain[:, k:k + 1])
                ins.then_inc(s.taken, 1)


def refine_rsqrt(dve, done, at, var, inv, spare):
    dve.tensor_tensor(spare, inv, inv, ALU.mult).then_inc(done, 1)
    dve.wait_ge(done, at + 1)
    dve.scalar_tensor_tensor(out=spare, in0=spare, scalar=-0.5, in1=var, op0=ALU.mult, op1=ALU.mult).then_inc(done, 1)
    dve.wait_ge(done, at + 2)
    dve.scalar_tensor_tensor(out=inv, in0=spare, scalar=1.5, in1=inv, op0=ALU.add, op1=ALU.mult).then_inc(done, 1)
    dve.wait_ge(done, at + 3)


def rms_rows(nc, m, src, tiles, dst, eps):
    with Tensors(nc) as sb, stage(nc, "summed", "shifted", "rooted", "inverted") as (block, s):
        sums = sb("sums", [P, 4])
        var = sb("var", [P, 4])
        root = sb("root", [P, 4])
        inv = sb("inv", [P, 4])

        @block.scalar
        def _(act):
            for t in range(tiles):
                act.activation(dst[:, t, :], src[:, t, :], ACT.Square, accum_out=sums[:, t:t + 1]).then_inc(s.summed, 1)
            act.wait_ge(s.shifted, 1)
            act.activation(root[:, 0:tiles], var[:, 0:tiles], ACT.Sqrt).then_inc(s.rooted, 1)

        @block.vector
        def _(dve):
            dve.wait_ge(s.summed, tiles)
            dve.tensor_scalar(var[:, 0:tiles], sums[:, 0:tiles], 1.0 / D, eps, ALU.mult, ALU.add).then_inc(s.shifted, 1)
            dve.wait_ge(s.rooted, 1)
            dve.reciprocal(inv[:, 0:tiles], root[:, 0:tiles]).then_inc(s.inverted, 1)
            dve.wait_ge(s.inverted, 1)
            refine_rsqrt(dve, s.inverted, 1, var[:, 0:tiles], inv[:, 0:tiles], root[:, 0:tiles])
            for t in range(tiles):
                dve.tensor_scalar(dst[:, t, :], src[:, t, :], inv[:, t:t + 1], None, ALU.mult)


def layer_norm_rows(nc, m, x, gain, shift):
    with Tensors(nc) as sb, stage(nc, "row_loaded", "totalled", "averaged", "centred", "squared", "shifted",
                                  "rooted", "inverted", "scaled", "gained") as (block, s):
        g = sb("g", [P, D])
        b = sb("b", [P, D])
        scratch = sb("scratch", [P, TT, D])
        sums = sb("sums", [P, 4])
        mean = sb("mean", [P, 4])
        squares = sb("squares", [P, 4])
        var = sb("var", [P, 4])
        root = sb("root", [P, 4])
        inv = sb("inv", [P, 4])

        @block.sync
        def _(sp):
            sp.dma_start(g[:, :], gain.partition_broadcast(P)).then_inc(s.row_loaded, 16)
            sp.dma_start(b[:, :], shift.partition_broadcast(P)).then_inc(s.row_loaded, 16)

        @block.scalar
        def _(act):
            for t in range(TT):
                act.activation(scratch[:, t, :], x[:, t, :], ACT.Copy, accum_out=sums[:, t:t + 1]).then_inc(s.totalled, 1)
            for t in range(TT):
                act.wait_ge(s.centred, t + 1)
                act.activation(scratch[:, t, :], x[:, t, :], ACT.Square, accum_out=squares[:, t:t + 1]).then_inc(s.squared, 1)
            act.wait_ge(s.shifted, 1)
            act.activation(root[:, :], var[:, :], ACT.Sqrt).then_inc(s.rooted, 1)

        @block.vector
        def _(dve):
            dve.wait_ge(s.totalled, TT)
            dve.tensor_scalar(mean[:, :], sums[:, :], 1.0 / D, None, ALU.mult).then_inc(s.averaged, 1)
            dve.wait_ge(s.averaged, 1)
            for t in range(TT):
                dve.tensor_scalar(x[:, t, :], x[:, t, :], mean[:, t:t + 1], None, ALU.subtract).then_inc(s.centred, 1)
            dve.wait_ge(s.squared, TT)
            dve.tensor_scalar(var[:, :], squares[:, :], 1.0 / D, LN_EPS, ALU.mult, ALU.add).then_inc(s.shifted, 1)
            dve.wait_ge(s.rooted, 1)
            dve.reciprocal(inv[:, :], root[:, :]).then_inc(s.inverted, 1)
            dve.wait_ge(s.inverted, 1)
            refine_rsqrt(dve, s.inverted, 1, var[:, :], inv[:, :], root[:, :])
            dve.wait_ge(s.row_loaded, 32)
            for t in range(TT):
                dve.scalar_tensor_tensor(out=scratch[:, t, :], in0=x[:, t, :], scalar=inv[:, t:t + 1], in1=g[:, :],
                                         op0=ALU.mult, op1=ALU.mult).then_inc(s.scaled, 1)
            for t in range(TT):
                dve.wait_ge(s.scaled, t + 1)
                dve.tensor_tensor(x[:, t, :], scratch[:, t, :], b[:, :], ALU.add)


def output_product(nc, m, yT, ktiles, w, x, rescale=1.0):
    half = ktiles // 2
    ps = m.ps
    with stage(nc, "weights_loaded*2", "slot_read*2", "sum_ready", "bank_free") as (block, s):

        @block.sync
        def _(sp):
            for n in range(2):
                for h in range(2):
                    if n:
                        sp.wait_ge(s.slot_read[h], 4 * n)
                    src = w[h * half * P:(h + 1) * half * P, n * 512:(n + 1) * 512].rearrange("(k p) n -> p k n", p=P)
                    sp.dma_start(m.w_slots[h][:, 0:half, :], src).then_inc(s.weights_loaded[h], 16)

        @block.tensor
        def _(pe):
            for n in range(2):
                for h in range(2):
                    pe.wait_ge(s.weights_loaded[h], 16 * n + 16)
                    for t in range(TT):
                        bank = 4 * n + t
                        for k in range(half):
                            mm = pe.matmul(ps[:, bank * BANK:(bank + 1) * BANK], yT[:, h * half + k, t * P:(t + 1) * P],
                                           m.w_slots[h][:, k, :], start=h == 0 and k == 0, stop=h == 1 and k == half - 1)
                        mm.then_inc(s.slot_read[h], 1)

        @block.vector
        def _(dve):
            for n in range(2):
                for t in range(TT):
                    dve.wait_ge(s.slot_read[1], 4 * n + t + 1)
                    cols = x[:, t, n * 512:(n + 1) * 512]
                    bank = 4 * n + t
                    dve.scalar_tensor_tensor(out=cols, in0=cols, scalar=rescale,
                                             in1=ps[:, bank * BANK:(bank + 1) * BANK], op0=ALU.mult, op1=ALU.add)


def gate_rows(nc, pairs_):
    with stage(nc) as (block, s):

        @block.vector
        def _(dve):
            for y, gate in pairs_:
                dve.tensor_tensor(y, y, gate, ALU.mult)




def attention(nc, m, n_iter, copies, items, width, n_score_banks, n_turn):
    n = len(items)
    ps = m.ps
    n_out = 8 - 2 * n_score_banks - n_turn
    turn_bank0 = 2 * n_score_banks
    out_bank0 = turn_bank0 + n_turn
    chunks = []
    for it in items:
        v = it["values"]
        chunks.append([v[a:a + 4] for a in range(0, len(v), 4)])
    chunk_base = np.cumsum([0] + [len(c) for c in chunks]).tolist()
    n_chunks = chunk_base[-1]
    n_segs = [len(it["segs"]) for it in items]
    seg_base = np.cumsum([0] + n_segs).tolist()
    n_seg = seg_base[-1]
    chunks_of = [(k, c) for k in range(n) for c in range(len(chunks[k]))]

    def score_ap(k, seg):
        c = ((k % 2) * n_score_banks + seg[2]) * BANK
        return ps[:, c:c + seg[3]]

    coef_base = np.cumsum([0] + [it.get("coef") is not None for it in items]).tolist()
    n_coef = coef_base[-1]
    assert n % 4 == 0 and n_chunks % n_turn == 0 and n % n_out == 0

    with Tensors(nc) as sb, stage(nc, "staged", "scores_ready", "biased", "top_found", "top_scaled", "exp_done",
                                  "turned", "keys_ready", "out_ready", "out_taken", "inverted",
                                  "weighted") as (block, s):
        sc, pr = (flat(w[:, :, :])[:, 0:2 * width].rearrange("p (a b) -> p a b", a=2) for w in m.w_slots)
        prT = sb("probs_by_key", [P, 2, max(len(c) for c in chunks) * 4 * P])
        top = sb("top", [P, 2])
        ntop = sb("ntop", [P, 2])
        total = sb("total", [P, 4])
        inv = sb("inv", [P, 2])
        wt = sb("wt", [P, 2])


        if copies:
            @block.gpsimd
            def _(pool):
                with pool.Fori(0, n_iter) as i:
                    pool.wait_ge(s.scores_ready, i * n + 1)
                    for dst, src in copies:
                        pool.tensor_copy(dst, src(i)).then_inc(s.staged, 1)

        @block.tensor
        def _(pe):
            pe.sem_inc(s.out_ready, 2)
            pe.sem_inc(s.scores_ready, 1)

            def scores(i, k):
                pe.wait_ge(s.top_found, i * n + (k + 1))
                for seg in items[k]["segs"]:
                    mm = pe.matmul(score_ap(k, seg), seg[0], seg[1](i), start=True, stop=True)
                mm.then_inc(s.scores_ready, 1)

            def turn(i, k):
                pe.wait_ge(s.exp_done, i * n + (k + 3))
                for c, chunk in enumerate(chunks[k]):
                    q = chunk_base[k] + c
                    pe.wait_ge(s.keys_ready, i * n_chunks + (q + 1))
                    bank = (turn_bank0 + q % n_turn) * BANK
                    for j, (col, rows, _) in enumerate(chunk):
                        mm = pe.transpose(ps[0:rows, bank + j * P:bank + (j + 1) * P],
                                          pr[:, k % 2, col:col + rows], m.ident[:, :])
                    mm.then_inc(s.turned, 1)

            def product(i, k):
                pe.wait_ge(s.out_taken, i * n + (k + 1))
                hd = items[k]["hd"]
                out = ps[:, (out_bank0 + k % n_out) * BANK:(out_bank0 + k % n_out) * BANK + hd]
                last = len(items[k]["values"]) - 1
                t = 0
                for c, chunk in enumerate(chunks[k]):
                    pe.wait_ge(s.keys_ready, i * n_chunks + (chunk_base[k] + c + 1 + n_turn))
                    for col, rows, v in chunk:
                        mm = pe.matmul(out, prT[0:rows, k % 2, t * P:(t + 1) * P], v(i), start=t == 0, stop=t == last)
                        t += 1
                mm.then_inc(s.out_ready, 1)

            with pe.Fori(0, n_iter) as i:
                if copies:
                    pe.wait_ge(s.staged, i * len(copies) + len(copies))
                scores(i, 0)
                for k in range(n):
                    if k + 1 < n:
                        scores(i, k + 1)
                    turn(i, k)
                    if k:
                        product(i, k - 1)
                product(i, n - 1)

        @block.vector
        def _(dve):
            dve.sem_inc(s.top_found, 2)
            dve.sem_inc(s.out_taken, n_out)

            def bias(i, k):
                dve.wait_ge(s.scores_ready, i * n + (k + 2))
                dve.wait_ge(s.exp_done, i * n + (k + 1))
                at = 0
                for seg in items[k]["segs"]:
                    dst = sc[:, k % 2, at:at + seg[3]]
                    if seg[4] is None:
                        ins = dve.tensor_copy(dst, score_ap(k, seg))
                    elif seg[5] is None:
                        ins = dve.tensor_tensor(dst, score_ap(k, seg), seg[4], ALU.add)
                    else:
                        ins = dve.scalar_tensor_tensor(out=dst, in0=seg[4], scalar=seg[5](i), in1=score_ap(k, seg),
                                                       op0=ALU.mult, op1=ALU.add)
                    ins.then_inc(s.biased, 1)
                    at += seg[3]
                dve.wait_ge(s.biased, i * n_seg + seg_base[k + 1])
                dve.reduce_max(top[:, k % 2:k % 2 + 1], sc[:, k % 2, 0:at], AX_X).then_inc(s.top_found, 1)
                dve.wait_ge(s.top_found, i * n + (k + 3))
                dve.tensor_scalar(ntop[:, k % 2:k % 2 + 1], top[:, k % 2:k % 2 + 1], -items[k]["scale"], None,
                                  ALU.mult).then_inc(s.top_scaled, 1)

            def finish(i, k):
                it = items[k]
                hd = it["hd"]
                b = (out_bank0 + k % n_out) * BANK
                dve.wait_ge(s.exp_done, i * n + (k + 3))
                dve.reciprocal(inv[:, k % 2:k % 2 + 1], total[:, k % 4:k % 4 + 1]).then_inc(s.inverted, 1)
                factor = inv
                dve.wait_ge(s.inverted, i * n + (k + 1))
                if it.get("coef") is not None:
                    dve.tensor_tensor(wt[:, k % 2:k % 2 + 1], inv[:, k % 2:k % 2 + 1], it["coef"](i),
                                      ALU.mult).then_inc(s.weighted, 1)
                    dve.wait_ge(s.weighted, i * n_coef + coef_base[k + 1])
                    factor = wt
                dve.wait_ge(s.out_ready, i * n + (k + 3))
                dst = it["dst"](i)
                f = factor[:, k % 2:k % 2 + 1]
                if it.get("add"):
                    dve.wait_ge(s.out_taken, i * n + (k + n_out))
                    ins = dve.scalar_tensor_tensor(out=dst, in0=ps[:, b:b + hd], scalar=f, in1=dst, op0=ALU.mult, op1=ALU.add)
                else:
                    ins = dve.tensor_scalar(dst, ps[:, b:b + hd], f, None, ALU.mult)
                ins.then_inc(s.out_taken, 1)

            with dve.Fori(0, n_iter) as i:
                bias(i, 0)
                for k in range(n):
                    if k + 1 < n:
                        bias(i, k + 1)
                    if k:
                        finish(i, k - 1)
                finish(i, n - 1)

        @block.scalar
        def _(act):
            act.sem_inc(s.exp_done, 2)
            act.sem_inc(s.keys_ready, n_turn)

            def exponent(i, k):
                it = items[k]
                w = sum(seg[3] for seg in it["segs"])
                act.wait_ge(s.top_scaled, i * n + (k + 1))
                act.activation(pr[:, k % 2, 0:w], sc[:, k % 2, 0:w], ACT.Exp, bias=ntop[:, k % 2:k % 2 + 1],
                               scale=it["scale"], accum_out=total[:, k % 4:k % 4 + 1]).then_inc(s.exp_done, 1)

            def take(i, k):
                act.wait_ge(s.out_ready, i * n + (k + 1))
                for c, chunk in enumerate(chunks[k]):
                    q = chunk_base[k] + c
                    act.wait_ge(s.turned, i * n_chunks + (q + 1))
                    rows = chunk[0][1]
                    bank = (turn_bank0 + q % n_turn) * BANK
                    act.activation(prT[0:rows, k % 2, 4 * c * P:(4 * c + len(chunk)) * P],
                                   ps[0:rows, bank:bank + len(chunk) * P], ACT.Copy).then_inc(s.keys_ready, 1)

            with act.Fori(0, n_iter) as i:
                exponent(i, 0)
                for k in range(n):
                    if k + 1 < n:
                        exponent(i, k + 1)
                    take(i, k)


def seg(lhsT, rhs, cols, bank=0, table=None, slope=None):
    return (lhsT, rhs, bank, cols, table, slope)


def memory_attention(nc, m, heads, hd, qT, kT, v, y, y_col):
    per = P // hd
    with Tensors(nc) as sb:
        q_here = sb("q_here", [P, SEQ])
        k_here = sb("k_here", [P, N_MEM])
        items = []
        for h in range(per):
            rows = slice(h * hd, (h + 1) * hd)
            for t in range(TT):
                items.append(dict(
                    segs=[seg(q_here[rows, t * P:(t + 1) * P], lambda i, rows=rows: k_here[rows, :], N_MEM)],
                    scale=hd ** -0.5,
                    values=[(j * P, P, lambda i, j=j, h=h: v[:, j, bass.ds(i * P + h * hd, hd)]) for j in range(MT)],
                    hd=hd, dst=lambda i, t=t, h=h: y[:, t, bass.ds(i * P + (y_col + h * hd), hd)]))
        attention(nc, m, heads // per, [(q_here[:, :], lambda i: one(qT, i)), (k_here[:, :], lambda i: one(kT, i))],
                  items, N_MEM, 1, 2)




def lru(nc, m, a, xa, yT):
    K = LRU // P
    with Tensors(nc) as sb, stage(nc, "zeroed", "blocks_loaded", "padded", "conv", "gates_ready", "gated_r", "gated_x",
                                  "rate", "soft", "s_ready", "root_ready", "step", "banks") as (block, s):
        cw = m.col["hawk_conv_w"].rearrange("p (j k) -> p j k", k=K)
        cb, gab, gxb, lam = (m.col[f"hawk_{n}"] for n in ("conv_b", "gate_a_b", "gate_x_b", "lambda"))
        sp_ = sb("softplus", [P, 6, K])
        blocks = [sb("blocks_a", [P, K, P]), sb("blocks_x", [P, K, P])]
        xc = sb("xc", [P, K, SEQ])
        gi = sb("gi", [P, K, SEQ])
        r1 = sb("r1", [P, K, SEQ])

        @block.sync
        def _(sp):
            sp.wait_ge(s.zeroed, 2)
            for blk, name in zip(blocks, ("hawk_gate_a_w", "hawk_gate_x_w")):
                for b in range(2):
                    sp.dma_start(blk[64 * b:64 * b + 64, :, 64 * b:64 * b + 64],
                                 a[name][0].rearrange("(k b) i j -> b i k j", b=2)[b]).then_inc(s.blocks_loaded, 16)

        @block.gpsimd
        def _(pool):
            for blk in blocks:
                pool.memset(blk[:, :, :], 0.0).then_inc(s.zeroed, 1)

        @block.tensor
        def _(pe):
            pe.wait_ge(s.blocks_loaded, 64)
            pe.wait_ge(s.conv, K * CONV_W)
            for c in range(K):
                for g in range(2):
                    n = 2 * c + g
                    if n >= 8:
                        pe.wait_ge(s.banks, n - 7)
                    pe.matmul(m.ps[:, (n % 8) * BANK:(n % 8 + 1) * BANK], blocks[g][:, c, :], xc[:, c, :],
                              start=True, stop=True).then_inc(s.gates_ready, 1)

        @block.scalar
        def _(act):
            act.activation(sp_[:, 0, :], lam[:, :], ACT.Abs).then_inc(s.soft, 1)
            act.wait_ge(s.soft, 1)
            act.activation(sp_[:, 1, :], sp_[:, 0, :], ACT.Exp, scale=-1.0).then_inc(s.soft, 1)
            act.wait_ge(s.soft, 2)
            act.activation(sp_[:, 2, :], sp_[:, 1, :], ACT.Ln, bias=1.0).then_inc(s.soft, 1)
            act.activation(sp_[:, 3, :], lam[:, :], ACT.Relu, scale=-1.0).then_inc(s.soft, 1)
            for c in range(K):
                for g, (dst, bias) in enumerate(((r1, gab), (gi, gxb))):
                    n = 2 * c + g
                    act.wait_ge(s.gates_ready, n + 1)
                    act.activation(dst[:, c, :], m.ps[:, (n % 8) * BANK:(n % 8 + 1) * BANK], ACT.Sigmoid,
                                   bias=bias[:, c:c + 1]).then_inc(s.banks, 1)
            act.wait_ge(s.rate, 1)
            act.wait_ge(s.banks, 2 * K)
            for c in range(K):
                act.activation(r1[:, c, :], r1[:, c, :], ACT.Tanh, scale=sp_[:, 5, c:c + 1]).then_inc(s.s_ready, 1)
            act.wait_ge(s.s_ready, K)
            act.wait_ge(s.step, 2)
            act.activation(xa[:, :, 0:SEQ], r1[:, :, :], ACT.Sqrt).then_inc(s.root_ready, 1)

        @block.vector
        def _(dve):
            dve.memset(xa[:, :, 0:3], 0.0).then_inc(s.padded, 1)
            dve.wait_ge(s.padded, 1)
            for j in range(CONV_W):
                if j:
                    dve.wait_ge(s.conv, K * j)
                for c in range(K):
                    x = xa[:, c, j:j + SEQ]
                    if j == 0:
                        ins = dve.tensor_scalar(xc[:, c, :], x, cw[:, 0, c:c + 1], cb[:, c:c + 1], ALU.mult, ALU.add)
                    else:
                        ins = dve.scalar_tensor_tensor(out=xc[:, c, :], in0=x, scalar=cw[:, j, c:c + 1], in1=xc[:, c, :],
                                                       op0=ALU.mult, op1=ALU.add)
                    ins.then_inc(s.conv, 1)
            dve.wait_ge(s.soft, 4)
            dve.tensor_tensor(sp_[:, 4, :], sp_[:, 2, :], sp_[:, 3, :], ALU.add).then_inc(s.padded, 1)
            dve.wait_ge(s.padded, 2)
            dve.tensor_scalar(sp_[:, 5, :], sp_[:, 4, :], 4.0, None, ALU.mult).then_inc(s.rate, 1)
            dve.wait_ge(s.banks, 2 * K)
            dve.wait_ge(s.conv, K * CONV_W)
            dve.tensor_tensor(flat(gi[:, :, :]), flat(gi[:, :, :]), flat(xc[:, :, :]), ALU.mult).then_inc(s.step, 1)
            dve.wait_ge(s.step, 1)
            dve.wait_ge(s.s_ready, K)
            dve.tensor_scalar(flat(xc[:, :, :]), flat(r1[:, :, :]), 1.0, None, ALU.add).then_inc(s.step, 1)
            dve.wait_ge(s.step, 2)
            dve.reciprocal(flat(xc[:, :, :]), flat(xc[:, :, :])).then_inc(s.step, 1)
            dve.wait_ge(s.step, 3)
            dve.wait_ge(s.root_ready, 1)
            dve.scalar_tensor_tensor(out=xa[:, :, 0:SEQ], in0=xa[:, :, 0:SEQ], scalar=2.0, in1=xc[:, :, :],
                                     op0=ALU.mult, op1=ALU.mult).then_inc(s.step, 1)
            dve.wait_ge(s.step, 4)
            dve.memset(xa[:, :, 0:1], 1.0).then_inc(s.step, 1)
            dve.wait_ge(s.step, 5)
            dve.tensor_tensor(gi[:, :, :], gi[:, :, :], xa[:, :, 0:SEQ], ALU.mult).then_inc(s.step, 1)
            dve.tensor_scalar(flat(r1[:, :, :]), flat(r1[:, :, :]), -1.0, 1.0, ALU.mult, ALU.add).then_inc(s.step, 1)
            dve.wait_ge(s.step, 7)
            dve.tensor_tensor(flat(r1[:, :, :]), flat(r1[:, :, :]), flat(xc[:, :, :]), ALU.mult).then_inc(s.step, 1)
            dve.wait_ge(s.step, 8)
            for c in range(K):
                dve.tensor_tensor_scan(xc[:, c, :], r1[:, c, :], gi[:, c, :], 0.0, ALU.mult, ALU.add).then_inc(s.step, 1)
            for c in range(K):
                dve.wait_ge(s.step, 9 + c)
                dve.tensor_tensor(yT[:, c, :], yT[:, c, :], xc[:, c, :], ALU.mult)


def hawk_layer(nc, m, a, x):
    with Tensors(nc) as sb:
        xT = sb("hawk_xT", [P, DK, SEQ])
        yT = sb("hawk_yT", [P, HAWK_OUT // P, SEQ])
        w = a["hawk_w_in"][0]

        def job(name, chunks, width, kind, take, skip=0):
            return dict(w=w, col=HAWK_COLS[name] + skip, chunks=chunks, width=width, kind=kind, take=take)

        with Tensors(nc) as sb1:
            rows = sb1("rows", [P, TT, D])
            rms_rows(nc, m, x, TT, rows, NORM_EPS)
            to_columns(nc, m, rows, TT, xT, m.col["hawk_norm"])
        with Tensors(nc) as sb1:
            xa = sb1("xa", [P, DK, 3 + SEQ])
            projection(nc, m, xT, DK, [
                job("xa", 2, 512, "T", lambda act, bank, c, j: act.activation(
                    xa[:, bass.ds(4 * c + j, 1), 3:3 + SEQ].rearrange("p a b -> p (a b)"), bank, ACT.Copy)),
                job("za", 2, 512, "T", take_T(yT, ACT.Silu)),
            ])
            lru(nc, m, a, xa, yT)
        n_rows = DIL_HEADS * DIL_HD + MEM_HEADS * MEM_HD
        with Tensors(nc) as sb1:
            y = sb1("y_rows", [P, TT, n_rows])
            with Tensors(nc) as sb2:
                qT = sb2("qT", [P, 12, SEQ])
                kT = sb2("kT", [P, 12, SEQ])
                v = sb2("v", [P, TT, 1536])
                projection(nc, m, xT, DK, [
                    job("q", 3, 512, "T", take_T(qT)),
                    job("k", 3, 512, "T", take_T(kT)),
                    job("v", 3, 512, "N", take_N(v)),
                ])
                dilated(nc, m, a, qT, kT, v, y)
            with Tensors(nc) as sb2:
                gate = sb2("gate_rows", [P, TT, n_rows])
                qmT = sb2("qmT", [P, 2, SEQ])
                kmT = sb2("kmT", [P, 2, N_MEM])
                vm = sb2("vm", [P, MT, MEM_HEADS * MEM_HD])
                memT = sb2("memT", [P, DK, N_MEM])
                projection(nc, m, xT, DK, [
                    job("zb", 1, 512, "N", take_N(gate, ACT.Silu)),
                    job("qm", 1, 256, "T", take_T(qmT, per=2)),
                    job("zm", 1, 256, "N", lambda act, bank, c, j: act.activation(gate[:, j, 512:768], bank, ACT.Silu)),
                ])
                normed_memory(nc, m, a["mem"][0], m.col["hawk_mem_norm"], memT)
                memory_kv(nc, m, memT, a["hawk_w_mem_kv"][0], 256, kmT, vm)
                memory_attention(nc, m, MEM_HEADS, MEM_HD, qmT, kmT, vm, y, 512)
                gate_rows(nc, [(flat(y[:, :, :]), flat(gate[:, :, :]))])
            to_columns(nc, m, y, TT, yT[:, 8:14, :])
        output_product(nc, m, yT, HAWK_OUT // P, a["hawk_w_out"][0], x)


COLUMN_VECTORS = [
    ("hawk_norm", DK), ("hawk_conv_w", CONV_W * DK), ("hawk_conv_b", DK), ("hawk_gate_a_b", DK), ("hawk_gate_x_b", DK),
    ("hawk_lambda", DK), ("hawk_mem_norm", DK), ("nsa_norm", DK), ("nsa_mem_norm", DK), ("conv_w_2", 24),
    ("nsa_pe_k", 16), ("nsa_pe_v", 16), ("diff_subln_g_2", 2),
]


def load_columns(nc, m, a):
    with Tensors(nc) as sb, stage(nc, "zeroed", "loaded", "turned") as (block, s):
        rows = sb("vector_rows", [P, 2, P])
        places, at = [], 0
        for name, n in COLUMN_VECTORS:
            if at // P != (at + n - 1) // P:
                at = P * (at // P + 1)
            places.append((name, n, at))
            m.col[name] = m.columns[:, at:at + n]
            at += n

        @block.vector
        def _(dve):
            dve.memset(rows[:, :, :], 0.0).then_inc(s.zeroed, 1)
            dve.wait_ge(s.turned, 2)
            dve.tensor_copy(m.columns[:, :], m.ps[:, 0:2 * P])

        @block.sync
        def _(sp):
            sp.wait_ge(s.zeroed, 1)
            for name, n, at in places:
                v = a[name]
                axes = " ".join(f"a{i}" for i in range(len(v.shape)))
                v = v.rearrange(f"{axes} -> ({axes})").rearrange("(k p) -> k p", p=P)
                sp.dma_start(rows[at % P:at % P + n, at // P, :], v).then_inc(s.loaded, 16)

        @block.tensor
        def _(pe):
            pe.wait_ge(s.loaded, 16 * len(places))
            for g in range(2):
                pe.transpose(m.ps[:, g * P:(g + 1) * P], rows[:, g, :], m.ident[:, :]).then_inc(s.turned, 1)


def normed_memory(nc, m, mem, gain, memT):
    with Tensors(nc) as sb:
        rows = sb("mem_rows", [P, MT, D])
        with stage(nc, "loaded") as (block, s):
            @block.sync
            def _(sp):
                sp.dma_start(rows[:, :, :], mem.rearrange("(t p) d -> p t d", p=P)).then_inc(s.loaded, 16)
                sp.wait_ge(s.loaded, 16)
        if gain is not None:
            normed = sb("mem_normed", [P, MT, D])
            rms_rows(nc, m, rows, MT, normed, NORM_EPS)
            to_columns(nc, m, normed, MT, memT, gain)
        else:
            to_columns(nc, m, rows, MT, memT)


def dilated(nc, m, a, qT, kT, v, y):
    with Tensors(nc) as sb:
        q_here = sb("q_here", [P, DIL_GROUPS, SEQ])
        tab = [sb("near", [P, 256]), sb("by4", [P, SEQ]), sb("by16", [P, SEQ])]
        slopes = sb("slopes", [P, DIL_GROUPS * DIL_HEADS])
        with stage(nc, "loaded") as (block, s):
            @block.sync
            def _(sp):
                for t, name in zip(tab, ("dist_near", "dist_by4", "dist_by16")):
                    sp.dma_start(t[:, :], a[name]).then_inc(s.loaded, 16)
                sp.dma_start(slopes[:, :], a["dil_slopes"].partition_broadcast(P)).then_inc(s.loaded, 16)
                sp.wait_ge(s.loaded, 64)
        items = []
        for t in range(TT):
            near = P if t == 0 else 2 * P
            near0 = max(t - 1, 0) * P
            reach = (t + 1) * P
            segs, values = [], []
            for bank, (g, k0, cols) in enumerate(((0, near0, near), (1, 0, reach), (2, 0, reach))):
                table = tab[g][:, tab[g].shape[1] - cols:]
                segs.append(seg(q_here[:, g, t * P:(t + 1) * P],
                                lambda i, g=g, k0=k0, cols=cols: kT[:, bass.ds(i + 4 * g, 1), k0:k0 + cols].rearrange("p a b -> p (a b)"),
                                cols, bank, table, lambda i, g=g: slopes[:, bass.ds(i + 4 * g, 1)]))
                at = sum(x[3] for x in segs[:-1])
                for j in range(cols // P):
                    values.append((at + j * P, P, lambda i, g=g, kt=k0 // P + j: v[:, kt, bass.ds(i * P + 512 * g, P)]))
            items.append(dict(segs=segs, scale=DIL_HD ** -0.5, values=values, hd=DIL_HD,
                              dst=lambda i, t=t: y[:, t, bass.ds(i * P, P)]))
        attention(nc, m, DIL_HEADS, [(q_here[:, g, :], lambda i, g=g: one(qT, i + 4 * g)) for g in range(DIL_GROUPS)],
                  items, 1280, 3, 1)




def take_halves(dst, shift):
    def take(act, bank, c, j, dst=dst):
        target = dst[j] if isinstance(dst, list) else dst
        for g in range(NSA_GROUPS):
            for h in range(2):
                n = SEQ - shift * h
                ins = act.activation(target[64 * h:64 * h + 64, g, 0:n], bank[64 * g:64 * g + 64, shift * h:SEQ], ACT.Copy)
        return ins
    return take


def compress(nc, m, a, kc, vc, k_cmp, v_cmp):
    n_pos = CMP_BLOCK // 2
    with Tensors(nc) as sb, stage(nc, "w1_loaded*2", "w2_loaded", "zeroed", "offset_ready", "offset", "hidden_ready",
                                  "hidden", "result_ready") as (block, s):
        w1 = [flat(w[:, :, :]).rearrange("p (k n) -> p k n", n=PHI) for w in m.w_slots]
        w2 = [sb("w2_k", [P, 2, P]), sb("w2_v", [P, 2, NSA_HD])]
        off = sb("offset", [P, 4])
        hid = sb("hidden", [P, 4, NSA_GROUPS * N_CMP])
        src = [kc, vc]
        N = NSA_GROUPS * N_CMP

        @block.sync
        def _(sp):
            for i, name in enumerate("kv"):
                sp.dma_start(w1[i], a[f"nsa_phi_{name}_w1"][0].rearrange("(k p) n -> p k n", p=P)).then_inc(s.w1_loaded[i], 16)
            w2k = a["nsa_phi_k_w2"][0].rearrange("(k p) n -> p k n", p=P)
            for h in range(2):
                sp.dma_start(w2[0][:, :, 64 * h:64 * h + 64], w2k).then_inc(s.w2_loaded, 16)
            sp.dma_start(w2[1][:, :, :], a["nsa_phi_v_w2"][0].rearrange("(k p) n -> p k n", p=P)).then_inc(s.w2_loaded, 16)

        @block.tensor
        def _(pe):
            for i in range(2):
                pe.wait_ge(s.w1_loaded[i], 16)
                pe_cols = m.col["nsa_pe_" + "kv"[i]]
                for h in range(2):
                    n = 2 * i + h
                    for k in range(n_pos):
                        mm = pe.matmul(m.ps[:, n * BANK:n * BANK + 1], w1[i][:, k, h * P:(h + 1) * P],
                                       pe_cols[:, k:k + 1], start=k == 0, stop=k == n_pos - 1)
                    mm.then_inc(s.offset_ready, 1)
                    for g in range(NSA_GROUPS):
                        for k in range(n_pos):
                            rhs = src[i][:, g, 2 * k:2 * k + CMP_STRIDE * (N_CMP - 1) + 1:CMP_STRIDE]
                            bank = (4 + n) * BANK + g * N_CMP
                            mm = pe.matmul(m.ps[:, bank:bank + N_CMP], w1[i][:, k, h * P:(h + 1) * P], rhs,
                                           start=k == 0, stop=k == n_pos - 1)
                    mm.then_inc(s.hidden_ready, 1)
            pe.wait_ge(s.w2_loaded, 48)
            pe.wait_ge(s.hidden, 4)
            for h in range(2):
                mm = pe.matmul(m.ps[:, 0:N], w2[0][:, h, :], hid[:, h, :], start=h == 0, stop=h == 1)
            mm.then_inc(s.result_ready, 1)
            for g in range(NSA_GROUPS):
                for h in range(2):
                    mm = pe.matmul(m.ps[0:N_CMP, BANK + g * NSA_HD:BANK + (g + 1) * NSA_HD],
                                   hid[:, 2 + h, g * N_CMP:(g + 1) * N_CMP], w2[1][:, h, :], start=h == 0, stop=h == 1)
            mm.then_inc(s.result_ready, 1)

        @block.vector
        def _(dve):
            dve.memset(k_cmp[:, :, :], 0.0).then_inc(s.zeroed, 1)
            for n in range(4):
                dve.wait_ge(s.offset_ready, n + 1)
                dve.tensor_copy(off[:, n:n + 1], m.ps[:, n * BANK:n * BANK + 1]).then_inc(s.offset, 1)
            dve.wait_ge(s.zeroed, 1)
            dve.wait_ge(s.result_ready, 2)
            dve.tensor_copy(k_cmp[:, :, 0:N_CMP], m.ps[:, 0:N].rearrange("p (g n) -> p g n", n=N_CMP))
            dve.tensor_copy(v_cmp[0:N_CMP, :], m.ps[0:N_CMP, BANK:BANK + NSA_GROUPS * NSA_HD])

        @block.scalar
        def _(act):
            for n in range(4):
                act.wait_ge(s.offset, n + 1)
                act.wait_ge(s.hidden_ready, n + 1)
                act.activation(hid[:, n, :], m.ps[:, (4 + n) * BANK:(4 + n) * BANK + N], ACT.Silu,
                               bias=off[:, n:n + 1]).then_inc(s.hidden, 1)


def nsa_layer(nc, m, a, x):
    w = a["nsa_w_in"][0]

    def job(name, chunks, width, kind, take):
        return dict(w=w, col=NSA_COLS[name], chunks=chunks, width=width, kind=kind, take=take)

    with Tensors(nc) as sb:
        xT = sb("nsa_xT", [P, DK, SEQ])
        with Tensors(nc) as sb1:
            rows = sb1("rows", [P, TT, D])
            rms_rows(nc, m, x, TT, rows, NORM_EPS)
            to_columns(nc, m, rows, TT, xT, m.col["nsa_norm"])
        yT = sb("nsa_yT", [P, NSA_OUT // P, SEQ])
        with Tensors(nc) as sb1:
            y = sb1("y_rows", [P, TT, NSA_OUT])
            with Tensors(nc) as sb2:
                qT = sb2("qT", [P, 8, SEQ])
                kc, vc, ks, kw = (sb2(n, [P, NSA_GROUPS, SEQ]) for n in ("kc", "vc", "ks", "kw"))
                vs, vw = (sb2(n, [P, TT, P]) for n in ("vs", "vw"))
                k_cmp = sb2("k_cmp", [P, NSA_GROUPS, 32])
                v_cmp = sb2("v_cmp", [32, NSA_GROUPS * NSA_HD])
                gates = sb2("gates", [P, TT, 3 * NSA_HEADS])
                projection(nc, m, xT, DK, [
                    job("kc", 1, 256, "T", take_halves([kc, vc], 1)),
                    job("ks", 1, 128, "T", take_halves(ks, 0)),
                    job("vs", 1, 128, "N", take_N(vs, width=128)),
                    job("kw", 1, 128, "T", take_halves(kw, 0)),
                    job("vw", 1, 128, "N", take_N(vw, width=128)),
                    job("gates", 1, 48, "N", take_N(gates, ACT.Sigmoid, 48)),
                    job("q", 2, 512, "T", take_T(qT)),
                ])
                compress(nc, m, a, kc, vc, k_cmp, v_cmp)
                nsa_attention(nc, m, a, qT, ks, kw, k_cmp, vs, vw, v_cmp, gates, y)
            with Tensors(nc) as sb2:
                gate = sb2("gate_rows", [P, TT, NSA_OUT])
                qmT = sb2("qmT", [P, 2, SEQ])
                kmT = sb2("kmT", [P, 2, N_MEM])
                vm = sb2("vm", [P, MT, MEM_HEADS * MEM_HD])
                memT = sb2("memT", [P, DK, N_MEM])
                projection(nc, m, xT, DK, [
                    job("z", 2, 512, "N", take_N(gate, ACT.Silu)),
                    job("qm", 1, 256, "T", take_T(qmT, per=2)),
                    job("zm", 1, 256, "N", lambda act, bank, c, j: act.activation(gate[:, j, 1024:1280], bank, ACT.Silu)),
                ])
                normed_memory(nc, m, a["mem"][0], m.col["nsa_mem_norm"], memT)
                memory_kv(nc, m, memT, a["nsa_w_mem_kv"][0], 256, kmT, vm)
                memory_attention(nc, m, MEM_HEADS, MEM_HD, qmT, kmT, vm, y, 1024)
                gate_rows(nc, [(flat(y[:, :, :]), flat(gate[:, :, :]))])
            to_columns(nc, m, y, TT, yT)
        output_product(nc, m, yT, NSA_OUT // P, a["nsa_w_out"][0], x)


def nsa_attention(nc, m, a, qT, ks, kw, k_cmp, vs, vw, v_cmp, gates, y):
    with Tensors(nc) as sb:
        q_here = sb("q_here", [P, SEQ])
        causal = sb("causal", [P, SEQ])
        cmp_tab = sb("cmp_tab", [P, TT, 32])
        sees_any = sb("sees_any", [P, 1])
        slopes = sb("slopes", [P, NSA_HEADS])
        with stage(nc, "loaded") as (block, s):
            @block.sync
            def _(sp):
                sp.dma_start(causal[:, :], a["dist_causal"]).then_inc(s.loaded, 16)
                sp.dma_start(cmp_tab[:, :, :], a["dist_cmp"]).then_inc(s.loaded, 16)
                sp.dma_start(sees_any[:, :], a["sees_any"]).then_inc(s.loaded, 16)
                sp.dma_start(slopes[:, :], a["nsa_slopes"].partition_broadcast(P)).then_inc(s.loaded, 16)
                sp.wait_ge(s.loaded, 64)

            @block.vector
            def _(dve):
                dve.wait_ge(s.loaded, 64)
                g = gates[:, 0, 0:3 * NSA_HEADS:3]
                dve.tensor_scalar(g, g, sees_any[:, 0:1], None, ALU.mult)
        for g in range(NSA_GROUPS):
            items = []
            for h in range(2):
                rows = slice(64 * h, 64 * h + 64)
                for t in range(TT):
                    q = q_here[rows, t * P:(t + 1) * P]
                    reach = (t + 1) * P

                    def slope(i, g=g, h=h):
                        return slopes[:, bass.ds(2 * i + (8 * g + h), 1)]

                    def dst(i, g=g, h=h, t=t):
                        return y[:, t, bass.ds(i * P + (512 * g + 64 * h), NSA_HD)]

                    def gate(b):
                        return lambda i, g=g, h=h, t=t: gates[:, t, bass.ds(6 * i + (24 * g + 3 * h + b), 1)]

                    items.append(dict(
                        segs=[seg(q, lambda i, g=g, rows=rows: k_cmp[rows, g, :], 32, 0, cmp_tab[:, t, :], slope)],
                        scale=NSA_HD ** -0.5, hd=NSA_HD, coef=gate(0), dst=dst,
                        values=[(0, N_CMP, lambda i, g=g: v_cmp[0:N_CMP, g * NSA_HD:(g + 1) * NSA_HD])]))
                    for b, (k_, v_) in enumerate(((ks, vs), (kw, vw))):
                        items.append(dict(
                            segs=[seg(q, lambda i, k_=k_, g=g, rows=rows, reach=reach: k_[rows, g, 0:reach], reach, 0,
                                      causal[:, SEQ - reach:], slope)],
                            scale=NSA_HD ** -0.5, hd=NSA_HD, coef=gate(b + 1), dst=dst, add=True,
                            values=[(j * P, P, lambda i, v_=v_, j=j, g=g: v_[:, j, g * NSA_HD:(g + 1) * NSA_HD])
                                    for j in range(t + 1)]))
            attention(nc, m, 4, [(q_here[:, :], lambda i, g=g: one(qT, i + 4 * g))], items, SEQ, 1, 2)




def rope_tables(nc, m, a, cos, sin):
    magic = 1.5 * 2.0 ** 23
    c1 = 6.28125
    c2 = float(np.float32(np.round((2 * np.pi - c1) * 2 ** 21) / 2 ** 21))
    c3 = float(np.float32(2 * np.pi - c1 - c2))
    with Tensors(nc) as sb, stage(nc, "loaded", "step", "reduced") as (block, s):
        pos = sb("pos", [P, SEQ], I32)
        posf = sb("posf", [P, SEQ])
        freq = sb("freq", [P, 1])
        ang = sb("ang", [P, SEQ])
        turns = sb("turns", [P, SEQ])

        @block.sync
        def _(sp):
            sp.dma_start(pos[:, :], a["positions_2"].partition_broadcast(P)).then_inc(s.loaded, 16)
            sp.dma_start(freq[:, :], a["rope_freq"]).then_inc(s.loaded, 16)

        @block.vector
        def _(dve):
            count = 0

            def link(ins):
                nonlocal count
                count += 1
                ins.then_inc(s.step, 1)
                dve.wait_ge(s.step, count)

            dve.wait_ge(s.loaded, 32)
            link(dve.tensor_copy(posf[:, :], pos[:, :]))
            link(dve.tensor_scalar(ang[:, :], posf[:, :], freq[:, 0:1], None, ALU.mult))
            for dst, quarter in ((sin, 0.0), (cos, 0.25)):
                link(dve.tensor_scalar(turns[:, :], ang[:, :], 1 / (2 * np.pi), quarter, ALU.mult, ALU.add))
                link(dve.tensor_scalar(turns[:, :], turns[:, :], magic, None, ALU.add))
                link(dve.tensor_scalar(turns[:, :], turns[:, :], -magic, None, ALU.add))
                src = ang
                for c in (c1, c2, c3):
                    link(dve.scalar_tensor_tensor(out=dst[:, :], in0=turns[:, :], scalar=-c, in1=src[:, :],
                                                  op0=ALU.mult, op1=ALU.add))
                    src = dst
                if quarter:
                    link(dve.tensor_scalar(dst[:, :], dst[:, :], np.pi / 2, None, ALU.add))
                top = float(np.nextafter(np.float32(np.pi), np.float32(0)))
                link(dve.tensor_scalar(dst[:, :], dst[:, :], top, -top, ALU.min, ALU.max))
            dve.sem_inc(s.reduced, 1)

        @block.scalar
        def _(act):
            act.wait_ge(s.reduced, 1)
            act.activation(sin[:, :], sin[:, :], ACT.Sin)
            act.activation(cos[:, :], cos[:, :], ACT.Sin)


def rope(nc, m, tensors, cos, sin):
    with Tensors(nc) as sb, stage(nc, "rotated", "straight", "crossed", "summed") as (block, s):
        a_ = sb("straight", [P, 2, SEQ])
        b_ = sb("crossed", [P, 2, SEQ])
        n_tiles = tensors[0].shape[1]

        def tiles(eng):
            for w, t in enumerate(tensors):
                with eng.Fori(0, n_tiles // 2) as i:
                    for u in range(2):
                        yield t, 2 * i + u, u, 2 * i + (w * n_tiles + u)


        @block.tensor
        def _(pe):
            for t, tile, u, q in tiles(pe):
                pe.wait_ge(s.summed, q + 1)
                pe.matmul(m.ps[:, u * BANK:(u + 1) * BANK], m.rotate[:, :], one(t, tile), start=True, stop=True).then_inc(s.rotated, 1)

        @block.gpsimd
        def _(pool):
            for t, tile, u, q in tiles(pool):
                pool.wait_ge(s.summed, q + 1)
                pool.tensor_tensor(a_[:, u, :], one(t, tile), cos[:, :], ALU.mult).then_inc(s.straight, 1)

        @block.vector
        def _(dve):
            dve.sem_inc(s.summed, 2)
            for t, tile, u, q in tiles(dve):
                dve.wait_ge(s.rotated, q + 1)
                dve.tensor_tensor(b_[:, u, :], m.ps[:, u * BANK:(u + 1) * BANK], sin[:, :], ALU.mult).then_inc(s.crossed, 1)
                dve.wait_ge(s.crossed, q + 1)
                dve.wait_ge(s.straight, q + 1)
                dve.tensor_tensor(one(t, tile), a_[:, u, :], b_[:, u, :], ALU.add).then_inc(s.summed, 1)


def diff_lambda(nc, m, a, layer, minus_lam):
    init = 0.8 - 0.6 * float(np.exp(-0.3 * layer))
    with Tensors(nc) as sb, stage(nc, "loaded", "step", "exped") as (block, s):
        v = sb("lambda_rows", [P, 4, 64])
        prod = sb("prod", [P, 2, 64])
        dots = sb("dots", [P, 2])
        ex = sb("exps", [P, 2])

        @block.sync
        def _(sp):
            for i, name in enumerate(("q1", "q2", "k1", "k2")):
                sp.dma_start(v[:, i, :], a[f"lambda_{name}_2"][layer:layer + 1, :].partition_broadcast(P)).then_inc(s.loaded, 16)

        @block.vector
        def _(dve):
            dve.wait_ge(s.loaded, 64)
            dve.tensor_tensor(prod[:, :, :], v[:, 0:2, :], v[:, 2:4, :], ALU.mult).then_inc(s.step, 1)
            dve.wait_ge(s.step, 1)
            dve.tensor_reduce(dots[:, :], prod[:, :, :], AX_X, ALU.add).then_inc(s.step, 1)
            dve.wait_ge(s.exped, 1)
            dve.tensor_tensor(dots[:, 0:1], ex[:, 1:2], ex[:, 0:1], ALU.subtract).then_inc(s.step, 1)
            dve.wait_ge(s.step, 3)
            dve.tensor_scalar(minus_lam[:, :], dots[:, 0:1], -init, None, ALU.add)

        @block.scalar
        def _(act):
            act.wait_ge(s.step, 2)
            act.activation(ex[:, :], dots[:, :], ACT.Exp).then_inc(s.exped, 1)


def diff_attention(nc, m, a, qT, kT, v, minus_lam, y):
    with Tensors(nc) as sb:
        q_here = sb("q_here", [P, SEQ])
        k_here = sb("k_here", [P, SEQ])
        mask = sb("mask", [P, SEQ])
        with stage(nc, "loaded") as (block, s):
            @block.sync
            def _(sp):
                sp.dma_start(mask[:, :], a["mask_causal"]).then_inc(s.loaded, 16)
                sp.wait_ge(s.loaded, 16)
        items = []
        for t in range(TT):
            for c in range(2):
                rows = slice(64 * c, 64 * c + 64)
                reach = (t + 1) * P
                items.append(dict(
                    segs=[seg(q_here[rows, t * P:(t + 1) * P], lambda i, rows=rows, reach=reach: k_here[rows, 0:reach],
                              reach, 0, mask[:, SEQ - reach:])],
                    scale=0.125, hd=DA_V, add=c == 1, coef=(lambda i: minus_lam[:, 0:1]) if c else None,
                    dst=lambda i, t=t: y[:, t, bass.ds(i * P, P)],
                    values=[(j * P, P, lambda i, j=j: v[:, j, bass.ds(i * P, P)]) for j in range(t + 1)]))
        attention(nc, m, DA_HEADS, [(q_here[:, :], lambda i: one(qT, i)), (k_here[:, :], lambda i: one(kT, i))],
                  items, SEQ, 1, 2)


def head_norm(nc, m, y, factor):
    n = TT * DA_HEADS
    with Tensors(nc) as sb, stage(nc, "squared", "step", "rooted") as (block, s):
        sq = sb("squares", [P, n, P])
        sums, root, inv = (sb(x, [P, n]) for x in ("sums", "root", "inv"))
        heads = flat(y[:, :, :]).rearrange("p (n d) -> p n d", d=P)

        @block.scalar
        def _(act):
            act.activation(flat(sq[:, :, :]), flat(y[:, :, :]), ACT.Square).then_inc(s.squared, 1)
            act.wait_ge(s.step, 2)
            act.activation(root[:, :], sums[:, :], ACT.Sqrt).then_inc(s.rooted, 1)

        @block.vector
        def _(dve):
            dve.wait_ge(s.squared, 1)
            dve.tensor_reduce(sums[:, :], sq[:, :, :], AX_X, ALU.add).then_inc(s.step, 1)
            dve.wait_ge(s.step, 1)
            dve.tensor_scalar(sums[:, :], sums[:, :], 1.0 / P, LN_EPS, ALU.mult, ALU.add).then_inc(s.step, 1)
            dve.wait_ge(s.rooted, 1)
            dve.reciprocal(inv[:, :], root[:, :]).then_inc(s.step, 1)
            dve.wait_ge(s.step, 3)
            refine_rsqrt(dve, s.step, 3, sums[:, :], inv[:, :], root[:, :])
            dve.tensor_scalar(inv[:, :], inv[:, :], factor, None, ALU.mult).then_inc(s.step, 1)
            dve.wait_ge(s.step, 7)
            dve.tensor_tensor(heads, heads, inv[:, :].unsqueeze(2).broadcast_to([P, n, P]), ALU.mult)


def gated_conv(nc, m, cb, cc, cu, weights, yT):
    K = CONV2 // P
    with Tensors(nc) as sb, stage(nc, "step") as (block, s):
        z = sb("z", [P, K, 2 + SEQ])

        @block.vector
        def _(dve):
            dve.memset(z[:, :, 0:2], 0.0).then_inc(s.step, 1)
            dve.tensor_tensor(z[:, :, 2:], cc[:, :, :], cu[:, :, :], ALU.mult).then_inc(s.step, 1)
            dve.wait_ge(s.step, 2)
            for j in range(3):
                if j:
                    dve.wait_ge(s.step, 2 + K * j)
                for k in range(K):
                    col = weights[:, j * K + k:j * K + k + 1]
                    if j == 0:
                        ins = dve.tensor_scalar(yT[:, k, :], z[:, k, 0:SEQ], col, None, ALU.mult)
                    else:
                        ins = dve.scalar_tensor_tensor(out=yT[:, k, :], in0=z[:, k, j:j + SEQ], scalar=col, in1=yT[:, k, :],
                                                       op0=ALU.mult, op1=ALU.add)
                    ins.then_inc(s.step, 1)
            dve.wait_ge(s.step, 2 + 3 * K)
            dve.tensor_tensor(yT[:, :, :], yT[:, :, :], cb[:, :, :], ALU.mult)


def merge_branches(nc, m, xT, w_gates, branches, mergedT):
    steps = [(n, b) for n in range(2) for b in range(3)]
    with Tensors(nc) as sb, stage(nc, "w_gate_loaded", "w_branch_loaded", "gate_ready", "product_ready", "gated",
                                  "multiplied", "added") as (block, s):
        sig = sb("sig", [P, 4, SEQ])
        prod = sb("prod", [P, 2, SEQ])

        @block.sync
        def _(sp):
            for q, (n, b) in enumerate(steps):
                col = b * D + n * 512
                yT, w, K = branches[b]
                if q:
                    sp.wait_ge(s.gate_ready, 4 * q)
                sp.dma_start(m.w_slots[0][:, :, :], w_gates[:, col:col + 512].rearrange("(k p) n -> p k n", p=P)).then_inc(s.w_gate_loaded, 16)
                if q:
                    sp.wait_ge(s.product_ready, 4 * q)
                sp.dma_start(m.w_slots[1][:, 0:K, :], w[:, n * 512:(n + 1) * 512].rearrange("(k p) n -> p k n", p=P)).then_inc(s.w_branch_loaded, 16)

        @block.tensor
        def _(pe):
            for q, (n, b) in enumerate(steps):
                yT, w, K = branches[b]
                pe.wait_ge(s.w_gate_loaded, 16 * q + 16)
                for j in range(4):
                    if q:
                        pe.wait_ge(s.gated, 4 * (q - 1) + j + 1)
                    for k in range(DK):
                        mm = pe.matmul(m.ps[:, j * BANK:(j + 1) * BANK], m.w_slots[0][:, k, j * P:(j + 1) * P], xT[:, k, :],
                                       start=k == 0, stop=k == DK - 1)
                    mm.then_inc(s.gate_ready, 1)
                pe.wait_ge(s.w_branch_loaded, 16 * q + 16)
                for j in range(4):
                    if q:
                        pe.wait_ge(s.multiplied, 4 * (q - 1) + j + 1)
                    for k in range(K):
                        mm = pe.matmul(m.ps[:, (4 + j) * BANK:(5 + j) * BANK], m.w_slots[1][:, k, j * P:(j + 1) * P], yT[:, k, :],
                                       start=k == 0, stop=k == K - 1)
                    mm.then_inc(s.product_ready, 1)

        @block.scalar
        def _(act):
            for q in range(len(steps)):
                for j in range(4):
                    act.wait_ge(s.gate_ready, 4 * q + j + 1)
                    if q:
                        act.wait_ge(s.multiplied, 4 * (q - 1) + j + 1)
                    act.activation(sig[:, j, :], m.ps[:, j * BANK:(j + 1) * BANK], ACT.Sigmoid).then_inc(s.gated, 1)

        @block.vector
        def _(dve):
            added = 0
            for q, (n, b) in enumerate(steps):
                for j in range(4):
                    dve.wait_ge(s.gated, 4 * q + j + 1)
                    dve.wait_ge(s.product_ready, 4 * q + j + 1)
                    dst = mergedT[:, 4 * n + j, :]
                    to = prod[:, j % 2, :] if b else dst
                    dve.tensor_tensor(to, sig[:, j, :], m.ps[:, (4 + j) * BANK:(5 + j) * BANK], ALU.mult).then_inc(s.multiplied, 1)
                    if b:
                        dve.wait_ge(s.multiplied, 4 * q + j + 1)
                        if b == 2:
                            dve.wait_ge(s.added, added - 3)
                        dve.tensor_tensor(dst, dst, prod[:, j % 2, :], ALU.add).then_inc(s.added, 1)
                        added += 1


def route(nc, m, a, xT, x, moe):
    G, E = N_EGROUPS, PER_GROUP
    with Tensors(nc) as sb, stage(nc, "loaded", "logits_ready", "step", "centred", "exped", "chosen", "ranked",
                                  "placed", "copied") as (block, s):
        w = sb("w_router", [P, DK, N_EXPERTS])
        bias = sb("bias", [P, N_EXPERTS])
        lg = sb("logits", [P, TT, N_EXPERTS])
        sc = sb("scores", [P, TT, N_EXPERTS])
        one_, two, best = (sb(n, [P, TT]) for n in ("one", "two", "best"))
        gm, gsel, hit, first, second, inside = (sb(n, [P, TT, 4]) for n in (
            "group_top", "group_sel", "hit", "first", "second", "inside"))
        avail = sb("avail", [P, TT, 1])
        tmp = sb("tmp", [P, TT, N_EXPERTS])
        pick = [sb("pick_first", [P, TT, N_EXPERTS]), sb("pick_second", [P, TT, N_EXPERTS])]
        picked = sb("picked", [P, TT, N_EXPERTS])
        place = sb("place", [P, TT, N_EXPERTS])
        slot = sb("slot", [P, TT, 2])
        cnt, nblk, end = (sb(n, [P, N_EXPERTS]) for n in ("count", "blocks", "block_end"))
        number = sb("block_number", [P, MAX_BLOCKS])
        before = sb("before", [P, P])
        ones = sb("ones", [P, P])
        by_block = sb("by_block", [P, MAX_BLOCKS, N_EXPERTS])
        owner = sb("owner", [P, MAX_BLOCKS])

        @block.sync
        def _(sp):
            sp.dma_start(w[:, :, :], a["w_router_2"].rearrange("(k p) n -> p k n", p=P)).then_inc(s.loaded, 16)
            sp.dma_start(bias[:, :], a["router_bias_2"].rearrange("(a n) -> a n", a=1).partition_broadcast(P)).then_inc(s.loaded, 16)
            sp.dma_start(number[:, :], a["block_number"].partition_broadcast(P)).then_inc(s.loaded, 16)
            sp.dma_start(before[:, :], a["before"]).then_inc(s.loaded, 16)

        @block.tensor
        def _(pe):
            pe.wait_ge(s.loaded, 64)
            for t in range(TT):
                for k in range(DK):
                    mm = pe.matmul(m.ps[:, t * N_EXPERTS:(t + 1) * N_EXPERTS], xT[:, k, t * P:(t + 1) * P], w[:, k, :],
                                   start=k == 0, stop=k == DK - 1)
            mm.then_inc(s.logits_ready, 1)
            pe.wait_ge(s.chosen, 1)
            for t in range(TT):
                out = m.ps[:, BANK + t * N_EXPERTS:BANK + (t + 1) * N_EXPERTS]
                for u in range(t):
                    pe.matmul(out, ones[:, :], picked[:, u, :], start=u == 0, stop=False)
                pe.matmul(out, before[:, :], picked[:, t, :], start=t == 0, stop=True)
            for t in range(TT):
                mm = pe.matmul(m.ps[:, 2 * BANK:2 * BANK + N_EXPERTS], ones[:, :], picked[:, t, :], start=t == 0, stop=t == TT - 1)
            mm.then_inc(s.ranked, 1)

        @block.scalar
        def _(act):
            act.wait_ge(s.centred, 1)
            act.activation(flat(sc[:, :, :]), flat(lg[:, :, :]), ACT.Exp).then_inc(s.exped, 1)

        @block.gpsimd
        def _(pool):
            pool.wait_ge(s.placed, 1)
            pool.wait_ge(moe.cleared, 32)
            for t in range(TT):
                for i in range(2):
                    pool.indirect_dma_start(out=moe.x_rows, out_offset=bass.IndirectOffsetOnAxis(ap=moe.slot[:, 2 * t + i:2 * t + i + 1], axis=0),
                                            in_=x[:, t, :], in_offset=None).then_inc(s.copied, 16)
            pool.wait_ge(s.copied, 16 * 2 * TT)

        @block.vector
        def _(dve):
            count = 0

            def link(ins):
                nonlocal count
                count += 1
                ins.then_inc(s.step, 1)
                dve.wait_ge(s.step, count)

            def tt(out, x, y, op):
                link(dve.tensor_tensor(out, x, y, op))

            def spread(v, n):
                return v.unsqueeze(2).broadcast_to([P, TT, n])

            def first_of(out, values, top):
                tt(hit[:, :, :], values, spread(top, 4), ALU.is_equal)
                link(dve.memset(avail[:, :, :], 1.0))
                for j in range(4):
                    tt(out[:, :, j:j + 1], hit[:, :, j:j + 1], avail[:, :, :], ALU.mult)
                    tt(avail[:, :, :], avail[:, :, :], out[:, :, j:j + 1], ALU.subtract)

            link(dve.memset(ones[:, :], 1.0))
            dve.wait_ge(s.logits_ready, 1)
            tt(lg[:, :, :], m.ps[:, 0:TT * N_EXPERTS].rearrange("p (t e) -> p t e", t=TT),
               bias[:, :].unsqueeze(1).broadcast_to([P, TT, N_EXPERTS]), ALU.add)
            link(dve.tensor_reduce(best[:, :], lg[:, :, :], AX_X, ALU.max))
            tt(lg[:, :, :], lg[:, :, :], spread(best[:, :], N_EXPERTS), ALU.subtract)
            dve.sem_inc(s.centred, 1)
            dve.wait_ge(s.exped, 1)
            link(dve.tensor_reduce(one_[:, :], sc[:, :, :], AX_X, ALU.add))
            link(dve.reciprocal(two[:, :], one_[:, :]))
            tt(sc[:, :, :], sc[:, :, :], spread(two[:, :], N_EXPERTS), ALU.mult)
            link(dve.tensor_reduce(gm[:, :, :], sc[:, :, :].rearrange("p t (g e) -> p t g e", g=G), AX_X, ALU.max))
            link(dve.tensor_reduce(best[:, :], gm[:, :, :], AX_X, ALU.max))
            first_of(gsel[:, :, :], gm[:, :, :], best[:, :])
            for g in range(G):
                mine = sc[:, :, g * E:(g + 1) * E]
                sel = gsel[:, :, g:g + 1].broadcast_to([P, TT, E])
                if g == 0:
                    tt(inside[:, :, :], mine, sel, ALU.mult)
                else:
                    tt(tmp[:, :, 0:E], mine, sel, ALU.mult)
                    tt(inside[:, :, :], inside[:, :, :], tmp[:, :, 0:E], ALU.add)
            first_of(first[:, :, :], inside[:, :, :], best[:, :])
            link(dve.scalar_tensor_tensor(out=tmp[:, :, 0:E], in0=first[:, :, :], scalar=-2.0, in1=inside[:, :, :],
                                          op0=ALU.mult, op1=ALU.add))
            link(dve.tensor_reduce(two[:, :], tmp[:, :, 0:E], AX_X, ALU.max))
            first_of(second[:, :, :], tmp[:, :, 0:E], two[:, :])
            for p_, chosen in zip(pick, (first, second)):
                for g in range(G):
                    tt(p_[:, :, g * E:(g + 1) * E], chosen[:, :, :], gsel[:, :, g:g + 1].broadcast_to([P, TT, E]), ALU.mult)
            tt(picked[:, :, :], pick[0][:, :, :], pick[1][:, :, :], ALU.add)
            dve.sem_inc(s.chosen, 1)
            tt(one_[:, :], best[:, :], two[:, :], ALU.add)
            link(dve.reciprocal(one_[:, :], one_[:, :]))
            tt(moe.share[:, :, 0], best[:, :], one_[:, :], ALU.mult)
            tt(moe.share[:, :, 1], two[:, :], one_[:, :], ALU.mult)
            dve.wait_ge(s.ranked, 1)
            dve.wait_ge(s.loaded, 64)
            link(dve.tensor_copy(cnt[:, :], m.ps[:, 2 * BANK:2 * BANK + N_EXPERTS]))
            link(dve.tensor_scalar(nblk[:, :], cnt[:, :], 0.0, None, ALU.is_gt))
            for j in range(1, TT):
                link(dve.scalar_tensor_tensor(out=nblk[:, :], in0=cnt[:, :], scalar=float(j * P), in1=nblk[:, :],
                                              op0=ALU.is_gt, op1=ALU.add))
            link(dve.tensor_tensor_scan(end[:, :], ones[:, 0:N_EXPERTS], nblk[:, :], 0.0, ALU.mult, ALU.add))
            tt(cnt[:, :], end[:, :], nblk[:, :], ALU.subtract)
            link(dve.scalar_tensor_tensor(out=place[:, :, :], in0=cnt[:, :].unsqueeze(1).broadcast_to([P, TT, N_EXPERTS]),
                                          scalar=float(P), in1=m.ps[:, BANK:BANK + TT * N_EXPERTS].rearrange("p (t e) -> p t e", t=TT),
                                          op0=ALU.mult, op1=ALU.add))
            for i in range(2):
                tt(tmp[:, :, :], pick[i][:, :, :], place[:, :, :], ALU.mult)
                link(dve.tensor_reduce(slot[:, :, i], tmp[:, :, :], AX_X, ALU.add))
            link(dve.tensor_copy(moe.slot[:, :], flat(slot[:, :, :])))
            dve.sem_inc(s.placed, 1)
            tt(by_block[:, :, :], end[:, :].unsqueeze(1).broadcast_to([P, MAX_BLOCKS, N_EXPERTS]),
               number[:, :].unsqueeze(2).broadcast_to([P, MAX_BLOCKS, N_EXPERTS]), ALU.is_le)
            link(dve.tensor_reduce(owner[:, :], by_block[:, :, :], AX_X, ALU.add))
            link(dve.tensor_scalar(moe.block_expert[:, :], owner[:, :], float(N_EXPERTS - 1), None, ALU.min))
            link(dve.tensor_scalar(owner[:, 0:MAX_BLOCKS // 2], number[:, 0:MAX_BLOCKS:2], end[:, N_EXPERTS - 1:N_EXPERTS],
                                   None, ALU.is_lt))
            link(dve.tensor_reduce(cnt[:, 0:1], owner[:, 0:MAX_BLOCKS // 2], AX_X, ALU.add))
            link(dve.tensor_copy(moe.n_pairs[:, :], cnt[:, 0:1]))


def experts(nc, m, a, layer, moe):
    F = D_FF // P
    with Tensors(nc) as sb, stage(nc, "x_loaded*2", "up_loaded*2", "down_loaded*2", "x_turned*2", "xT_ready*2", "gate_ready*2",
                                  "up_ready*2", "silu_done*2", "hidden_done*2", "h_turned*2", "hT_ready*2", "out_ready*2",
                                  "out_taken*2", "y_stored*2", "y_left*2") as (block, s):
        wg = m.w_slots
        wu = [sb("w_up", [P, DK, D_FF]) for _ in range(2)]
        wd = [sb("w_down", [P, F, D]) for _ in range(2)]
        xe = [sb("block_x", [P, D]) for _ in range(2)]
        xeT = [sb("block_xT", [P, DK, P]) for _ in range(2)]
        sg = [sb("silu", [P, D_FF]) for _ in range(2)]
        h = [sb("hidden", [P, D_FF]) for _ in range(2)]
        hT = [sb("hidden_T", [P, F, P]) for _ in range(2)]
        ye = [sb("block_y", [P, D]) for _ in range(2)]
        x_banks, gate_bank, up_bank, turn_bank, out_banks = ((0, 1), (6, 7)), (2, 4), (3, 5), (0, 1), ((6, 7), (2, 3))

        def bank(b):
            return m.ps[:, b * BANK:(b + 1) * BANK]

        def n_pairs(eng):
            return eng.value_load(moe.n_pairs[0:1, 0:1], min_val=1, max_val=MAX_BLOCKS // 2)


        @block.sync
        def _(sp):
            with sp.Fori(0, n_pairs(sp)) as i:
                expert = [None, None]
                for u in range(2):
                    b = 2 * i + u
                    expert[u] = sp.value_load(moe.block_expert[0:1, bass.ds(b, 1)], min_val=0, max_val=N_EXPERTS - 1)
                    sp.wait_ge(s.up_ready[u], i + 1)
                    sp.dma_start(xe[u][:, :], moe.x_rows[bass.ds(b * P, P), :]).then_inc(s.x_loaded[u], 16)
                    for w, name in ((wg[u], "w_exp_gate_2"), (wu[u], "w_exp_up_2")):
                        src = a[name][layer][bass.ds(expert[u], 1), :, :].rearrange("e (k p) n -> p (e k) n", p=P)
                        sp.dma_start(w[:, :, :], src).then_inc(s.up_loaded[u], 16)
                for u in range(2):
                    sp.wait_ge(s.out_ready[u], 2 * i + 1)
                    src = a["w_exp_down_2"][layer][bass.ds(expert[u], 1), :, :].rearrange("e (k p) n -> p (e k) n", p=P)
                    sp.dma_start(wd[u][:, :, :], src).then_inc(s.down_loaded[u], 16)

        @block.tensor
        def _(pe):
            for u in range(2):
                pe.sem_inc(s.up_ready[u], 1)
                pe.sem_inc(s.out_ready[u], 1)

            def turn_x(i, u):
                pe.wait_ge(s.x_loaded[u], 16 * i + 16)
                if u:
                    pe.wait_ge(s.out_taken[0], 2 * i + 1)
                for half in range(2):
                    for k in range(4):
                        mm = pe.transpose(m.ps[:, x_banks[u][half] * BANK + k * P:x_banks[u][half] * BANK + (k + 1) * P],
                                          xe[u][:, (4 * half + k) * P:(4 * half + k + 1) * P], m.ident[:, :])
                    mm.then_inc(s.x_turned[u], 1)

            def project(i, u, w, out, done):
                for k in range(DK):
                    mm = pe.matmul(bank(out), xeT[u][:, k, :], w[:, k, :], start=k == 0, stop=k == DK - 1)
                mm.then_inc(done, 1)

            def gate(i, u):
                pe.wait_ge(s.xT_ready[u], 2 * i + 2)
                pe.wait_ge(s.up_loaded[u], 32 * i + 32)
                if u == 0:
                    pe.wait_ge(s.out_taken[1], 2 * i + 1)
                project(i, u, wg[u], gate_bank[u], s.gate_ready[u])

            def turn_h(i, u):
                pe.wait_ge(s.hidden_done[u], i + 1)
                for k in range(F):
                    mm = pe.transpose(m.ps[:, turn_bank[u] * BANK + k * P:turn_bank[u] * BANK + (k + 1) * P],
                                      h[u][:, k * P:(k + 1) * P], m.ident[:, :])
                mm.then_inc(s.h_turned[u], 1)

            def down(i, u):
                pe.wait_ge(s.hT_ready[u], i + 1)
                pe.wait_ge(s.down_loaded[u], 16 * i + 16)
                for n in range(2):
                    for k in range(F):
                        mm = pe.matmul(bank(out_banks[u][n]), hT[u][:, k, :], wd[u][:, k, n * 512:(n + 1) * 512],
                                       start=k == 0, stop=k == F - 1)
                    mm.then_inc(s.out_ready[u], 1)

            with pe.Fori(0, n_pairs(pe)) as i:
                turn_x(i, 0)
                turn_x(i, 1)
                gate(i, 0)
                project(i, 0, wu[0], up_bank[0], s.up_ready[0])
                gate(i, 1)
                turn_h(i, 0)
                project(i, 1, wu[1], up_bank[1], s.up_ready[1])
                down(i, 0)
                turn_h(i, 1)
                down(i, 1)

        @block.scalar
        def _(act):
            with act.Fori(0, n_pairs(act)) as i:
                for u in range(2):
                    act.wait_ge(s.x_turned[u], 2 * i + 1)
                    act.activation(flat(xeT[u][:, 0:4, :]), bank(x_banks[u][0]), ACT.Copy).then_inc(s.xT_ready[u], 1)
                for u in range(2):
                    act.wait_ge(s.gate_ready[u], i + 1)
                    act.activation(sg[u][:, :], bank(gate_bank[u]), ACT.Silu).then_inc(s.silu_done[u], 1)
                for u in range(2):
                    act.wait_ge(s.h_turned[u], i + 1)
                    act.activation(flat(hT[u][:, :, :]), bank(turn_bank[u]), ACT.Copy).then_inc(s.hT_ready[u], 1)

        @block.vector
        def _(dve):
            for u in range(2):
                dve.sem_inc(s.out_taken[u], 1)
                dve.sem_inc(s.y_left[u], 1)
            with dve.Fori(0, n_pairs(dve)) as i:
                for u in range(2):
                    dve.wait_ge(s.x_turned[u], 2 * i + 2)
                    dve.tensor_copy(flat(xeT[u][:, 4:8, :]), bank(x_banks[u][1])).then_inc(s.xT_ready[u], 1)
                for u in range(2):
                    dve.wait_ge(s.silu_done[u], i + 1)
                    dve.wait_ge(s.up_ready[u], i + 2)
                    dve.tensor_tensor(h[u][:, :], sg[u][:, :], bank(up_bank[u]), ALU.mult).then_inc(s.hidden_done[u], 1)
                for u in range(2):
                    dve.wait_ge(s.y_left[u], i + 1)
                    for n in range(2):
                        dve.wait_ge(s.out_ready[u], 2 * i + (n + 2))
                        dve.tensor_copy(ye[u][:, n * 512:(n + 1) * 512], bank(out_banks[u][n])).then_inc(s.out_taken[u], 1)

        @block.gpsimd
        def _(pool):
            with pool.Fori(0, n_pairs(pool)) as i:
                for u in range(2):
                    pool.wait_ge(s.out_taken[u], 2 * i + 3)
                    pool.dma_start(moe.y_rows[bass.ds((2 * i + u) * P, P), :], ye[u][:, :]).then_inc(s.y_stored[u], 16)
                for u in range(2):
                    pool.wait_ge(s.y_stored[u], 16 * i + 16)
                    pool.sem_inc(s.y_left[u], 1)


def clear_rows(nc, m, moe, zeros):
    with stage(nc, "zeroed") as (block, s):
        @block.vector
        def _(dve):
            dve.memset(zeros[:, :], 0.0).then_inc(s.zeroed, 1)

        @block.gpsimd
        def _(pool):
            pool.wait_ge(s.zeroed, 1)
            for rows in (moe.x_rows, moe.y_rows):
                pool.dma_start(rows.rearrange("(b p) d -> p b d", p=P),
                               zeros[:, :].unsqueeze(1).broadcast_to([P, MAX_BLOCKS, D])).then_inc(moe.cleared, 16)


def combine_experts(nc, m, x, moe):
    with Tensors(nc) as sb, stage(nc, "fetched*8", "scaled", "added") as (block, s):
        rows = sb("expert_rows", [P, 2 * TT, D])

        @block.gpsimd
        def _(pool):
            for n in range(2 * TT):
                pool.indirect_dma_start(out=rows[:, n, :], out_offset=None, in_=moe.y_rows,
                                        in_offset=bass.IndirectOffsetOnAxis(ap=moe.slot[:, n:n + 1], axis=0)).then_inc(s.fetched[n], 16)

        @block.vector
        def _(dve):
            for t in range(TT):
                dve.tensor_scalar(x[:, t, :], x[:, t, :], ALPHA, None, ALU.mult).then_inc(s.scaled, 1)
            dve.wait_ge(s.scaled, TT)
            for i in range(2):
                for t in range(TT):
                    if i:
                        dve.wait_ge(s.added, t + 1)
                    dve.wait_ge(s.fetched[2 * t + i], 16)
                    dve.scalar_tensor_tensor(out=x[:, t, :], in0=rows[:, 2 * t + i, :], scalar=moe.share[:, t, i:i + 1],
                                             in1=x[:, t, :], op0=ALU.mult, op1=ALU.add).then_inc(s.added, 1)


def second_layer(nc, m, a, x, layer, cos, sin, memT, moe):
    w = a["w_in_2"][layer]
    init = 0.8 - 0.6 * float(np.exp(-0.3 * layer))

    def job(name, chunks, width, kind, take):
        return dict(w=w, col=IN2[name], chunks=chunks, width=width, kind=kind, take=take)

    with Tensors(nc) as sb:
        xT = sb("x_cols", [P, DK, SEQ])
        to_columns(nc, m, x, TT, xT)
        with Tensors(nc) as sb0:
            ybT = [sb0("attn_T", [P, 8, SEQ]), sb0("conv_T", [P, 4, SEQ]), sb0("mem_T", [P, 4, SEQ])]
            with Tensors(nc) as sb1:
                cb, cc, cu = (sb1(n, [P, 4, SEQ]) for n in ("cb", "cc", "cu"))
                qmT = sb1("qmT", [P, 4, SEQ])
                kmT = sb1("kmT", [P, 4, N_MEM])
                vm = sb1("vm", [P, MT, 512])
                y = sb1("y_rows", [P, TT, 512])
                projection(nc, m, xT, DK, [
                    job("cb", 1, 512, "T", take_T(cb)),
                    job("cc", 1, 512, "T", take_T(cc)),
                    job("cu", 1, 512, "T", take_T(cu)),
                    job("qm", 1, 512, "T", take_T(qmT)),
                ])
                gated_conv(nc, m, cb, cc, cu, m.col["conv_w_2"][:, 12 * layer:12 * layer + 12], ybT[1])
                memory_kv(nc, m, memT, a["w_mem_kv_2"][layer], 512, kmT, vm)
                memory_attention(nc, m, MEM2_HEADS, MEM2_HD, qmT, kmT, vm, y, 0)
                to_columns(nc, m, y, TT, ybT[2])
            with Tensors(nc) as sb1:
                qT = sb1("qT", [P, 8, SEQ])
                kT = sb1("kT", [P, 8, SEQ])
                v = sb1("v", [P, TT, D])
                y = sb1("y_rows", [P, TT, D])
                minus_lam = sb1("minus_lam", [P, 1])
                projection(nc, m, xT, DK, [
                    job("q", 2, 512, "T", take_T(qT)),
                    job("k", 2, 512, "T", take_T(kT)),
                    job("v", 2, 512, "N", take_N(v)),
                ])
                rope(nc, m, [qT, kT], cos, sin)
                diff_lambda(nc, m, a, layer, minus_lam)
                diff_attention(nc, m, a, qT, kT, v, minus_lam, y)
                head_norm(nc, m, y, 1.0 - init)
                to_columns(nc, m, y, TT, ybT[0], m.col["diff_subln_g_2"][:, layer:layer + 1].broadcast_to([P, DK]))
            mergedT = sb0("merged_T", [P, DK, SEQ])
            merge_branches(nc, m, xT, w[:, IN2["gates"]:], [
                (ybT[0], a["w_br_attn_2"][layer], 8), (ybT[1], a["w_br_conv_2"][layer], 4), (ybT[2], a["w_br_mem_2"][layer], 4)], mergedT)
            output_product(nc, m, mergedT, DK, a["w_out_2"][layer], x, ALPHA)
        layer_norm_rows(nc, m, x, a["ln1_g_2"][layer:layer + 1, :], a["ln1_b_2"][layer:layer + 1, :])
        to_columns(nc, m, x, TT, xT)
        route(nc, m, a, xT, x, moe)
    experts(nc, m, a, layer, moe)
    combine_experts(nc, m, x, moe)
    layer_norm_rows(nc, m, x, a["ln2_g_2"][layer:layer + 1, :], a["ln2_b_2"][layer:layer + 1, :])


def final_norm(nc, m, a, x):
    with Tensors(nc) as sb:
        g = sb("final_gain", [P, D])
        rms_rows_in = sb("normed", [P, TT, D])
        rms_rows(nc, m, x, TT, rms_rows_in, NORM_EPS)
        with stage(nc, "loaded") as (block, s):
            @block.sync
            def _(sp):
                sp.dma_start(g[:, :], a["final_norm"].rearrange("(a n) -> a n", a=1).partition_broadcast(P)).then_inc(s.loaded, 16)

            @block.vector
            def _(dve):
                dve.wait_ge(s.loaded, 16)
                for t in range(TT):
                    dve.tensor_tensor(x[:, t, :], rms_rows_in[:, t, :], g[:, :], ALU.mult)




def constants():
    p = np.arange(P)[:, None]
    dist = (p + 384 - np.arange(SEQ)[None, :]).astype(np.float32)
    seen = dist >= 0
    near = np.where((dist >= 0) & (dist <= 128), dist, BIG)[:, 256:]

    ends = np.arange(32) * CMP_STRIDE + CMP_BLOCK - 1
    past = (np.arange(TT)[None, :, None] * P + p[:, :, None] - ends[None, None, :])
    cmp_ = np.where((past >= 0) & (np.arange(32) < N_CMP), past, BIG)

    rotate = np.zeros((P, P), np.float32)
    for r in range(P):
        rotate[r + 32 if r % 64 < 32 else r - 32, r] = -1.0 if r % 64 < 32 else 1.0

    def alibi(n):
        return np.exp2(-8.0 * np.arange(1, n + 1) / n).astype(np.float32)

    return {
        "ident": np.eye(P, dtype=np.float32),
        "dist_causal": np.where(seen, dist, BIG).astype(np.float32),
        "block_number": np.arange(MAX_BLOCKS, dtype=np.float32).reshape(1, MAX_BLOCKS),
        "before": np.triu(np.ones((P, P), np.float32), 1),
        "mask_causal": np.where(seen, 0.0, -BIG).astype(np.float32),
        "rotate": rotate,
        "rope_freq": np.tile(np.float32(10000.0) ** (-np.arange(0, 64, 2, dtype=np.float32) / np.float32(64)), 4)
        .astype(np.float32).reshape(P, 1),
        "dist_near": np.ascontiguousarray(near.astype(np.float32)),
        "dist_by4": np.where(seen & (dist % 4 == 0), dist, BIG).astype(np.float32),
        "dist_by16": np.where(seen & (dist % 16 == 0), dist, BIG).astype(np.float32),
        "dist_cmp": cmp_.astype(np.float32),
        "sees_any": (np.arange(P)[:, None] >= CMP_BLOCK - 1).astype(np.float32),
        "nsa_slopes": (-alibi(16) * np.float32(NSA_HD ** 0.5)).reshape(1, 16).astype(np.float32),
        "dil_slopes": (-alibi(12) * np.float32(DIL_HD ** 0.5)).reshape(1, 12).astype(np.float32),
    }


def program(nc, a, out, upto=99):
    with Tensors(nc) as sb, nc.psum_tensor("ps", [P, 8 * BANK], F32) as ps:
        m = Chip()
        m.ps, m.col = ps, {}
        m.ident = sb("ident", [P, P])
        m.columns = sb("columns", [P, 2 * P])
        m.w_slots = [sb("weights", [P, 8, 512]) for _ in range(2)]
        x = sb("x", [P, TT, D])
        with stage(nc, "loaded") as (block, s):
            @block.sync
            def _(sp):
                sp.dma_start(m.ident[:, :], a["ident"]).then_inc(s.loaded, 16)
                sp.dma_start(x[:, :, :], a["x"][0].rearrange("(t p) d -> p t d", p=P)).then_inc(s.loaded, 16)
                sp.wait_ge(s.loaded, 32)
        load_columns(nc, m, a)
        moe = bag(
            x_rows=nc.dram_tensor("expert_x_rows", (MAX_BLOCKS * P, D), F32, kind="Internal").ap(),
            y_rows=nc.dram_tensor("expert_y_rows", (MAX_BLOCKS * P, D), F32, kind="Internal").ap(),
            share=sb("share", [P, TT, 2]), slot=sb("slot", [P, 2 * TT], mybir.dt.uint32),
            block_expert=sb("block_expert", [P, MAX_BLOCKS], I32), n_pairs=sb("n_pairs", [P, 1], I32),
            cleared=nc.alloc_semaphore("rows_cleared"))
        clear_rows(nc, m, moe, sb("zero_row", [P, D]))
        if upto >= 1:
            hawk_layer(nc, m, a, x)
        if upto >= 2:
            nsa_layer(nc, m, a, x)
        if upto >= 3:
            final_norm(nc, m, a, x)
        if upto >= 4:
            m.rotate = sb("rotate", [P, P])
            cos, sin = sb("cos", [P, SEQ]), sb("sin", [P, SEQ])
            memT = sb("mem2_T", [P, DK, N_MEM])
            with stage(nc, "loaded") as (block, s):
                @block.sync
                def _(sp):
                    sp.dma_start(m.rotate[:, :], a["rotate"]).then_inc(s.loaded, 16)
                    sp.wait_ge(s.loaded, 16)
            rope_tables(nc, m, a, cos, sin)
            normed_memory(nc, m, a["mem_2"][0], None, memT)
            for layer in range(2):
                if upto >= 4 + layer:
                    second_layer(nc, m, a, x, layer, cos, sin, memT, moe)
        with stage(nc, "stored") as (block, s):
            @block.sync
            def _(sp):
                sp.dma_start(out[0].rearrange("(t p) d -> p t d", p=P), x[:, :, :]).then_inc(s.stored, 16)
                sp.wait_ge(s.stored, 16)


def kernel(**inputs):
    import concourse.bacc as bacc
    from concourse.bass_utils import run_bass_kernel_spmd

    nc = bacc.Bacc("TRN2", target_bir_lowering=False, num_devices=1)
    arrays, aps = {}, {}
    for name, value in {**inputs, **constants()}.items():
        array = np.ascontiguousarray(value)
        arrays[f"in_{name}"] = array
        aps[name] = nc.dram_tensor(f"in_{name}", array.shape, mybir.dt.from_np(array.dtype), kind="ExternalInput").ap()
    out = nc.dram_tensor("out", (1, SEQ, D), F32, kind="ExternalOutput").ap()
    program(nc, aps, out)
    result = run_bass_kernel_spmd(nc, [arrays], core_ids=[0])
    return result.results[0]["out"]
```

```python
import itertools
from collections import namedtuple
from contextlib import ExitStack, contextmanager

import concourse.bass as bass
import numpy as np
from concourse import mybir

F32 = mybir.dt.float32
F32R = mybir.dt.float32r
I32 = mybir.dt.int32
ALU = mybir.AluOpType
ACT = mybir.ActivationFunctionType
AX_X = mybir.AxisListType.X

P = 128
BANK = 512
SEQ = 512
TT = SEQ // P
D = 1024
DK = D // P
N_MEM = 256
MT = N_MEM // P
BIG = 1e30

LRU = 1024
CONV_W = 4
HAWK_COLS = dict(xa=0, za=1024, q=2048, k=3584, v=5120, zb=6656, qm=7168, zm=7424)
DIL_GROUPS, DIL_HEADS, DIL_HD = 3, 4, 128
MEM_HEADS, MEM_HD = 4, 64
HAWK_OUT = 1792
NORM_EPS = 1e-6

NSA_COLS = dict(q=0, kc=1024, vc=1152, ks=1280, vs=1408, kw=1536, vw=1664, gates=1792, z=1840, qm=2864, zm=3120)
NSA_HEADS, NSA_GROUPS, NSA_HD = 16, 2, 64
CMP_BLOCK, CMP_STRIDE = 32, 16
N_CMP = (SEQ - CMP_BLOCK) // CMP_STRIDE + 1
PHI = 256
NSA_OUT = 1280

IN2 = dict(q=0, k=1024, v=2048, cb=3072, cc=3584, cu=4096, qm=4608, gates=5120)
DA_HEADS, DA_V = 8, 128
MEM2_HEADS, MEM2_HD = 4, 128
CONV2 = 512
N_EXPERTS, N_EGROUPS, PER_GROUP, D_FF = 16, 4, 4, 512
MAX_BLOCKS = 24
LN_EPS = 1e-5
ALPHA = 4 ** 0.25


stages = itertools.count()
tensors_made = itertools.count()
places = {}
rounded_views = {}


def bag(**values):
    return namedtuple("Names", list(values))(**values)


class Chip:

    ps = ident = columns = w_slots = rotate = col = fetched = n_fetched = None


@contextmanager
def stage(nc, *names):
    sems, every, number = {}, [], next(stages)
    for name in names:
        base, _, n = name.partition("*")
        made = [nc.alloc_semaphore(f"{base}_{number}_{i}") for i in range(int(n or 1))]
        every += made
        sems[base] = made if n else made[0]
    with nc.Block() as block:
        yield block, bag(**sems)
    if every:
        nc.clear_and_free_semaphores(every)
    nc.all_engine_barrier()


@contextmanager
def Tensors(nc):
    with ExitStack() as stack:
        def make(name, shape, dtype=F32):
            t = stack.enter_context(nc.sbuf_tensor(f"{name}_{next(tensors_made)}", shape, dtype))
            places[t.name] = (nc, nc.sbuf_base - 4 * int(np.prod(shape[1:])))
            return t
        yield make


def flat(ap):
    return ap.rearrange("p a b -> p (a b)")


def one(t, index, parts=slice(0, P)):
    return t[parts, bass.ds(index, 1), :].rearrange("p a b -> p (a b)")


def pairs(eng, n, first=0):
    if n // 2 > 1:
        with eng.Fori(0, n // 2) as i:
            for u in range(2):
                yield 2 * i + u, (first + u) % 2, i
    else:
        for c in range(2 * (n // 2)):
            yield c, (first + c) % 2, c // 2
    if n % 2:
        yield n - 1, first, n // 2




def as_r(ap):
    t = ap.tensor
    if t.name not in rounded_views:
        nc, offset = places[t.name]
        rounded_views[t.name] = nc.alloc_sbuf_tensor_at(f"{t.name}_r", list(t.shape), F32R, offset=offset)
    return bass.AP(rounded_views[t.name], ap.offset, ap.ap)


def columns_pair(sb, name, k, n):
    return bag(hi=sb(f"{name}_hi", [P, k, n]), lo=sb(f"{name}_lo", [P, k, n]))


def three_passes(pe, out, left, right, start, stop):
    pe.matmul(out, as_r(left[1]), as_r(right[0]), start=start, stop=False)
    pe.matmul(out, as_r(left[0]), as_r(right[1]), start=False, stop=False)
    return pe.matmul(out, as_r(left[0]), as_r(right[0]), start=False, stop=stop)


def split(dve, hi, lo, rounded, at, done):
    dve.tensor_copy(as_r(hi), lo).then_inc(rounded, 1)
    dve.wait_ge(rounded, at)
    dve.tensor_tensor(as_r(lo), lo, as_r(hi).bitcast(F32), ALU.subtract).then_inc(done, 1)


def weight_part(m, slot):
    w = m.w_slots[slot]
    return w[:, 0:4, :], w[:, 4:8, :]


def rows_of(w, k0, ks, col, n):
    return w[k0 * P:(k0 + ks) * P, col:col + n].rearrange("(k p) n -> p k n", p=P)


def fetch_ahead(nc, m, pieces):
    with stage(nc) as (block, s):
        @block.sync
        def _(sp):
            for slot, src in enumerate(pieces):
                sp.dma_start(weight_part(m, slot)[1][:, 0:src.shape[1], 0:src.shape[2]], src).then_inc(m.fetched, 16)
    m.n_fetched += len(pieces)


def take_fetched(sp, m, loaded):
    sp.wait_ge(m.fetched, 16 * m.n_fetched)
    sp.sem_inc(loaded, 16)


def job_pieces(job):
    return [rows_of(job["w"], 4 * slot, 4, job["col"], job["width"]) for slot in range(2)]


def projection(nc, m, xT, jobs, ahead=False):
    ps = m.ps

    def tiles_of(job):
        if job["kind"] == "M":
            return len(job["parts"])
        return job["width"] // P if job["kind"] == "T" else job.get("ntok", SEQ) // P

    def walk(eng):
        first, chunk0, tiles = 0, 0, [0, 0]
        for job in jobs:
            n = job["chunks"]
            per = tiles_of(job)
            for c, half, turn in pairs(eng, n, first):
                other = tiles[1 - half] + per * (turn if half == first else turn + 1)
                yield job, c, half, chunk0 + c, tiles[half] + per * turn, other, per
            for half in range(2):
                tiles[half] += per * (n // 2 + (n % 2 if half == first else 0))
            chunk0 += n
            first = (first + n) % 2

    def products(pe, job, half, j, slot):
        x, (hi, lo) = job.get("x", xT), weight_part(m, slot)
        bank = (4 * half + j) * BANK
        kind, col, w, first_col, toks_of = job["kind"], j * P, job["width"], 0, [j]
        if kind == "M":
            kind, col, w = job["parts"][j]
            first_col, toks_of = col, range(TT)
        for n, t in enumerate(toks_of if kind == "N" else [0]):
            for k in range(4):
                row = 4 * slot + k
                if kind == "T":
                    ntok = job.get("ntok", SEQ)
                    cols = slice(col, col + P)
                    mm = three_passes(pe, ps[:, bank:bank + ntok], (hi[:, k, cols], lo[:, k, cols]),
                                      (x.hi[:, row, 0:ntok], x.lo[:, row, 0:ntok]), row == 0, row == DK - 1)
                else:
                    toks, cols = slice(t * P, (t + 1) * P), slice(first_col, first_col + w)
                    mm = three_passes(pe, ps[:, bank + n * w:bank + (n + 1) * w], (x.hi[:, row, toks], x.lo[:, row, toks]),
                                      (hi[:, k, cols], lo[:, k, cols]), row == 0 and n == 0,
                                      row == DK - 1 and n == len(toks_of) - 1)
        return mm

    with stage(nc, "weights_loaded*2", "rounded", "weights_split*2", "slot_read", "tile_ready*2",
               "tile_taken*2") as (block, s):
        @block.sync
        def _(sp):
            for step, (job, c, half, chunk, tile, other, per) in enumerate(walk(sp)):
                w = job["width"]
                for slot in range(2):
                    if ahead and step == 0:
                        take_fetched(sp, m, s.weights_loaded[slot])
                        continue
                    if slot == 0:
                        sp.wait_ge(s.slot_read, chunk + 1)
                    else:
                        sp.wait_ge(s.tile_ready[1 - half], other + 1)
                    src = job["w"][slot * 4 * P:(slot + 1) * 4 * P, bass.ds(c * w + job["col"], w)]
                    sp.dma_start(weight_part(m, slot)[1][:, :, 0:w], src.rearrange("(k p) n -> p k n", p=P)).then_inc(
                        s.weights_loaded[slot], 16)

        @block.vector
        def _(dve):
            for job, c, half, chunk, tile, other, per in walk(dve):
                w = job["width"]
                for slot in range(2):
                    dve.wait_ge(s.weights_loaded[slot], 16 * chunk + 16)
                    hi, lo = weight_part(m, slot)
                    for k in (0, 2):
                        split(dve, hi[:, k:k + 2, 0:w], lo[:, k:k + 2, 0:w], s.rounded,
                              4 * chunk + (2 * slot + k // 2 + 1), s.weights_split[slot])

        @block.tensor
        def _(pe):
            pe.sem_inc(s.slot_read, 1)
            for half in range(2):
                pe.sem_inc(s.tile_ready[half], 1)
            for job, c, half, chunk, tile, other, per in walk(pe):
                pe.wait_ge(s.tile_taken[half], tile + 1)
                pe.wait_ge(s.weights_split[0], 2 * chunk + 2)
                for j in range(per):
                    mm = products(pe, job, half, j, 0)
                mm.then_inc(s.slot_read, 1)
                pe.wait_ge(s.weights_split[1], 2 * chunk + 2)
                for j in range(per):
                    products(pe, job, half, j, 1).then_inc(s.tile_ready[half], 1)

        @block.scalar
        def _(act):
            for half in range(2):
                act.sem_inc(s.tile_taken[half], 1)
            for job, c, half, chunk, tile, other, per in walk(act):
                n = BANK if job["kind"] == "M" else job.get("ntok", SEQ) if job["kind"] == "T" else job["width"]
                for j in range(per):
                    act.wait_ge(s.tile_ready[half], tile + (j + 2))
                    bank = ps[:, (4 * half + j) * BANK:(4 * half + j) * BANK + n]
                    job["take"](act, bank, c, j).then_inc(s.tile_taken[half], 1)


def take_T(dst, func=ACT.Copy, first=0, per=4):
    return lambda act, bank, c, j: act.activation(one(dst, per * c + (first + j)), bank, func)


def take_N(dst, func=ACT.Copy, width=512):
    return lambda act, bank, c, j: act.activation(
        dst[:, j, bass.ds(c * width, width)], bank, func)


def memory_kv(memT, w_kv, n_cols, KT, V):
    return [
        dict(w=w_kv, col=0, chunks=1, width=n_cols, kind="T", take=take_T(KT), x=memT, ntok=N_MEM),
        dict(w=w_kv, col=n_cols, chunks=1, width=n_cols, kind="N", take=take_N(V, width=n_cols), x=memT, ntok=N_MEM),
    ]




def to_columns(nc, m, src, tiles, dst, gain=None, pair=None):
    n = src.shape[2] // P
    width = tiles * P
    with stage(nc, "turned", "taken", "split") as (block, s):

        @block.tensor
        def _(pe):
            for k in range(n):
                if k >= 8:
                    pe.wait_ge(s.split if pair else s.taken, k - 7)
                for t in range(tiles):
                    mm = pe.transpose(m.ps[:, (k % 8) * BANK + t * P:(k % 8) * BANK + (t + 1) * P],
                                      src[:, t, k * P:(k + 1) * P], m.ident[:, :])
                mm.then_inc(s.turned, 1)

        @block.scalar
        def _(act):
            for k in range(n):
                act.wait_ge(s.turned, k + 1)
                bank = m.ps[:, (k % 8) * BANK:(k % 8) * BANK + width]
                to = as_r(pair.hi[:, k, 0:width]) if pair else dst[k][:, 0:width]
                scale = 1.0 if gain is None else gain[:, k:k + 1]
                act.activation(to, bank, ACT.Copy, scale=scale).then_inc(s.taken, 1)

        if pair:
            @block.vector
            def _(dve):
                for k in range(n):
                    dve.wait_ge(s.taken, k + 1)
                    bank = m.ps[:, (k % 8) * BANK:(k % 8) * BANK + width]
                    dve.scalar_tensor_tensor(out=as_r(pair.lo[:, k, 0:width]), in0=bank,
                                             scalar=1.0 if gain is None else gain[:, k:k + 1],
                                             in1=as_r(pair.hi[:, k, 0:width]).bitcast(F32), op0=ALU.mult, op1=ALU.subtract).then_inc(s.split, 1)


def refine_rsqrt(dve, done, at, var, inv, spare):
    dve.tensor_tensor(spare, inv, inv, ALU.mult).then_inc(done, 1)
    dve.wait_ge(done, at + 1)
    dve.scalar_tensor_tensor(out=spare, in0=spare, scalar=-0.5, in1=var, op0=ALU.mult, op1=ALU.mult).then_inc(done, 1)
    dve.wait_ge(done, at + 2)
    dve.scalar_tensor_tensor(out=inv, in0=spare, scalar=1.5, in1=inv, op0=ALU.add, op1=ALU.mult).then_inc(done, 1)
    dve.wait_ge(done, at + 3)


def rms_rows(nc, m, src, tiles, dst, eps):
    with Tensors(nc) as sb, stage(nc, "summed", "shifted", "rooted", "inverted") as (block, s):
        sums = sb("sums", [P, 4])
        var = sb("var", [P, 4])
        root = sb("root", [P, 4])
        inv = sb("inv", [P, 4])

        @block.scalar
        def _(act):
            for t in range(tiles):
                act.activation(dst[:, t, :], src[:, t, :], ACT.Square, accum_out=sums[:, t:t + 1]).then_inc(s.summed, 1)
            act.wait_ge(s.shifted, 1)
            act.activation(root[:, 0:tiles], var[:, 0:tiles], ACT.Sqrt).then_inc(s.rooted, 1)

        @block.vector
        def _(dve):
            dve.wait_ge(s.summed, tiles)
            dve.tensor_scalar(var[:, 0:tiles], sums[:, 0:tiles], 1.0 / D, eps, ALU.mult, ALU.add).then_inc(s.shifted, 1)
            dve.wait_ge(s.rooted, 1)
            dve.reciprocal(inv[:, 0:tiles], root[:, 0:tiles]).then_inc(s.inverted, 1)
            dve.wait_ge(s.inverted, 1)
            refine_rsqrt(dve, s.inverted, 1, var[:, 0:tiles], inv[:, 0:tiles], root[:, 0:tiles])
            for t in range(tiles):
                dve.tensor_scalar(dst[:, t, :], src[:, t, :], inv[:, t:t + 1], None, ALU.mult)


def layer_norm_rows(nc, m, x, gain, shift):
    with Tensors(nc) as sb, stage(nc, "row_loaded", "totalled", "averaged", "centred", "squared", "shifted",
                                  "rooted", "inverted") as (block, s):
        g = sb("g", [P, D])
        b = sb("b", [P, D])
        scratch = sb("scratch", [P, TT, D])
        sums = sb("sums", [P, 4])
        squared = sb("squared", [P, TT, D])
        mean = sb("mean", [P, 4])
        minus_mean = sb("minus_mean", [P, 4])
        squares = sb("squares", [P, 4])
        var = sb("var", [P, 4])
        root = sb("root", [P, 4])
        inv = sb("inv", [P, 4])

        @block.sync
        def _(sp):
            sp.dma_start(g[:, :], gain.partition_broadcast(P)).then_inc(s.row_loaded, 16)
            sp.dma_start(b[:, :], shift.partition_broadcast(P)).then_inc(s.row_loaded, 16)

        @block.scalar
        def _(act):
            for t in range(TT):
                act.activation(scratch[:, t, :], x[:, t, :], ACT.Copy, accum_out=sums[:, t:t + 1]).then_inc(s.totalled, 1)
            for t in range(TT):
                act.wait_ge(s.averaged, 2)
                act.activation(squared[:, t, :], x[:, t, :], ACT.Square, bias=minus_mean[:, t:t + 1],
                               accum_out=squares[:, t:t + 1]).then_inc(s.squared, 1)
            act.wait_ge(s.shifted, 1)
            act.activation(root[:, :], var[:, :], ACT.Sqrt).then_inc(s.rooted, 1)

        @block.vector
        def _(dve):
            dve.wait_ge(s.totalled, TT)
            dve.tensor_scalar(mean[:, :], sums[:, :], 1.0 / D, None, ALU.mult).then_inc(s.averaged, 1)
            dve.tensor_scalar(minus_mean[:, :], sums[:, :], -1.0 / D, None, ALU.mult).then_inc(s.averaged, 1)
            dve.wait_ge(s.averaged, 2)
            dve.wait_ge(s.row_loaded, 32)
            for t in range(TT):
                dve.scalar_tensor_tensor(out=scratch[:, t, :], in0=x[:, t, :], scalar=mean[:, t:t + 1], in1=g[:, :],
                                         op0=ALU.subtract, op1=ALU.mult).then_inc(s.centred, 1)
            dve.wait_ge(s.squared, TT)
            dve.tensor_scalar(var[:, :], squares[:, :], 1.0 / D, LN_EPS, ALU.mult, ALU.add).then_inc(s.shifted, 1)
            dve.wait_ge(s.rooted, 1)
            dve.reciprocal(inv[:, :], root[:, :]).then_inc(s.inverted, 1)
            dve.wait_ge(s.inverted, 1)
            refine_rsqrt(dve, s.inverted, 1, var[:, :], inv[:, :], root[:, :])
            dve.wait_ge(s.centred, TT)
            for t in range(TT):
                dve.scalar_tensor_tensor(out=x[:, t, :], in0=scratch[:, t, :], scalar=inv[:, t:t + 1], in1=b[:, :],
                                         op0=ALU.mult, op1=ALU.add)


def pieces_of(ktiles):
    n = (ktiles + 3) // 4
    cuts = [ktiles * i // n for i in range(n + 1)]
    return [(a, b - a) for a, b in zip(cuts, cuts[1:])]


def output_pieces(w):
    return [rows_of(w, k0, ks, 0, 512) for k0, ks in pieces_of(w.shape[0] // P)[:2]]


def output_product(nc, m, yT, w, x, rescale=1.0, ahead=False):
    K = len(yT)
    steps = [(n, k0, ks) for n in range(2) for k0, ks in pieces_of(K)]
    per_half = len(steps) // 2
    with Tensors(nc) as sb, stage(nc, "weights_loaded*2", "rounded", "y_split", "weights_split", "read") as (block, s):
        hi = sb("y_hi", [P, K, SEQ])

        @block.sync
        def _(sp):
            for q, (n, k0, ks) in enumerate(steps):
                if ahead and q < 2:
                    take_fetched(sp, m, s.weights_loaded[q])
                    continue
                if q >= 2:
                    sp.wait_ge(s.read, TT * (q - 1))
                src = rows_of(w, k0, ks, n * 512, 512)
                sp.dma_start(weight_part(m, q % 2)[1][:, 0:ks, :], src).then_inc(s.weights_loaded[q % 2], 16)

        @block.tensor
        def _(pe):
            for q, (n, k0, ks) in enumerate(steps):
                w_hi, w_lo = weight_part(m, q % 2)
                pe.wait_ge(s.y_split, k0 + ks)
                pe.wait_ge(s.weights_split, q + 1)
                for t in range(TT):
                    toks = slice(t * P, (t + 1) * P)
                    bank = 4 * n + t
                    for k in range(ks):
                        mm = three_passes(pe, m.ps[:, bank * BANK:(bank + 1) * BANK],
                                          (hi[:, k0 + k, toks], yT[k0 + k][:, toks]), (w_hi[:, k, :], w_lo[:, k, :]),
                                          k0 + k == 0, k0 + k == K - 1)
                    mm.then_inc(s.read, 1)

        @block.vector
        def _(dve):
            done = 0

            def add(n):
                for t in range(TT):
                    dve.wait_ge(s.read, TT * ((n + 1) * per_half - 1) + t + 1)
                    cols = x[:, t, n * 512:(n + 1) * 512]
                    bank = 4 * n + t
                    dve.scalar_tensor_tensor(out=cols, in0=cols, scalar=rescale,
                                             in1=m.ps[:, bank * BANK:(bank + 1) * BANK], op0=ALU.mult, op1=ALU.add)

            for q, (n, k0, ks) in enumerate(steps):
                if n == 0:
                    for k in range(k0, k0 + ks):
                        done += 1
                        split(dve, hi[:, k, :], yT[k], s.rounded, done, s.y_split)
                w_hi, w_lo = weight_part(m, q % 2)
                dve.wait_ge(s.weights_loaded[q % 2], 16 * (q // 2) + 16)
                done += 1
                split(dve, w_hi[:, 0:ks, :], w_lo[:, 0:ks, :], s.rounded, done, s.weights_split)
                if q == per_half:
                    add(0)
            add(1)


def gate_rows(nc, pairs_):
    with stage(nc) as (block, s):

        @block.vector
        def _(dve):
            for y, gate in pairs_:
                dve.tensor_tensor(y, y, gate, ALU.mult)




def attention(nc, m, n_iter, copies, items, width, n_score_banks, n_turn, clear=(), zeros=None, ahead=1):
    n = len(items)
    ps = m.ps
    R = 2 * ahead
    n_out = 8 - R * n_score_banks - n_turn
    turn_bank0 = R * n_score_banks
    out_bank0 = turn_bank0 + n_turn
    chunks = []
    for it in items:
        v = it["values"]
        chunks.append([v[a:a + 4] for a in range(0, len(v), 4)])
    chunk_base = np.cumsum([0] + [len(c) for c in chunks]).tolist()
    n_chunks = chunk_base[-1]
    n_segs = [len(it["segs"]) for it in items]
    seg_base = np.cumsum([0] + n_segs).tolist()
    n_seg = seg_base[-1]
    chunks_of = [(k, c) for k in range(n) for c in range(len(chunks[k]))]

    def score_ap(k, seg):
        c = ((k % R) * n_score_banks + seg[2]) * BANK
        return ps[:, c:c + seg[3]]

    coef_base = np.cumsum([0] + [it.get("coef") is not None for it in items]).tolist()
    n_coef = coef_base[-1]
    assert n % 4 == 0 and n_chunks % n_turn == 0 and n % n_out == 0

    with Tensors(nc) as sb, stage(nc, "staged", "cleared", "scores_ready", "biased", "top_found", "top_scaled", "exp_done",
                                  "turned", "keys_ready", "out_ready", "out_taken", "inverted",
                                  "weighted") as (block, s):
        sc, pr = (flat(w[:, :, :])[:, 0:R * width].rearrange("p (a b) -> p a b", a=R) for w in m.w_slots)
        by_key = max(len(c) for c in chunks) * 4 * P
        if R * width + 2 * by_key <= flat(m.w_slots[0][:, :, :]).shape[1]:
            prT = flat(m.w_slots[0][:, :, :])[:, R * width:R * width + 2 * by_key].rearrange("p (a b) -> p a b", a=2)
        else:
            prT = sb("probs_by_key", [P, 2, by_key])
        top = sb("top", [P, R])
        ntop = sb("ntop", [P, R])
        total = sb("total", [P, 4])
        inv = sb("inv", [P, 2])
        wt = sb("wt", [P, 2])


        if clear:
            @block.sync
            def _(sp):
                for rows in clear:
                    sp.dma_start(rows.rearrange("(b p) d -> p b d", p=P),
                                 zeros[:, :].unsqueeze(1).broadcast_to([P, MAX_BLOCKS, D])).then_inc(s.cleared, 16)
                sp.wait_ge(s.cleared, 16 * len(clear))

        if copies:
            @block.gpsimd
            def _(pool):
                with pool.Fori(0, n_iter) as i:
                    pool.wait_ge(s.scores_ready, i * n + 1)
                    for dst, src in copies:
                        pool.tensor_copy(dst, src(i)).then_inc(s.staged, 1)

        @block.tensor
        def _(pe):
            pe.sem_inc(s.out_ready, 2)
            pe.sem_inc(s.scores_ready, 1)

            def scores(i, k):
                if items[k].get("needs"):
                    pe.wait_ge(s.staged, i * len(copies) + items[k]["needs"])
                pe.wait_ge(s.top_found, i * n + (k + 1))
                for seg in items[k]["segs"]:
                    mm = pe.matmul(score_ap(k, seg), seg[0], seg[1](i), start=True, stop=True)
                mm.then_inc(s.scores_ready, 1)

            def turn(i, k, c):
                if c == 0:
                    pe.wait_ge(s.exp_done, i * n + (k + 1 + R))
                q = chunk_base[k] + c
                pe.wait_ge(s.keys_ready, i * n_chunks + (q + 1))
                bank = (turn_bank0 + q % n_turn) * BANK
                for j, (col, rows, _) in enumerate(chunks[k][c]):
                    mm = pe.transpose(ps[0:rows, bank + j * P:bank + (j + 1) * P],
                                      pr[:, k % R, col:col + rows], m.ident[:, :])
                mm.then_inc(s.turned, 1)

            def product(i, k, c):
                if c == 0:
                    pe.wait_ge(s.out_taken, i * n + (k + 1))
                hd = items[k]["hd"]
                out = ps[:, (out_bank0 + k % n_out) * BANK:(out_bank0 + k % n_out) * BANK + hd]
                last = len(items[k]["values"]) - 1
                pe.wait_ge(s.keys_ready, i * n_chunks + (chunk_base[k] + c + 1 + n_turn))
                for t, (col, rows, v) in enumerate(chunks[k][c], 4 * c):
                    mm = pe.matmul(out, prT[0:rows, k % 2, t * P:(t + 1) * P], v(i), start=t == 0, stop=t == last)
                if t == last:
                    mm.then_inc(s.out_ready, 1)

            with pe.Fori(0, n_iter) as i:
                for k in range(ahead):
                    scores(i, k)
                for k in range(n + 1):
                    if k + ahead < n:
                        scores(i, k + ahead)
                    turning = len(chunks[k]) if k < n else 0
                    multiplying = len(chunks[k - 1]) if k else 0
                    for c in range(max(turning, multiplying)):
                        if c < turning:
                            turn(i, k, c)
                        if c < multiplying:
                            product(i, k - 1, c)

        @block.vector
        def _(dve):
            dve.sem_inc(s.top_found, R)
            dve.sem_inc(s.out_taken, n_out)

            def bias(i, k):
                dve.wait_ge(s.scores_ready, i * n + (k + 2))
                dve.wait_ge(s.exp_done, i * n + (k + 1))
                at = 0
                for seg in items[k]["segs"]:
                    dst = sc[:, k % R, at:at + seg[3]]
                    if seg[4] is None:
                        ins = dve.tensor_copy(dst, score_ap(k, seg))
                    elif seg[5] is None:
                        ins = dve.tensor_tensor(dst, score_ap(k, seg), seg[4], ALU.add)
                    else:
                        ins = dve.scalar_tensor_tensor(out=dst, in0=seg[4], scalar=seg[5](i), in1=score_ap(k, seg),
                                                       op0=ALU.mult, op1=ALU.add)
                    ins.then_inc(s.biased, 1)
                    at += seg[3]
                dve.wait_ge(s.biased, i * n_seg + seg_base[k + 1])
                dve.reduce_max(top[:, k % R:k % R + 1], sc[:, k % R, 0:at], AX_X).then_inc(s.top_found, 1)
                dve.wait_ge(s.top_found, i * n + (k + 1 + R))
                dve.tensor_scalar(ntop[:, k % R:k % R + 1], top[:, k % R:k % R + 1], -items[k]["scale"], None,
                                  ALU.mult).then_inc(s.top_scaled, 1)

            def finish(i, k):
                it = items[k]
                hd = it["hd"]
                b = (out_bank0 + k % n_out) * BANK
                dve.wait_ge(s.exp_done, i * n + (k + 1 + R))
                dve.reciprocal(inv[:, k % 2:k % 2 + 1], total[:, k % 4:k % 4 + 1]).then_inc(s.inverted, 1)
                factor = inv
                dve.wait_ge(s.inverted, i * n + (k + 1))
                if it.get("coef") is not None:
                    dve.tensor_tensor(wt[:, k % 2:k % 2 + 1], inv[:, k % 2:k % 2 + 1], it["coef"](i),
                                      ALU.mult).then_inc(s.weighted, 1)
                    dve.wait_ge(s.weighted, i * n_coef + coef_base[k + 1])
                    factor = wt
                dve.wait_ge(s.out_ready, i * n + (k + 3))
                dst = it["dst"](i)
                f = factor[:, k % 2:k % 2 + 1]
                if it.get("add"):
                    dve.wait_ge(s.out_taken, i * n + (k + n_out))
                    ins = dve.scalar_tensor_tensor(out=dst, in0=ps[:, b:b + hd], scalar=f, in1=dst, op0=ALU.mult, op1=ALU.add)
                else:
                    ins = dve.tensor_scalar(dst, ps[:, b:b + hd], f, None, ALU.mult)
                ins.then_inc(s.out_taken, 1)

            with dve.Fori(0, n_iter) as i:
                for k in range(ahead):
                    bias(i, k)
                for k in range(n):
                    if k + ahead < n:
                        bias(i, k + ahead)
                    if k:
                        finish(i, k - 1)
                finish(i, n - 1)

        @block.scalar
        def _(act):
            act.sem_inc(s.exp_done, R)
            act.sem_inc(s.keys_ready, n_turn)

            def exponent(i, k):
                it = items[k]
                w = sum(seg[3] for seg in it["segs"])
                act.wait_ge(s.top_scaled, i * n + (k + 1))
                act.activation(pr[:, k % R, 0:w], sc[:, k % R, 0:w], ACT.Exp, bias=ntop[:, k % R:k % R + 1],
                               scale=it["scale"], accum_out=total[:, k % 4:k % 4 + 1]).then_inc(s.exp_done, 1)

            def take(i, k):
                act.wait_ge(s.out_ready, i * n + (k + 1))
                for c, chunk in enumerate(chunks[k]):
                    q = chunk_base[k] + c
                    act.wait_ge(s.turned, i * n_chunks + (q + 1))
                    rows = chunk[0][1]
                    bank = (turn_bank0 + q % n_turn) * BANK
                    act.activation(prT[0:rows, k % 2, 4 * c * P:(4 * c + len(chunk)) * P],
                                   ps[0:rows, bank:bank + len(chunk) * P], ACT.Copy).then_inc(s.keys_ready, 1)

            with act.Fori(0, n_iter) as i:
                for k in range(ahead):
                    exponent(i, k)
                for k in range(n):
                    if k + ahead < n:
                        exponent(i, k + ahead)
                    take(i, k)


def seg(lhsT, rhs, cols, bank=0, table=None, slope=None):
    return (lhsT, rhs, bank, cols, table, slope)


def turns(per, item_list, needs):
    every = []
    for u in range(per):
        def at(fn, u=u):
            return fn and (lambda i: fn(per * i + u))

        for n, it in enumerate(item_list(u)):
            it = dict(it, segs=[(lhsT, at(rhs), bank, cols, table, at(slope)) for lhsT, rhs, bank, cols, table, slope in it["segs"]],
                      values=[(col, rows, at(v)) for col, rows, v in it["values"]], coef=at(it.get("coef")), dst=at(it["dst"]))
            if n == 0:
                it["needs"] = (u + 1) * needs
            every.append(it)
    return every


def staging(m, n):
    every = flat(m.w_slots[1][:, :, :])
    end = every.shape[1]
    return [every[:, end - (k + 1) * SEQ:end - k * SEQ] for k in range(n)]


def memory_attention(nc, m, heads, hd, qT, kT, v, y, y_col):
    per = P // hd
    stage_to = staging(m, 4)

    def tile_items(u):
        q_here, k_here = stage_to[2 * u], stage_to[2 * u + 1]
        items = []
        for h in range(per):
            rows = slice(h * hd, (h + 1) * hd)
            for t in range(TT):
                items.append(dict(
                    segs=[seg(q_here[rows, t * P:(t + 1) * P], lambda i, rows=rows: k_here[rows, 0:N_MEM], N_MEM)],
                    scale=hd ** -0.5,
                    values=[(j * P, P, lambda i, j=j, h=h: v[:, j, bass.ds(i * P + h * hd, hd)]) for j in range(MT)],
                    hd=hd, dst=lambda i, t=t, h=h: y[:, t, bass.ds(i * P + (y_col + h * hd), hd)]))
        return items

    copies = []
    for u in range(2):
        copies += [(stage_to[2 * u], lambda i, u=u: one(qT, 2 * i + u)),
                   (stage_to[2 * u + 1][:, 0:N_MEM], lambda i, u=u: one(kT, 2 * i + u))]
    attention(nc, m, heads // per // 2, copies, turns(2, tile_items, 2), N_MEM, 1, 2)




def lru(nc, m, a, xa, yT):
    K = LRU // P
    with Tensors(nc) as sb, stage(nc, "zeroed", "blocks_loaded", "padded", "conv", "gates_ready",
                                  "rate", "soft", "s_ready", "root_ready", "step", "banks") as (block, s):
        cw = m.col["hawk_conv_w"].rearrange("p (j k) -> p j k", k=K)
        cb, gab, gxb, lam = (m.col[f"hawk_{n}"] for n in ("conv_b", "gate_a_b", "gate_x_b", "lambda"))
        sp_ = sb("softplus", [P, 6, K])
        blocks = [sb("blocks_a", [P, K, P]), sb("blocks_x", [P, K, P])]
        xc = sb("xc", [P, K, SEQ])
        gi = sb("gi", [P, K, SEQ])
        r1 = sb("r1", [P, K, SEQ])

        @block.sync
        def _(sp):
            sp.wait_ge(s.zeroed, 2)
            for blk, name in zip(blocks, ("hawk_gate_a_w", "hawk_gate_x_w")):
                for b in range(2):
                    sp.dma_start(blk[64 * b:64 * b + 64, :, 64 * b:64 * b + 64],
                                 a[name][0].rearrange("(k b) i j -> b i k j", b=2)[b]).then_inc(s.blocks_loaded, 16)

        @block.gpsimd
        def _(pool):
            for blk in blocks:
                pool.memset(blk[:, :, :], 0.0).then_inc(s.zeroed, 1)

        @block.tensor
        def _(pe):
            pe.wait_ge(s.blocks_loaded, 64)
            pe.wait_ge(s.conv, K * CONV_W)
            for c in range(K):
                for g in range(2):
                    n = 2 * c + g
                    if n >= 8:
                        pe.wait_ge(s.banks, n - 7)
                    pe.matmul(m.ps[:, (n % 8) * BANK:(n % 8 + 1) * BANK], blocks[g][:, c, :], xc[:, c, :],
                              start=True, stop=True).then_inc(s.gates_ready, 1)

        @block.scalar
        def _(act):
            act.activation(sp_[:, 0, :], lam[:, :], ACT.Abs).then_inc(s.soft, 1)
            act.wait_ge(s.soft, 1)
            act.activation(sp_[:, 1, :], sp_[:, 0, :], ACT.Exp, scale=-1.0).then_inc(s.soft, 1)
            act.wait_ge(s.soft, 2)
            act.activation(sp_[:, 2, :], sp_[:, 1, :], ACT.Ln, bias=1.0).then_inc(s.soft, 1)
            act.activation(sp_[:, 3, :], lam[:, :], ACT.Relu, scale=-1.0).then_inc(s.soft, 1)
            for c in range(K):
                for g, (dst, bias) in enumerate(((r1, gab), (gi, gxb))):
                    n = 2 * c + g
                    act.wait_ge(s.gates_ready, n + 1)
                    act.activation(dst[:, c, :], m.ps[:, (n % 8) * BANK:(n % 8 + 1) * BANK], ACT.Sigmoid,
                                   bias=bias[:, c:c + 1]).then_inc(s.banks, 1)
            act.wait_ge(s.rate, 1)
            act.wait_ge(s.banks, 2 * K)
            for c in range(K):
                act.activation(r1[:, c, :], r1[:, c, :], ACT.Tanh, scale=sp_[:, 5, c:c + 1]).then_inc(s.s_ready, 1)
            act.wait_ge(s.s_ready, K)
            act.wait_ge(s.step, 2)
            act.activation(xa[:, :, 0:SEQ], r1[:, :, :], ACT.Sqrt).then_inc(s.root_ready, 1)

        @block.vector
        def _(dve):
            dve.memset(xa[:, :, 0:3], 0.0).then_inc(s.padded, 1)
            dve.wait_ge(s.padded, 1)
            for j in range(CONV_W):
                if j:
                    dve.wait_ge(s.conv, K * j)
                for c in range(K):
                    x = xa[:, c, j:j + SEQ]
                    if j == 0:
                        ins = dve.tensor_scalar(xc[:, c, :], x, cw[:, 0, c:c + 1], cb[:, c:c + 1], ALU.mult, ALU.add)
                    else:
                        ins = dve.scalar_tensor_tensor(out=xc[:, c, :], in0=x, scalar=cw[:, j, c:c + 1], in1=xc[:, c, :],
                                                       op0=ALU.mult, op1=ALU.add)
                    ins.then_inc(s.conv, 1)
            dve.wait_ge(s.soft, 4)
            dve.tensor_tensor(sp_[:, 4, :], sp_[:, 2, :], sp_[:, 3, :], ALU.add).then_inc(s.padded, 1)
            dve.wait_ge(s.padded, 2)
            dve.tensor_scalar(sp_[:, 5, :], sp_[:, 4, :], 4.0, None, ALU.mult).then_inc(s.rate, 1)
            dve.wait_ge(s.banks, 2 * K)
            dve.wait_ge(s.conv, K * CONV_W)
            dve.tensor_tensor(flat(gi[:, :, :]), flat(gi[:, :, :]), flat(xc[:, :, :]), ALU.mult).then_inc(s.step, 1)
            dve.wait_ge(s.step, 1)
            dve.wait_ge(s.s_ready, K)
            dve.tensor_scalar(flat(xc[:, :, :]), flat(r1[:, :, :]), 1.0, None, ALU.add).then_inc(s.step, 1)
            dve.wait_ge(s.step, 2)
            dve.reciprocal(flat(xc[:, :, :]), flat(xc[:, :, :])).then_inc(s.step, 1)
            dve.wait_ge(s.step, 3)
            dve.wait_ge(s.root_ready, 1)
            dve.scalar_tensor_tensor(out=xa[:, :, 0:SEQ], in0=xa[:, :, 0:SEQ], scalar=2.0, in1=xc[:, :, :],
                                     op0=ALU.mult, op1=ALU.mult).then_inc(s.step, 1)
            dve.wait_ge(s.step, 4)
            dve.memset(xa[:, :, 0:1], 1.0).then_inc(s.step, 1)
            dve.wait_ge(s.step, 5)
            dve.tensor_tensor(gi[:, :, :], gi[:, :, :], xa[:, :, 0:SEQ], ALU.mult).then_inc(s.step, 1)
            dve.tensor_scalar(flat(r1[:, :, :]), flat(r1[:, :, :]), -1.0, 1.0, ALU.mult, ALU.add).then_inc(s.step, 1)
            dve.wait_ge(s.step, 7)
            dve.tensor_tensor(flat(r1[:, :, :]), flat(r1[:, :, :]), flat(xc[:, :, :]), ALU.mult).then_inc(s.step, 1)
            dve.wait_ge(s.step, 8)
            for c in range(K):
                dve.tensor_tensor_scan(xc[:, c, :], r1[:, c, :], gi[:, c, :], 0.0, ALU.mult, ALU.add).then_inc(s.step, 1)
            for c in range(K):
                dve.wait_ge(s.step, 9 + c)
                dve.tensor_tensor(yT[:, c, :], yT[:, c, :], xc[:, c, :], ALU.mult)


def hawk_layer(nc, m, a, x):
    with Tensors(nc) as sb:
        xT = columns_pair(sb, "hawk_xT", DK, SEQ)
        lruT = sb("lru_T", [P, DK, SEQ])
        w = a["hawk_w_in"][0]

        def job(name, chunks, width, kind, take, skip=0):
            return dict(w=w, col=HAWK_COLS[name] + skip, chunks=chunks, width=width, kind=kind, take=take)

        fetch_ahead(nc, m, job_pieces(job("xa", 2, 512, "T", None)))
        with Tensors(nc) as sb1:
            rows = sb1("rows", [P, TT, D])
            rms_rows(nc, m, x, TT, rows, NORM_EPS)
            to_columns(nc, m, rows, TT, None, m.col["hawk_norm"], xT)
        with Tensors(nc) as sb1:
            xa = sb1("xa", [P, DK, 3 + SEQ])
            projection(nc, m, xT, [
                job("xa", 2, 512, "T", lambda act, bank, c, j: act.activation(
                    xa[:, bass.ds(4 * c + j, 1), 3:3 + SEQ].rearrange("p a b -> p (a b)"), bank, ACT.Copy)),
                job("za", 2, 512, "T", take_T(lruT, ACT.Silu)),
            ], ahead=True)
            fetch_ahead(nc, m, job_pieces(job("q", 3, 512, "T", None)))
            lru(nc, m, a, xa, lruT)
        n_rows = DIL_HEADS * DIL_HD + MEM_HEADS * MEM_HD
        with Tensors(nc) as sb1:
            y = sb1("y_rows", [P, TT, n_rows])
            with Tensors(nc) as sb2:
                qT = sb2("qT", [P, 12, SEQ])
                kT = sb2("kT", [P, 12, SEQ])
                v = sb2("v", [P, TT, 1536])
                projection(nc, m, xT, [
                    job("q", 3, 512, "T", take_T(qT)),
                    job("k", 3, 512, "T", take_T(kT)),
                    job("v", 3, 512, "N", take_N(v)),
                ], ahead=True)
                dilated(nc, m, a, qT, kT, v, y)
            with Tensors(nc) as sb2:
                gate = sb2("gate_rows", [P, TT, n_rows])
                qmT = sb2("qmT", [P, 2, SEQ])
                kmT = sb2("kmT", [P, 2, N_MEM])
                vm = sb2("vm", [P, MT, MEM_HEADS * MEM_HD])
                memT = columns_pair(sb2, "memT", DK, N_MEM)
                fetch_ahead(nc, m, job_pieces(job("zb", 1, 512, "N", None)))
                normed_memory(nc, m, a["mem"][0], m.col["hawk_mem_norm"], memT)
                projection(nc, m, xT, [
                    job("zb", 1, 512, "N", take_N(gate, ACT.Silu)),
                    job("qm", 1, 256, "T", take_T(qmT, per=2)),
                    job("zm", 1, 256, "N", lambda act, bank, c, j: act.activation(gate[:, j, 512:768], bank, ACT.Silu)),
                ] + memory_kv(memT, a["hawk_w_mem_kv"][0], 256, kmT, vm), ahead=True)
                memory_attention(nc, m, MEM_HEADS, MEM_HD, qmT, kmT, vm, y, 512)
                fetch_ahead(nc, m, output_pieces(a["hawk_w_out"][0]))
                gate_rows(nc, [(flat(y[:, :, :]), flat(gate[:, :, :]))])
            restT = sb1("rest_T", [P, n_rows // P, SEQ])
            to_columns(nc, m, y, TT, [restT[:, k, :] for k in range(n_rows // P)])
            yT = [lruT[:, k, :] for k in range(DK)] + [restT[:, k, :] for k in range(n_rows // P)]
            output_product(nc, m, yT, a["hawk_w_out"][0], x, ahead=True)


COLUMN_VECTORS = [
    ("hawk_norm", DK), ("hawk_conv_w", CONV_W * DK), ("hawk_conv_b", DK), ("hawk_gate_a_b", DK), ("hawk_gate_x_b", DK),
    ("hawk_lambda", DK), ("hawk_mem_norm", DK), ("nsa_norm", DK), ("nsa_mem_norm", DK), ("conv_w_2", 24),
    ("nsa_pe_k", 16), ("nsa_pe_v", 16), ("diff_subln_g_2", 2),
]


def load_columns(nc, m, a):
    with Tensors(nc) as sb, stage(nc, "zeroed", "loaded", "turned") as (block, s):
        rows = sb("vector_rows", [P, 2, P])
        places, at = [], 0
        for name, n in COLUMN_VECTORS:
            if at // P != (at + n - 1) // P:
                at = P * (at // P + 1)
            places.append((name, n, at))
            m.col[name] = m.columns[:, at:at + n]
            at += n

        @block.vector
        def _(dve):
            dve.memset(rows[:, :, :], 0.0).then_inc(s.zeroed, 1)
            dve.wait_ge(s.turned, 2)
            dve.tensor_copy(m.columns[:, :], m.ps[:, 0:2 * P])

        @block.sync
        def _(sp):
            sp.wait_ge(s.zeroed, 1)
            for name, n, at in places:
                v = a[name]
                axes = " ".join(f"a{i}" for i in range(len(v.shape)))
                v = v.rearrange(f"{axes} -> ({axes})").rearrange("(k p) -> k p", p=P)
                sp.dma_start(rows[at % P:at % P + n, at // P, :], v).then_inc(s.loaded, 16)

        @block.tensor
        def _(pe):
            pe.wait_ge(s.loaded, 16 * len(places))
            for g in range(2):
                pe.transpose(m.ps[:, g * P:(g + 1) * P], rows[:, g, :], m.ident[:, :]).then_inc(s.turned, 1)


def normed_memory(nc, m, mem, gain, memT):
    with Tensors(nc) as sb:
        rows = sb("mem_rows", [P, MT, D])
        with stage(nc, "loaded") as (block, s):
            @block.sync
            def _(sp):
                sp.dma_start(rows[:, :, :], mem.rearrange("(t p) d -> p t d", p=P)).then_inc(s.loaded, 16)
                sp.wait_ge(s.loaded, 16)
        if gain is not None:
            normed = sb("mem_normed", [P, MT, D])
            rms_rows(nc, m, rows, MT, normed, NORM_EPS)
            to_columns(nc, m, normed, MT, None, gain, memT)
        else:
            to_columns(nc, m, rows, MT, None, None, memT)


def dilated(nc, m, a, qT, kT, v, y):
    with Tensors(nc) as sb:
        stage_to = staging(m, DIL_GROUPS) + [sb("q_here", [P, SEQ])[:, :] for _ in range(DIL_GROUPS)]
        tab = [sb("near", [P, 256]), sb("by4", [P, SEQ]), sb("by16", [P, SEQ])]
        slopes = sb("slopes", [P, DIL_GROUPS * DIL_HEADS])
        with stage(nc, "loaded") as (block, s):
            @block.sync
            def _(sp):
                for t, name in zip(tab, ("dist_near", "dist_by4", "dist_by16")):
                    sp.dma_start(t[:, :], a[name]).then_inc(s.loaded, 16)
                sp.dma_start(slopes[:, :], a["dil_slopes"].partition_broadcast(P)).then_inc(s.loaded, 16)
                sp.wait_ge(s.loaded, 64)

        def head_items(u):
            items = []
            for t in range(TT):
                near = P if t == 0 else 2 * P
                near0 = max(t - 1, 0) * P
                reach = (t + 1) * P
                segs, values = [], []
                for bank, (g, k0, cols) in enumerate(((0, near0, near), (1, 0, reach), (2, 0, reach))):
                    table = tab[g][:, tab[g].shape[1] - cols:]
                    segs.append(seg(stage_to[DIL_GROUPS * u + g][:, t * P:(t + 1) * P],
                                    lambda i, g=g, k0=k0, cols=cols: kT[:, bass.ds(i + 4 * g, 1), k0:k0 + cols].rearrange("p a b -> p (a b)"),
                                    cols, bank, table, lambda i, g=g: slopes[:, bass.ds(i + 4 * g, 1)]))
                    at = sum(x[3] for x in segs[:-1])
                    for j in range(cols // P):
                        values.append((at + j * P, P, lambda i, g=g, kt=k0 // P + j: v[:, kt, bass.ds(i * P + 512 * g, P)]))
                items.append(dict(segs=segs, scale=DIL_HD ** -0.5, values=values, hd=DIL_HD,
                                  dst=lambda i, t=t: y[:, t, bass.ds(i * P, P)]))
            return items

        copies = [(stage_to[DIL_GROUPS * u + g], lambda i, u=u, g=g: one(qT, 2 * i + (u + 4 * g)))
                  for u in range(2) for g in range(DIL_GROUPS)]
        attention(nc, m, DIL_HEADS // 2, copies, turns(2, head_items, DIL_GROUPS), 1280, 3, 1)




def take_halves(dst, shift):
    def take(act, bank):
        for g in range(NSA_GROUPS):
            for h in range(2):
                n = SEQ - shift * h
                ins = act.activation(dst[64 * h:64 * h + 64, g, 0:n], bank[64 * g:64 * g + 64, shift * h:SEQ], ACT.Copy)
        return ins
    return take


def take_all(dst, func=ACT.Copy):
    return lambda act, bank: act.activation(flat(dst[:, :, :]), bank[:, 0:dst.shape[1] * dst.shape[2]], func)


def take_part(takes):
    return lambda act, bank, c, j: takes[j](act, bank)


def compress(nc, m, a, kc, vc, k_cmp, v_cmp):
    n_pos = CMP_BLOCK // 2
    n_col = SEQ // CMP_STRIDE + 1
    with Tensors(nc) as sb, stage(nc, "w1_loaded*2", "w2_loaded", "zeroed", "embedded", "offset", "hidden_ready",
                                  "hidden", "result_ready") as (block, s):
        w1 = [flat(w[:, :, :]).rearrange("p (k n) -> p k n", n=PHI) for w in m.w_slots]
        w2 = [sb("w2_k", [P, 2, P]), sb("w2_v", [P, 2, NSA_HD])]
        off = sb("offset", [P, 4])
        hid = sb("hidden", [P, 4, NSA_GROUPS * N_CMP])
        src = [kc, vc]
        N = NSA_GROUPS * N_CMP

        @block.sync
        def _(sp):
            for i, name in enumerate("kv"):
                sp.dma_start(w1[i], a[f"nsa_phi_{name}_w1"][0].rearrange("(k p) n -> p k n", p=P)).then_inc(s.w1_loaded[i], 16)
            w2k = a["nsa_phi_k_w2"][0].rearrange("(k p) n -> p k n", p=P)
            for h in range(2):
                sp.dma_start(w2[0][:, :, 64 * h:64 * h + 64], w2k).then_inc(s.w2_loaded, 16)
            sp.dma_start(w2[1][:, :, :], a["nsa_phi_v_w2"][0].rearrange("(k p) n -> p k n", p=P)).then_inc(s.w2_loaded, 16)

        @block.tensor
        def _(pe):
            pe.wait_ge(s.embedded, 2)
            for i in range(2):
                pe.wait_ge(s.w1_loaded[i], 16)
                for h in range(2):
                    n = 2 * i + h
                    for k in range(n_pos):
                        rhs = src[i][:, :, 2 * k:2 * k + CMP_STRIDE * (n_col - 1) + 1:CMP_STRIDE]
                        mm = pe.matmul(m.ps[:, (4 + n) * BANK:(4 + n) * BANK + NSA_GROUPS * n_col], w1[i][:, k, h * P:(h + 1) * P],
                                       rhs, start=k == 0, stop=k == n_pos - 1)
                    mm.then_inc(s.hidden_ready, 1)
            pe.wait_ge(s.w2_loaded, 48)
            pe.wait_ge(s.hidden, 4)
            for h in range(2):
                mm = pe.matmul(m.ps[:, 0:N], w2[0][:, h, :], hid[:, h, :], start=h == 0, stop=h == 1)
            mm.then_inc(s.result_ready, 1)
            for g in range(NSA_GROUPS):
                for h in range(2):
                    mm = pe.matmul(m.ps[0:N_CMP, BANK + g * NSA_HD:BANK + (g + 1) * NSA_HD],
                                   hid[:, 2 + h, g * N_CMP:(g + 1) * N_CMP], w2[1][:, h, :], start=h == 0, stop=h == 1)
            mm.then_inc(s.result_ready, 1)

        @block.vector
        def _(dve):
            for t in src:
                dve.memset(t[:, :, SEQ:], 0.0).then_inc(s.zeroed, 1)
            dve.wait_ge(s.zeroed, 2)
            for t, name in zip(src, "kv"):
                dve.tensor_copy(t[:, 0, SEQ::2], m.col[f"nsa_pe_{name}"][:, 0:n_pos]).then_inc(s.embedded, 1)
            dve.memset(k_cmp[:, :, :], 0.0).then_inc(s.zeroed, 1)
            for n in range(4):
                dve.wait_ge(s.hidden_ready, n + 1)
                at = (4 + n) * BANK + n_col - 1
                dve.tensor_copy(off[:, n:n + 1], m.ps[:, at:at + 1]).then_inc(s.offset, 1)
            dve.wait_ge(s.zeroed, 3)
            dve.wait_ge(s.result_ready, 2)
            dve.tensor_copy(k_cmp[:, :, 0:N_CMP], m.ps[:, 0:N].rearrange("p (g n) -> p g n", n=N_CMP))
            dve.tensor_copy(v_cmp[0:N_CMP, :], m.ps[0:N_CMP, BANK:BANK + NSA_GROUPS * NSA_HD])

        @block.scalar
        def _(act):
            for n in range(4):
                act.wait_ge(s.offset, n + 1)
                blocks = m.ps[:, (4 + n) * BANK:(4 + n) * BANK + NSA_GROUPS * n_col].rearrange("p (g n) -> p g n", n=n_col)
                act.activation(hid[:, n, :].rearrange("p (g n) -> p g n", n=N_CMP), blocks[:, :, 0:N_CMP], ACT.Silu,
                               bias=off[:, n:n + 1]).then_inc(s.hidden, 1)


def nsa_layer(nc, m, a, x, moe):
    w = a["nsa_w_in"][0]

    def job(name, chunks, width, kind, take):
        return dict(w=w, col=NSA_COLS[name], chunks=chunks, width=width, kind=kind, take=take)

    with Tensors(nc) as sb:
        xT = columns_pair(sb, "nsa_xT", DK, SEQ)
        fetch_ahead(nc, m, job_pieces(job("kc", 1, 512, "M", None)))
        with Tensors(nc) as sb1:
            rows = sb1("rows", [P, TT, D])
            rms_rows(nc, m, x, TT, rows, NORM_EPS)
            to_columns(nc, m, rows, TT, None, m.col["nsa_norm"], xT)
        yT = sb("nsa_yT", [P, NSA_OUT // P, SEQ])
        with Tensors(nc) as sb1:
            y = sb1("y_rows", [P, TT, NSA_OUT])
            with Tensors(nc) as sb2:
                qT = sb2("qT", [P, 8, SEQ])
                kc, vc = (sb2(n, [P, NSA_GROUPS, SEQ + CMP_BLOCK]) for n in ("kc", "vc"))
                ks, kw = (sb2(n, [P, NSA_GROUPS, SEQ]) for n in ("ks", "kw"))
                vs, vw = (sb2(n, [P, TT, P]) for n in ("vs", "vw"))
                k_cmp = sb2("k_cmp", [P, NSA_GROUPS, 32])
                v_cmp = sb2("v_cmp", [32, NSA_GROUPS * NSA_HD])
                gates = sb2("gates", [P, TT, 3 * NSA_HEADS])
                projection(nc, m, xT, [
                    dict(job("kc", 1, 512, "M", take_part([take_halves(kc, 1), take_halves(vc, 1), take_halves(ks, 0),
                                                           take_all(vs)])),
                         parts=[("T", 0, P), ("T", P, P), ("T", 2 * P, P), ("N", 3 * P, P)]),
                    dict(job("kw", 1, 304, "M", take_part([take_halves(kw, 0), take_all(vw), take_all(gates, ACT.Sigmoid)])),
                         parts=[("T", 0, P), ("N", P, P), ("N", 2 * P, 3 * NSA_HEADS)]),
                    job("q", 2, 512, "T", take_T(qT)),
                ], ahead=True)
                compress(nc, m, a, kc, vc, k_cmp, v_cmp)
                nsa_attention(nc, m, a, qT, ks, kw, k_cmp, vs, vw, v_cmp, gates, y, moe)
            with Tensors(nc) as sb2:
                gate = sb2("gate_rows", [P, TT, NSA_OUT])
                qmT = sb2("qmT", [P, 2, SEQ])
                kmT = sb2("kmT", [P, 2, N_MEM])
                vm = sb2("vm", [P, MT, MEM_HEADS * MEM_HD])
                memT = columns_pair(sb2, "memT", DK, N_MEM)
                fetch_ahead(nc, m, job_pieces(job("z", 2, 512, "N", None)))
                normed_memory(nc, m, a["mem"][0], m.col["nsa_mem_norm"], memT)
                projection(nc, m, xT, [
                    job("z", 2, 512, "N", take_N(gate, ACT.Silu)),
                    job("qm", 1, 256, "T", take_T(qmT, per=2)),
                    job("zm", 1, 256, "N", lambda act, bank, c, j: act.activation(gate[:, j, 1024:1280], bank, ACT.Silu)),
                ] + memory_kv(memT, a["nsa_w_mem_kv"][0], 256, kmT, vm), ahead=True)
                memory_attention(nc, m, MEM_HEADS, MEM_HD, qmT, kmT, vm, y, 1024)
                fetch_ahead(nc, m, output_pieces(a["nsa_w_out"][0]))
                gate_rows(nc, [(flat(y[:, :, :]), flat(gate[:, :, :]))])
            yT = [yT[:, k, :] for k in range(NSA_OUT // P)]
            to_columns(nc, m, y, TT, yT)
        output_product(nc, m, yT, a["nsa_w_out"][0], x, ahead=True)


def nsa_attention(nc, m, a, qT, ks, kw, k_cmp, vs, vw, v_cmp, gates, y, moe):
    with Tensors(nc) as sb:
        stage_to = staging(m, 2)
        causal = sb("causal", [P, SEQ])
        cmp_tab = sb("cmp_tab", [P, TT, 32])
        sees_any = sb("sees_any", [P, 1])
        slopes = sb("slopes", [P, NSA_HEADS])
        zeros = sb("zeros", [P, D])
        with stage(nc, "loaded") as (block, s):
            @block.sync
            def _(sp):
                sp.dma_start(causal[:, :], a["dist_causal"]).then_inc(s.loaded, 16)
                sp.dma_start(cmp_tab[:, :, :], a["dist_cmp"]).then_inc(s.loaded, 16)
                sp.dma_start(sees_any[:, :], a["sees_any"]).then_inc(s.loaded, 16)
                sp.dma_start(slopes[:, :], a["nsa_slopes"].partition_broadcast(P)).then_inc(s.loaded, 16)
                sp.wait_ge(s.loaded, 64)

            @block.gpsimd
            def _(pool):
                pool.memset(zeros[:, :], 0.0)

            @block.vector
            def _(dve):
                dve.wait_ge(s.loaded, 64)
                g = gates[:, 0, 0:3 * NSA_HEADS:3]
                dve.tensor_scalar(g, g, sees_any[:, 0:1], None, ALU.mult)
        for g in range(NSA_GROUPS):
            def pair_items(u, g=g):
                items = []
                for h in range(2):
                    rows = slice(64 * h, 64 * h + 64)
                    for t in range(TT):
                        q = stage_to[u][rows, t * P:(t + 1) * P]
                        reach = (t + 1) * P

                        def slope(i, g=g, h=h):
                            return slopes[:, bass.ds(2 * i + (8 * g + h), 1)]

                        def dst(i, g=g, h=h, t=t):
                            return y[:, t, bass.ds(i * P + (512 * g + 64 * h), NSA_HD)]

                        def gate(b):
                            return lambda i, g=g, h=h, t=t: gates[:, t, bass.ds(6 * i + (24 * g + 3 * h + b), 1)]

                        items.append(dict(
                            segs=[seg(q, lambda i, g=g, rows=rows: k_cmp[rows, g, :], 32, 0, cmp_tab[:, t, :], slope)],
                            scale=NSA_HD ** -0.5, hd=NSA_HD, coef=gate(0), dst=dst,
                            values=[(0, N_CMP, lambda i, g=g: v_cmp[0:N_CMP, g * NSA_HD:(g + 1) * NSA_HD])]))
                        for b, (k_, v_) in enumerate(((ks, vs), (kw, vw))):
                            items.append(dict(
                                segs=[seg(q, lambda i, k_=k_, g=g, rows=rows, reach=reach: k_[rows, g, 0:reach], reach, 0,
                                          causal[:, SEQ - reach:], slope)],
                                scale=NSA_HD ** -0.5, hd=NSA_HD, coef=gate(b + 1), dst=dst, add=True,
                                values=[(j * P, P, lambda i, v_=v_, j=j, g=g: v_[:, j, g * NSA_HD:(g + 1) * NSA_HD])
                                        for j in range(t + 1)]))
                return items

            copies = [(stage_to[u], lambda i, u=u, g=g: one(qT, 2 * i + (u + 4 * g))) for u in range(2)]
            attention(nc, m, 2, copies, turns(2, pair_items, 1), SEQ, 1, 2, [(moe.x_rows, moe.y_rows)[g]], zeros, ahead=2)




def rope_tables(nc, m, a, cos, sin):
    magic = 1.5 * 2.0 ** 23
    c1 = 6.28125
    c2 = float(np.float32(np.round((2 * np.pi - c1) * 2 ** 21) / 2 ** 21))
    c3 = float(np.float32(2 * np.pi - c1 - c2))
    with Tensors(nc) as sb, stage(nc, "loaded", "step", "reduced") as (block, s):
        pos = sb("pos", [P, SEQ], I32)
        posf = sb("posf", [P, SEQ])
        freq = sb("freq", [P, 1])
        ang = sb("ang", [P, SEQ])
        turns = sb("turns", [P, SEQ])

        @block.sync
        def _(sp):
            sp.dma_start(pos[:, :], a["positions_2"].partition_broadcast(P)).then_inc(s.loaded, 16)
            sp.dma_start(freq[:, :], a["rope_freq"]).then_inc(s.loaded, 16)

        @block.vector
        def _(dve):
            count = 0

            def link(ins):
                nonlocal count
                count += 1
                ins.then_inc(s.step, 1)
                dve.wait_ge(s.step, count)

            dve.wait_ge(s.loaded, 32)
            link(dve.tensor_copy(posf[:, :], pos[:, :]))
            link(dve.tensor_scalar(ang[:, :], posf[:, :], freq[:, 0:1], None, ALU.mult))
            for dst, quarter in ((sin, 0.0), (cos, 0.25)):
                link(dve.tensor_scalar(turns[:, :], ang[:, :], 1 / (2 * np.pi), quarter, ALU.mult, ALU.add))
                link(dve.tensor_scalar(turns[:, :], turns[:, :], magic, None, ALU.add))
                link(dve.tensor_scalar(turns[:, :], turns[:, :], -magic, None, ALU.add))
                src = ang
                for c in (c1, c2, c3):
                    link(dve.scalar_tensor_tensor(out=dst[:, :], in0=turns[:, :], scalar=-c, in1=src[:, :],
                                                  op0=ALU.mult, op1=ALU.add))
                    src = dst
                if quarter:
                    link(dve.tensor_scalar(dst[:, :], dst[:, :], np.pi / 2, None, ALU.add))
                top = float(np.nextafter(np.float32(np.pi), np.float32(0)))
                link(dve.tensor_scalar(dst[:, :], dst[:, :], top, -top, ALU.min, ALU.max))
            dve.sem_inc(s.reduced, 1)

        @block.scalar
        def _(act):
            act.wait_ge(s.reduced, 1)
            act.activation(sin[:, :], sin[:, :], ACT.Sin)
            act.activation(cos[:, :], cos[:, :], ACT.Sin)


def rope(nc, m, tensors, cos, sin):
    with Tensors(nc) as sb, stage(nc, "rotated", "straight", "crossed", "summed") as (block, s):
        a_ = sb("straight", [P, 2, SEQ])
        b_ = sb("crossed", [P, 2, SEQ])
        n_tiles = tensors[0].shape[1]

        def tiles(eng):
            for w, t in enumerate(tensors):
                with eng.Fori(0, n_tiles // 2) as i:
                    for u in range(2):
                        yield t, 2 * i + u, u, 2 * i + (w * n_tiles + u)


        @block.tensor
        def _(pe):
            for t, tile, u, q in tiles(pe):
                pe.wait_ge(s.summed, q + 1)
                pe.matmul(m.ps[:, u * BANK:(u + 1) * BANK], m.rotate[:, :], one(t, tile), start=True, stop=True).then_inc(s.rotated, 1)

        @block.gpsimd
        def _(pool):
            for t, tile, u, q in tiles(pool):
                pool.wait_ge(s.summed, q + 1)
                pool.tensor_tensor(a_[:, u, :], one(t, tile), cos[:, :], ALU.mult).then_inc(s.straight, 1)

        @block.vector
        def _(dve):
            dve.sem_inc(s.summed, 2)
            for t, tile, u, q in tiles(dve):
                dve.wait_ge(s.rotated, q + 1)
                dve.tensor_tensor(b_[:, u, :], m.ps[:, u * BANK:(u + 1) * BANK], sin[:, :], ALU.mult).then_inc(s.crossed, 1)
                dve.wait_ge(s.crossed, q + 1)
                dve.wait_ge(s.straight, q + 1)
                dve.tensor_tensor(one(t, tile), a_[:, u, :], b_[:, u, :], ALU.add).then_inc(s.summed, 1)


def diff_lambda(nc, m, a, layer, minus_lam):
    init = 0.8 - 0.6 * float(np.exp(-0.3 * layer))
    with Tensors(nc) as sb, stage(nc, "loaded", "step", "exped") as (block, s):
        v = sb("lambda_rows", [P, 4, 64])
        prod = sb("prod", [P, 2, 64])
        dots = sb("dots", [P, 2])
        ex = sb("exps", [P, 2])

        @block.sync
        def _(sp):
            for i, name in enumerate(("q1", "q2", "k1", "k2")):
                sp.dma_start(v[:, i, :], a[f"lambda_{name}_2"][layer:layer + 1, :].partition_broadcast(P)).then_inc(s.loaded, 16)

        @block.vector
        def _(dve):
            dve.wait_ge(s.loaded, 64)
            dve.tensor_tensor(prod[:, :, :], v[:, 0:2, :], v[:, 2:4, :], ALU.mult).then_inc(s.step, 1)
            dve.wait_ge(s.step, 1)
            dve.tensor_reduce(dots[:, :], prod[:, :, :], AX_X, ALU.add).then_inc(s.step, 1)
            dve.wait_ge(s.exped, 1)
            dve.tensor_tensor(dots[:, 0:1], ex[:, 1:2], ex[:, 0:1], ALU.subtract).then_inc(s.step, 1)
            dve.wait_ge(s.step, 3)
            dve.tensor_scalar(minus_lam[:, :], dots[:, 0:1], -init, None, ALU.add)

        @block.scalar
        def _(act):
            act.wait_ge(s.step, 2)
            act.activation(ex[:, :], dots[:, :], ACT.Exp).then_inc(s.exped, 1)


def diff_attention(nc, m, a, qT, kT, v, minus_lam, y):
    with Tensors(nc) as sb:
        stage_to = staging(m, 4)
        mask = sb("mask", [P, SEQ])
        with stage(nc, "loaded") as (block, s):
            @block.sync
            def _(sp):
                sp.dma_start(mask[:, :], a["mask_causal"]).then_inc(s.loaded, 16)
                sp.wait_ge(s.loaded, 16)

        def head_items(u):
            q_here, k_here = stage_to[2 * u], stage_to[2 * u + 1]
            items = []
            for t in range(TT):
                for c in range(2):
                    rows = slice(64 * c, 64 * c + 64)
                    reach = (t + 1) * P
                    items.append(dict(
                        segs=[seg(q_here[rows, t * P:(t + 1) * P], lambda i, rows=rows, reach=reach: k_here[rows, 0:reach],
                                  reach, 0, mask[:, SEQ - reach:])],
                        scale=0.125, hd=DA_V, add=c == 1, coef=(lambda i: minus_lam[:, 0:1]) if c else None,
                        dst=lambda i, t=t: y[:, t, bass.ds(i * P, P)],
                        values=[(j * P, P, lambda i, j=j: v[:, j, bass.ds(i * P, P)]) for j in range(t + 1)]))
            return items

        copies = []
        for u in range(2):
            copies += [(stage_to[2 * u], lambda i, u=u: one(qT, 2 * i + u)), (stage_to[2 * u + 1], lambda i, u=u: one(kT, 2 * i + u))]
        attention(nc, m, DA_HEADS // 2, copies, turns(2, head_items, 2), SEQ, 1, 2)


def head_norm(nc, m, y, factor):
    n = TT * DA_HEADS
    with Tensors(nc) as sb, stage(nc, "squared", "step", "rooted") as (block, s):
        sq = m.w_slots[0][:, :, :].rearrange("p a b -> p (a b)").rearrange("p (n c) -> p n c", c=P)
        sums, root, inv = (sb(x, [P, n]) for x in ("sums", "root", "inv"))
        heads = flat(y[:, :, :]).rearrange("p (n d) -> p n d", d=P)

        @block.scalar
        def _(act):
            act.activation(flat(sq[:, :, :]), flat(y[:, :, :]), ACT.Square).then_inc(s.squared, 1)
            act.wait_ge(s.step, 2)
            act.activation(root[:, :], sums[:, :], ACT.Sqrt).then_inc(s.rooted, 1)

        @block.vector
        def _(dve):
            dve.wait_ge(s.squared, 1)
            dve.tensor_reduce(sums[:, :], sq[:, :, :], AX_X, ALU.add).then_inc(s.step, 1)
            dve.wait_ge(s.step, 1)
            dve.tensor_scalar(sums[:, :], sums[:, :], 1.0 / P, LN_EPS, ALU.mult, ALU.add).then_inc(s.step, 1)
            dve.wait_ge(s.rooted, 1)
            dve.reciprocal(inv[:, :], root[:, :]).then_inc(s.step, 1)
            dve.wait_ge(s.step, 3)
            refine_rsqrt(dve, s.step, 3, sums[:, :], inv[:, :], root[:, :])
            dve.tensor_scalar(inv[:, :], inv[:, :], factor, None, ALU.mult).then_inc(s.step, 1)
            dve.wait_ge(s.step, 7)
            dve.tensor_tensor(heads, heads, inv[:, :].unsqueeze(2).broadcast_to([P, n, P]), ALU.mult)


def gated_conv(nc, m, cb, cc, cu, weights, yT):
    K = CONV2 // P
    with Tensors(nc) as sb, stage(nc, "step") as (block, s):
        z = sb("z", [P, K, 2 + SEQ])

        @block.vector
        def _(dve):
            dve.memset(z[:, :, 0:2], 0.0).then_inc(s.step, 1)
            dve.tensor_tensor(z[:, :, 2:], cc[:, :, :], cu[:, :, :], ALU.mult).then_inc(s.step, 1)
            dve.wait_ge(s.step, 2)
            for j in range(3):
                if j:
                    dve.wait_ge(s.step, 2 + K * j)
                for k in range(K):
                    col = weights[:, j * K + k:j * K + k + 1]
                    if j == 0:
                        ins = dve.tensor_scalar(yT[:, k, :], z[:, k, 0:SEQ], col, None, ALU.mult)
                    else:
                        ins = dve.scalar_tensor_tensor(out=yT[:, k, :], in0=z[:, k, j:j + SEQ], scalar=col, in1=yT[:, k, :],
                                                       op0=ALU.mult, op1=ALU.add)
                    ins.then_inc(s.step, 1)
            dve.wait_ge(s.step, 2 + 3 * K)
            dve.tensor_tensor(yT[:, :, :], yT[:, :, :], cb[:, :, :], ALU.mult)


def merge_branches(nc, m, xT, w_gates, branches, mergedT):
    steps = [(n, b) for n in range(2) for b in range(3)]
    pieces = []
    for q, (n, b) in enumerate(steps):
        pieces += [(q, True, 0, False), (q, True, 4, True)]
        K = branches[b][2]
        pieces += [(q, False, k, k + 4 == K) for k in range(0, K, 4)]
    last_of = {(q, gate): r for r, (q, gate, k0, last) in enumerate(pieces) if last}
    with Tensors(nc) as sb, stage(nc, "weights_loaded*2", "rounded", "y_split", "weights_split", "read", "gated",
                                  "multiplied", "added") as (block, s):
        sig = sb("sig", [P, 4, SEQ])
        prod = sb("prod", [P, 2, SEQ])
        y_hi = [sb("branch_hi", [P, K, SEQ]) for _, _, K in branches]
        y_base = [0]
        for _, _, K in branches:
            y_base.append(y_base[-1] + K)

        @block.sync
        def _(sp):
            for r, (q, gate, k0, last) in enumerate(pieces):
                n, b = steps[q]
                if r < 2:
                    take_fetched(sp, m, s.weights_loaded[r])
                    continue
                sp.wait_ge(s.read, 4 * (r - 1))
                if gate:
                    src = rows_of(w_gates, k0, 4, b * D + n * 512, 512)
                else:
                    src = rows_of(branches[b][1], k0, 4, n * 512, 512)
                sp.dma_start(weight_part(m, r % 2)[1], src).then_inc(
                    s.weights_loaded[r % 2], 16)

        @block.tensor
        def _(pe):
            for r, (q, gate, k0, last) in enumerate(pieces):
                n, b = steps[q]
                hi, lo = weight_part(m, r % 2)
                pe.wait_ge(s.weights_split, r + 1)
                if gate:
                    right_hi, right_lo = xT.hi, xT.lo
                else:
                    right_hi, right_lo = y_hi[b], branches[b][0]
                    pe.wait_ge(s.y_split, y_base[b] + k0 + 4)
                for j in range(4):
                    if k0 == 0 and q:
                        pe.wait_ge(s.gated if gate else s.multiplied, 4 * (q - 1) + j + 1)
                    bank = (j if gate else 4 + j) * BANK
                    for k in range(4):
                        mm = three_passes(pe, m.ps[:, bank:bank + BANK], (hi[:, k, j * P:(j + 1) * P], lo[:, k, j * P:(j + 1) * P]),
                                          (right_hi[:, k0 + k, :], right_lo[:, k0 + k, :]), k0 + k == 0, last and k == 3)
                    mm.then_inc(s.read, 1)

        @block.scalar
        def _(act):
            for q in range(len(steps)):
                for j in range(4):
                    act.wait_ge(s.read, 4 * last_of[q, True] + j + 1)
                    if q:
                        act.wait_ge(s.multiplied, 4 * (q - 1) + j + 1)
                    act.activation(sig[:, j, :], m.ps[:, j * BANK:(j + 1) * BANK], ACT.Sigmoid).then_inc(s.gated, 1)

        @block.vector
        def _(dve):
            counts = [0, 0]

            def split_weights(r):
                dve.wait_ge(s.weights_loaded[r % 2], 16 * (r // 2) + 16)
                counts[0] += 1
                split(dve, *weight_part(m, r % 2), s.rounded, counts[0], s.weights_split)

            def split_branch(b):
                for k in range(branches[b][2]):
                    counts[0] += 1
                    split(dve, y_hi[b][:, k, :], branches[b][0][:, k, :], s.rounded, counts[0], s.y_split)

            def merge(q):
                n, b = steps[q]
                for j in range(4):
                    dve.wait_ge(s.gated, 4 * q + j + 1)
                    dve.wait_ge(s.read, 4 * last_of[q, False] + j + 1)
                    dst = mergedT[:, 4 * n + j, :]
                    to = prod[:, j % 2, :] if b else dst
                    dve.tensor_tensor(to, sig[:, j, :], m.ps[:, (4 + j) * BANK:(5 + j) * BANK], ALU.mult).then_inc(s.multiplied, 1)
                    if b:
                        dve.wait_ge(s.multiplied, 4 * q + j + 1)
                        if b == 2:
                            dve.wait_ge(s.added, counts[1] - 3)
                        dve.tensor_tensor(dst, dst, prod[:, j % 2, :], ALU.add).then_inc(s.added, 1)
                        counts[1] += 1

            merge_after = {min(last_of[q, False] + 1, len(pieces) - 1): q for q in range(len(steps) - 1)}
            for r, (q, gate, k0, last) in enumerate(pieces):
                split_weights(r)
                if q < 3 and gate and k0 == 4:
                    split_branch(steps[q][1])
                if r in merge_after:
                    merge(merge_after[r])
            merge(len(steps) - 1)


def route(nc, m, a, xT, x, moe):
    G, E = N_EGROUPS, PER_GROUP
    with Tensors(nc) as sb, stage(nc, "loaded", "logits_ready", "step", "centred", "exped", "chosen", "ranked",
                                  "placed", "copied") as (block, s):
        w = sb("w_router", [P, DK, N_EXPERTS])
        bias = sb("bias", [P, N_EXPERTS])
        lg = sb("logits", [P, TT, N_EXPERTS])
        sc = sb("scores", [P, TT, N_EXPERTS])
        one_, two, best = (sb(n, [P, TT]) for n in ("one", "two", "best"))
        gm, gsel, hit, first, second, inside = (sb(n, [P, TT, 4]) for n in (
            "group_top", "group_sel", "hit", "first", "second", "inside"))
        avail = sb("avail", [P, TT, 1])
        tmp = sb("tmp", [P, TT, N_EXPERTS])
        pick = [sb("pick_first", [P, TT, N_EXPERTS]), sb("pick_second", [P, TT, N_EXPERTS])]
        picked = sb("picked", [P, TT, N_EXPERTS])
        place = sb("place", [P, TT, N_EXPERTS])
        slot = sb("slot", [P, TT, 2])
        cnt, nblk, end = (sb(n, [P, N_EXPERTS]) for n in ("count", "blocks", "block_end"))
        number = sb("block_number", [P, MAX_BLOCKS])
        before = sb("before", [P, P])
        ones = sb("ones", [P, P])
        by_block = sb("by_block", [P, MAX_BLOCKS, N_EXPERTS])
        owner = sb("owner", [P, MAX_BLOCKS])

        @block.sync
        def _(sp):
            sp.dma_start(w[:, :, :], a["w_router_2"].rearrange("(k p) n -> p k n", p=P)).then_inc(s.loaded, 16)
            sp.dma_start(bias[:, :], a["router_bias_2"].rearrange("(a n) -> a n", a=1).partition_broadcast(P)).then_inc(s.loaded, 16)
            sp.dma_start(number[:, :], a["block_number"].partition_broadcast(P)).then_inc(s.loaded, 16)
            sp.dma_start(before[:, :], a["before"]).then_inc(s.loaded, 16)

        @block.tensor
        def _(pe):
            pe.wait_ge(s.loaded, 64)
            for t in range(TT):
                for k in range(DK):
                    mm = pe.matmul(m.ps[:, t * N_EXPERTS:(t + 1) * N_EXPERTS], xT[:, k, t * P:(t + 1) * P], w[:, k, :],
                                   start=k == 0, stop=k == DK - 1)
            mm.then_inc(s.logits_ready, 1)
            pe.wait_ge(s.chosen, 1)
            for t in range(TT):
                out = m.ps[:, BANK + t * N_EXPERTS:BANK + (t + 1) * N_EXPERTS]
                for u in range(t):
                    pe.matmul(out, ones[:, :], picked[:, u, :], start=u == 0, stop=False)
                pe.matmul(out, before[:, :], picked[:, t, :], start=t == 0, stop=True)
            for t in range(TT):
                mm = pe.matmul(m.ps[:, 2 * BANK:2 * BANK + N_EXPERTS], ones[:, :], picked[:, t, :], start=t == 0, stop=t == TT - 1)
            mm.then_inc(s.ranked, 1)

        @block.scalar
        def _(act):
            act.wait_ge(s.centred, 1)
            act.activation(flat(sc[:, :, :]), flat(lg[:, :, :]), ACT.Exp).then_inc(s.exped, 1)

        @block.gpsimd
        def _(pool):
            pool.wait_ge(s.placed, 1)
            for t in range(TT):
                for i in range(2):
                    pool.indirect_dma_start(out=moe.x_rows, out_offset=bass.IndirectOffsetOnAxis(ap=moe.slot[:, 2 * t + i:2 * t + i + 1], axis=0),
                                            in_=x[:, t, :], in_offset=None).then_inc(s.copied, 16)
            pool.wait_ge(s.copied, 16 * 2 * TT)

        @block.vector
        def _(dve):
            count = 0

            def link(ins):
                nonlocal count
                count += 1
                ins.then_inc(s.step, 1)
                dve.wait_ge(s.step, count)

            def tt(out, x, y, op):
                link(dve.tensor_tensor(out, x, y, op))

            def spread(v, n):
                return v.unsqueeze(2).broadcast_to([P, TT, n])

            def first_of(out, values, top):
                tt(hit[:, :, :], values, spread(top, 4), ALU.is_equal)
                link(dve.memset(avail[:, :, :], 1.0))
                for j in range(4):
                    tt(out[:, :, j:j + 1], hit[:, :, j:j + 1], avail[:, :, :], ALU.mult)
                    tt(avail[:, :, :], avail[:, :, :], out[:, :, j:j + 1], ALU.subtract)

            link(dve.memset(ones[:, :], 1.0))
            dve.wait_ge(s.logits_ready, 1)
            tt(lg[:, :, :], m.ps[:, 0:TT * N_EXPERTS].rearrange("p (t e) -> p t e", t=TT),
               bias[:, :].unsqueeze(1).broadcast_to([P, TT, N_EXPERTS]), ALU.add)
            link(dve.tensor_reduce(best[:, :], lg[:, :, :], AX_X, ALU.max))
            tt(lg[:, :, :], lg[:, :, :], spread(best[:, :], N_EXPERTS), ALU.subtract)
            dve.sem_inc(s.centred, 1)
            dve.wait_ge(s.exped, 1)
            link(dve.tensor_reduce(one_[:, :], sc[:, :, :], AX_X, ALU.add))
            link(dve.reciprocal(two[:, :], one_[:, :]))
            tt(sc[:, :, :], sc[:, :, :], spread(two[:, :], N_EXPERTS), ALU.mult)
            link(dve.tensor_reduce(gm[:, :, :], sc[:, :, :].rearrange("p t (g e) -> p t g e", g=G), AX_X, ALU.max))
            link(dve.tensor_reduce(best[:, :], gm[:, :, :], AX_X, ALU.max))
            first_of(gsel[:, :, :], gm[:, :, :], best[:, :])
            for g in range(G):
                mine = sc[:, :, g * E:(g + 1) * E]
                sel = gsel[:, :, g:g + 1].broadcast_to([P, TT, E])
                if g == 0:
                    tt(inside[:, :, :], mine, sel, ALU.mult)
                else:
                    tt(tmp[:, :, 0:E], mine, sel, ALU.mult)
                    tt(inside[:, :, :], inside[:, :, :], tmp[:, :, 0:E], ALU.add)
            first_of(first[:, :, :], inside[:, :, :], best[:, :])
            link(dve.scalar_tensor_tensor(out=tmp[:, :, 0:E], in0=first[:, :, :], scalar=-2.0, in1=inside[:, :, :],
                                          op0=ALU.mult, op1=ALU.add))
            link(dve.tensor_reduce(two[:, :], tmp[:, :, 0:E], AX_X, ALU.max))
            first_of(second[:, :, :], tmp[:, :, 0:E], two[:, :])
            for p_, chosen in zip(pick, (first, second)):
                for g in range(G):
                    tt(p_[:, :, g * E:(g + 1) * E], chosen[:, :, :], gsel[:, :, g:g + 1].broadcast_to([P, TT, E]), ALU.mult)
            tt(picked[:, :, :], pick[0][:, :, :], pick[1][:, :, :], ALU.add)
            dve.sem_inc(s.chosen, 1)
            tt(one_[:, :], best[:, :], two[:, :], ALU.add)
            link(dve.reciprocal(one_[:, :], one_[:, :]))
            tt(moe.share[:, :, 0], best[:, :], one_[:, :], ALU.mult)
            tt(moe.share[:, :, 1], two[:, :], one_[:, :], ALU.mult)
            dve.wait_ge(s.ranked, 1)
            dve.wait_ge(s.loaded, 64)
            link(dve.tensor_copy(cnt[:, :], m.ps[:, 2 * BANK:2 * BANK + N_EXPERTS]))
            link(dve.tensor_scalar(nblk[:, :], cnt[:, :], 0.0, None, ALU.is_gt))
            for j in range(1, TT):
                link(dve.scalar_tensor_tensor(out=nblk[:, :], in0=cnt[:, :], scalar=float(j * P), in1=nblk[:, :],
                                              op0=ALU.is_gt, op1=ALU.add))
            link(dve.tensor_tensor_scan(end[:, :], ones[:, 0:N_EXPERTS], nblk[:, :], 0.0, ALU.mult, ALU.add))
            tt(cnt[:, :], end[:, :], nblk[:, :], ALU.subtract)
            link(dve.scalar_tensor_tensor(out=place[:, :, :], in0=cnt[:, :].unsqueeze(1).broadcast_to([P, TT, N_EXPERTS]),
                                          scalar=float(P), in1=m.ps[:, BANK:BANK + TT * N_EXPERTS].rearrange("p (t e) -> p t e", t=TT),
                                          op0=ALU.mult, op1=ALU.add))
            for i in range(2):
                tt(tmp[:, :, :], pick[i][:, :, :], place[:, :, :], ALU.mult)
                link(dve.tensor_reduce(slot[:, :, i], tmp[:, :, :], AX_X, ALU.add))
            link(dve.tensor_copy(moe.slot[:, :], flat(slot[:, :, :])))
            dve.sem_inc(s.placed, 1)
            tt(by_block[:, :, :], end[:, :].unsqueeze(1).broadcast_to([P, MAX_BLOCKS, N_EXPERTS]),
               number[:, :].unsqueeze(2).broadcast_to([P, MAX_BLOCKS, N_EXPERTS]), ALU.is_le)
            link(dve.tensor_reduce(owner[:, :], by_block[:, :, :], AX_X, ALU.add))
            link(dve.tensor_scalar(moe.block_expert[:, :], owner[:, :], float(N_EXPERTS - 1), None, ALU.min))
            link(dve.tensor_scalar(owner[:, 0:MAX_BLOCKS // 2], number[:, 0:MAX_BLOCKS:2], end[:, N_EXPERTS - 1:N_EXPERTS],
                                   None, ALU.is_lt))
            link(dve.tensor_reduce(cnt[:, 0:1], owner[:, 0:MAX_BLOCKS // 2], AX_X, ALU.add))
            link(dve.tensor_copy(moe.n_pairs[:, :], cnt[:, 0:1]))


def experts(nc, m, a, layer, moe):
    F = D_FF // P
    with Tensors(nc) as sb, stage(nc, "x_loaded*2", "gate_loaded*2", "up_loaded*2", "down_loaded*2", "x_turned*2", "xT_ready*2", "gate_ready*2",
                                  "up_ready*2", "silu_done*2", "hidden_done*2", "h_turned*2", "hT_ready*2", "out_ready*2",
                                  "out_taken*2", "y_stored*2", "y_left*2") as (block, s):
        wg = m.w_slots
        wu = [sb("w_up", [P, DK, D_FF]) for _ in range(2)]
        wd = [sb("w_down", [P, F, D]) for _ in range(2)]
        xe = [sb("block_x", [P, D]) for _ in range(2)]
        xeT = [sb("block_xT", [P, DK, P]) for _ in range(2)]
        sg = [sb("silu", [P, D_FF]) for _ in range(2)]
        h = [sb("hidden", [P, D_FF]) for _ in range(2)]
        hT = [sb("hidden_T", [P, F, P]) for _ in range(2)]
        ye = [sb("block_y", [P, D]) for _ in range(2)]
        x_banks, gate_bank, up_bank, turn_bank, out_banks = ((0, 1), (6, 7)), (2, 4), (3, 5), (0, 1), ((6, 7), (2, 3))

        def bank(b):
            return m.ps[:, b * BANK:(b + 1) * BANK]

        def n_pairs(eng):
            return eng.value_load(moe.n_pairs[0:1, 0:1], min_val=1, max_val=MAX_BLOCKS // 2)


        @block.sync
        def _(sp):
            with sp.Fori(0, n_pairs(sp)) as i:
                expert = [None, None]
                for u in range(2):
                    b = 2 * i + u
                    expert[u] = sp.value_load(moe.block_expert[0:1, bass.ds(b, 1)], min_val=0, max_val=N_EXPERTS - 1)
                    sp.wait_ge(s.up_ready[u], i + 1)
                    sp.dma_start(xe[u][:, :], moe.x_rows[bass.ds(b * P, P), :]).then_inc(s.x_loaded[u], 16)
                    for w, name, loaded in ((wg[u], "w_exp_gate_2", s.gate_loaded[u]), (wu[u], "w_exp_up_2", s.up_loaded[u])):
                        src = a[name][layer][bass.ds(expert[u], 1), :, :].rearrange("e (k p) n -> p (e k) n", p=P)
                        sp.dma_start(w[:, :, :], src).then_inc(loaded, 16)
                for u in range(2):
                    sp.wait_ge(s.out_ready[u], 2 * i + 1)
                    src = a["w_exp_down_2"][layer][bass.ds(expert[u], 1), :, :].rearrange("e (k p) n -> p (e k) n", p=P)
                    sp.dma_start(wd[u][:, :, :], src).then_inc(s.down_loaded[u], 16)

        @block.tensor
        def _(pe):
            for u in range(2):
                pe.sem_inc(s.up_ready[u], 1)
                pe.sem_inc(s.out_ready[u], 1)

            def turn_x(i, u):
                pe.wait_ge(s.x_loaded[u], 16 * i + 16)
                if u:
                    pe.wait_ge(s.out_taken[0], 2 * i + 1)
                for half in range(2):
                    for k in range(4):
                        mm = pe.transpose(m.ps[:, x_banks[u][half] * BANK + k * P:x_banks[u][half] * BANK + (k + 1) * P],
                                          xe[u][:, (4 * half + k) * P:(4 * half + k + 1) * P], m.ident[:, :])
                    mm.then_inc(s.x_turned[u], 1)

            def project(i, u, w, out, done):
                for k in range(DK):
                    mm = pe.matmul(bank(out), xeT[u][:, k, :], w[:, k, :], start=k == 0, stop=k == DK - 1)
                mm.then_inc(done, 1)

            def gate(i, u):
                pe.wait_ge(s.xT_ready[u], 2 * i + 2)
                pe.wait_ge(s.gate_loaded[u], 16 * i + 16)
                if u == 0:
                    pe.wait_ge(s.out_taken[1], 2 * i + 1)
                project(i, u, wg[u], gate_bank[u], s.gate_ready[u])

            def up(i, u):
                pe.wait_ge(s.up_loaded[u], 16 * i + 16)
                project(i, u, wu[u], up_bank[u], s.up_ready[u])

            def turn_h(i, u):
                pe.wait_ge(s.hidden_done[u], i + 1)
                for k in range(F):
                    mm = pe.transpose(m.ps[:, turn_bank[u] * BANK + k * P:turn_bank[u] * BANK + (k + 1) * P],
                                      h[u][:, k * P:(k + 1) * P], m.ident[:, :])
                mm.then_inc(s.h_turned[u], 1)

            def down(i, u):
                pe.wait_ge(s.hT_ready[u], i + 1)
                pe.wait_ge(s.down_loaded[u], 16 * i + 16)
                for n in range(2):
                    for k in range(F):
                        mm = pe.matmul(bank(out_banks[u][n]), hT[u][:, k, :], wd[u][:, k, n * 512:(n + 1) * 512],
                                       start=k == 0, stop=k == F - 1)
                    mm.then_inc(s.out_ready[u], 1)

            with pe.Fori(0, n_pairs(pe)) as i:
                turn_x(i, 0)
                turn_x(i, 1)
                gate(i, 0)
                up(i, 0)
                gate(i, 1)
                turn_h(i, 0)
                up(i, 1)
                down(i, 0)
                turn_h(i, 1)
                down(i, 1)

        @block.scalar
        def _(act):
            with act.Fori(0, n_pairs(act)) as i:
                for u in range(2):
                    act.wait_ge(s.x_turned[u], 2 * i + 1)
                    act.activation(flat(xeT[u][:, 0:4, :]), bank(x_banks[u][0]), ACT.Copy).then_inc(s.xT_ready[u], 1)
                for u in range(2):
                    act.wait_ge(s.gate_ready[u], i + 1)
                    act.activation(sg[u][:, :], bank(gate_bank[u]), ACT.Silu).then_inc(s.silu_done[u], 1)
                for u in range(2):
                    act.wait_ge(s.h_turned[u], i + 1)
                    act.activation(flat(hT[u][:, :, :]), bank(turn_bank[u]), ACT.Copy).then_inc(s.hT_ready[u], 1)

        @block.vector
        def _(dve):
            for u in range(2):
                dve.sem_inc(s.out_taken[u], 1)
                dve.sem_inc(s.y_left[u], 1)
            with dve.Fori(0, n_pairs(dve)) as i:
                for u in range(2):
                    dve.wait_ge(s.x_turned[u], 2 * i + 2)
                    dve.tensor_copy(flat(xeT[u][:, 4:8, :]), bank(x_banks[u][1])).then_inc(s.xT_ready[u], 1)
                for u in range(2):
                    dve.wait_ge(s.silu_done[u], i + 1)
                    dve.wait_ge(s.up_ready[u], i + 2)
                    dve.tensor_tensor(h[u][:, :], sg[u][:, :], bank(up_bank[u]), ALU.mult).then_inc(s.hidden_done[u], 1)
                for u in range(2):
                    dve.wait_ge(s.y_left[u], i + 1)
                    for n in range(2):
                        dve.wait_ge(s.out_ready[u], 2 * i + (n + 2))
                        dve.tensor_copy(ye[u][:, n * 512:(n + 1) * 512], bank(out_banks[u][n])).then_inc(s.out_taken[u], 1)

        @block.gpsimd
        def _(pool):
            with pool.Fori(0, n_pairs(pool)) as i:
                for u in range(2):
                    pool.wait_ge(s.out_taken[u], 2 * i + 3)
                    pool.dma_start(moe.y_rows[bass.ds((2 * i + u) * P, P), :], ye[u][:, :]).then_inc(s.y_stored[u], 16)
                for u in range(2):
                    pool.wait_ge(s.y_stored[u], 16 * i + 16)
                    pool.sem_inc(s.y_left[u], 1)


def combine_experts(nc, m, x, moe):
    with Tensors(nc) as sb, stage(nc, "fetched*8", "scaled", "added") as (block, s):
        rows = sb("expert_rows", [P, 2 * TT, D])

        @block.gpsimd
        def _(pool):
            for n in range(2 * TT):
                pool.indirect_dma_start(out=rows[:, n, :], out_offset=None, in_=moe.y_rows,
                                        in_offset=bass.IndirectOffsetOnAxis(ap=moe.slot[:, n:n + 1], axis=0)).then_inc(s.fetched[n], 16)

        @block.vector
        def _(dve):
            for t in range(TT):
                dve.tensor_scalar(x[:, t, :], x[:, t, :], ALPHA, None, ALU.mult).then_inc(s.scaled, 1)
            dve.wait_ge(s.scaled, TT)
            for i in range(2):
                for t in range(TT):
                    if i:
                        dve.wait_ge(s.added, t + 1)
                    dve.wait_ge(s.fetched[2 * t + i], 16)
                    dve.scalar_tensor_tensor(out=x[:, t, :], in0=rows[:, 2 * t + i, :], scalar=moe.share[:, t, i:i + 1],
                                             in1=x[:, t, :], op0=ALU.mult, op1=ALU.add).then_inc(s.added, 1)


def second_layer(nc, m, a, x, layer, cos, sin, memT, moe):
    w = a["w_in_2"][layer]
    init = 0.8 - 0.6 * float(np.exp(-0.3 * layer))

    def job(name, chunks, width, kind, take):
        return dict(w=w, col=IN2[name], chunks=chunks, width=width, kind=kind, take=take)

    with Tensors(nc) as sb:
        xT = columns_pair(sb, "x_cols", DK, SEQ)
        fetch_ahead(nc, m, job_pieces(job("cb", 1, 512, "T", None)))
        to_columns(nc, m, x, TT, None, None, xT)
        with Tensors(nc) as sb0:
            ybT = [sb0("attn_T", [P, 8, SEQ]), sb0("conv_T", [P, 4, SEQ]), sb0("mem_T", [P, 4, SEQ])]
            with Tensors(nc) as sb1:
                cb, cc, cu = (sb1(n, [P, 4, SEQ]) for n in ("cb", "cc", "cu"))
                qmT = sb1("qmT", [P, 4, SEQ])
                kmT = sb1("kmT", [P, 4, N_MEM])
                vm = sb1("vm", [P, MT, 512])
                y = sb1("y_rows", [P, TT, 512])
                projection(nc, m, xT, [
                    job("cb", 1, 512, "T", take_T(cb)),
                    job("cc", 1, 512, "T", take_T(cc)),
                    job("cu", 1, 512, "T", take_T(cu)),
                    job("qm", 1, 512, "T", take_T(qmT)),
                ] + memory_kv(memT, a["w_mem_kv_2"][layer], 512, kmT, vm), ahead=True)
                gated_conv(nc, m, cb, cc, cu, m.col["conv_w_2"][:, 12 * layer:12 * layer + 12], ybT[1])
                memory_attention(nc, m, MEM2_HEADS, MEM2_HD, qmT, kmT, vm, y, 0)
                fetch_ahead(nc, m, job_pieces(job("q", 2, 512, "T", None)))
                to_columns(nc, m, y, TT, [ybT[2][:, k, :] for k in range(4)])
            with Tensors(nc) as sb1:
                qT = sb1("qT", [P, 8, SEQ])
                kT = sb1("kT", [P, 8, SEQ])
                v = sb1("v", [P, TT, D])
                y = sb1("y_rows", [P, TT, D])
                minus_lam = sb1("minus_lam", [P, 1])
                projection(nc, m, xT, [
                    job("q", 2, 512, "T", take_T(qT)),
                    job("k", 2, 512, "T", take_T(kT)),
                    job("v", 2, 512, "N", take_N(v)),
                ], ahead=True)
                rope(nc, m, [qT, kT], cos, sin)
                diff_lambda(nc, m, a, layer, minus_lam)
                diff_attention(nc, m, a, qT, kT, v, minus_lam, y)
                head_norm(nc, m, y, 1.0 - init)
                fetch_ahead(nc, m, [rows_of(w, k0, 4, IN2["gates"], 512) for k0 in (0, 4)])
                to_columns(nc, m, y, TT, [ybT[0][:, k, :] for k in range(DK)], m.col["diff_subln_g_2"][:, layer:layer + 1].broadcast_to([P, DK]))
            mergedT = sb0("merged_T", [P, DK, SEQ])
            merge_branches(nc, m, xT, w[:, IN2["gates"]:], [
                (ybT[0], a["w_br_attn_2"][layer], 8), (ybT[1], a["w_br_conv_2"][layer], 4), (ybT[2], a["w_br_mem_2"][layer], 4)], mergedT)
            output_product(nc, m, [mergedT[:, k, :] for k in range(DK)], a["w_out_2"][layer], x, ALPHA)
        layer_norm_rows(nc, m, x, a["ln1_g_2"][layer:layer + 1, :], a["ln1_b_2"][layer:layer + 1, :])
        to_columns(nc, m, x, TT, [xT.hi[:, k, :] for k in range(DK)])
        route(nc, m, a, xT.hi, x, moe)
    experts(nc, m, a, layer, moe)
    combine_experts(nc, m, x, moe)
    layer_norm_rows(nc, m, x, a["ln2_g_2"][layer:layer + 1, :], a["ln2_b_2"][layer:layer + 1, :])


def final_norm(nc, m, a, x):
    with Tensors(nc) as sb:
        g = sb("final_gain", [P, D])
        normed = sb("normed", [P, TT, D])
        with stage(nc) as (block, s):
            @block.sync
            def _(sp):
                sp.dma_start(g[:, :], a["final_norm"].rearrange("(a n) -> a n", a=1).partition_broadcast(P)).then_inc(m.fetched, 16)
        m.n_fetched += 1
        rms_rows(nc, m, x, TT, normed, NORM_EPS)
        with stage(nc) as (block, s):
            @block.vector
            def _(dve):
                dve.wait_ge(m.fetched, 16 * m.n_fetched)
                for t in range(TT):
                    dve.tensor_tensor(x[:, t, :], normed[:, t, :], g[:, :], ALU.mult)




def constants():
    p = np.arange(P)[:, None]
    dist = (p + 384 - np.arange(SEQ)[None, :]).astype(np.float32)
    seen = dist >= 0
    near = np.where((dist >= 0) & (dist <= 128), dist, BIG)[:, 256:]

    ends = np.arange(32) * CMP_STRIDE + CMP_BLOCK - 1
    past = (np.arange(TT)[None, :, None] * P + p[:, :, None] - ends[None, None, :])
    cmp_ = np.where((past >= 0) & (np.arange(32) < N_CMP), past, BIG)

    rotate = np.zeros((P, P), np.float32)
    for r in range(P):
        rotate[r + 32 if r % 64 < 32 else r - 32, r] = -1.0 if r % 64 < 32 else 1.0

    def alibi(n):
        return np.exp2(-8.0 * np.arange(1, n + 1) / n).astype(np.float32)

    return {
        "ident": np.eye(P, dtype=np.float32),
        "dist_causal": np.where(seen, dist, BIG).astype(np.float32),
        "block_number": np.arange(MAX_BLOCKS, dtype=np.float32).reshape(1, MAX_BLOCKS),
        "before": np.triu(np.ones((P, P), np.float32), 1),
        "mask_causal": np.where(seen, 0.0, -BIG).astype(np.float32),
        "rotate": rotate,
        "rope_freq": np.tile(np.float32(10000.0) ** (-np.arange(0, 64, 2, dtype=np.float32) / np.float32(64)), 4)
        .astype(np.float32).reshape(P, 1),
        "dist_near": np.ascontiguousarray(near.astype(np.float32)),
        "dist_by4": np.where(seen & (dist % 4 == 0), dist, BIG).astype(np.float32),
        "dist_by16": np.where(seen & (dist % 16 == 0), dist, BIG).astype(np.float32),
        "dist_cmp": cmp_.astype(np.float32),
        "sees_any": (np.arange(P)[:, None] >= CMP_BLOCK - 1).astype(np.float32),
        "nsa_slopes": (-alibi(16) * np.float32(NSA_HD ** 0.5)).reshape(1, 16).astype(np.float32),
        "dil_slopes": (-alibi(12) * np.float32(DIL_HD ** 0.5)).reshape(1, 12).astype(np.float32),
    }


def program(nc, a, out):
    with Tensors(nc) as sb, nc.psum_tensor("ps", [P, 8 * BANK], F32) as ps:
        m = Chip()
        m.ps, m.col = ps, {}
        m.fetched, m.n_fetched = nc.alloc_semaphore("pieces_fetched"), 0
        m.ident = sb("ident", [P, P])
        m.columns = sb("columns", [P, 2 * P])
        m.w_slots = [sb("weights", [P, 8, 512]) for _ in range(2)]
        x = sb("x", [P, TT, D])
        with stage(nc, "loaded") as (block, s):
            @block.sync
            def _(sp):
                sp.dma_start(m.ident[:, :], a["ident"]).then_inc(s.loaded, 16)
                sp.dma_start(x[:, :, :], a["x"][0].rearrange("(t p) d -> p t d", p=P)).then_inc(s.loaded, 16)
                sp.wait_ge(s.loaded, 32)
        load_columns(nc, m, a)
        moe = bag(
            x_rows=nc.dram_tensor("expert_x_rows", (MAX_BLOCKS * P, D), F32, kind="Internal").ap(),
            y_rows=nc.dram_tensor("expert_y_rows", (MAX_BLOCKS * P, D), F32, kind="Internal").ap(),
            share=sb("share", [P, TT, 2]), slot=sb("slot", [P, 2 * TT], mybir.dt.uint32),
            block_expert=sb("block_expert", [P, MAX_BLOCKS], I32), n_pairs=sb("n_pairs", [P, 1], I32))
        hawk_layer(nc, m, a, x)
        nsa_layer(nc, m, a, x, moe)
        final_norm(nc, m, a, x)
        m.rotate = sb("rotate", [P, P])
        cos, sin = sb("cos", [P, SEQ]), sb("sin", [P, SEQ])
        memT = columns_pair(sb, "mem2_T", DK, N_MEM)
        with stage(nc, "loaded") as (block, s):
            @block.sync
            def _(sp):
                sp.dma_start(m.rotate[:, :], a["rotate"]).then_inc(s.loaded, 16)
                sp.wait_ge(s.loaded, 16)
        rope_tables(nc, m, a, cos, sin)
        normed_memory(nc, m, a["mem_2"][0], None, memT)
        for layer in range(2):
            second_layer(nc, m, a, x, layer, cos, sin, memT, moe)
        with stage(nc, "stored") as (block, s):
            @block.sync
            def _(sp):
                sp.dma_start(out[0].rearrange("(t p) d -> p t d", p=P), x[:, :, :]).then_inc(s.stored, 16)
                sp.wait_ge(s.stored, 16)


def kernel(**inputs):
    import concourse.bacc as bacc
    from concourse.bass_utils import run_bass_kernel_spmd

    nc = bacc.Bacc("TRN2", target_bir_lowering=False, num_devices=1)
    arrays, aps = {}, {}
    for name, value in {**inputs, **constants()}.items():
        array = np.ascontiguousarray(value)
        arrays[f"in_{name}"] = array
        aps[name] = nc.dram_tensor(f"in_{name}", array.shape, mybir.dt.from_np(array.dtype), kind="ExternalInput").ap()
    out = nc.dram_tensor("out", (1, SEQ, D), F32, kind="ExternalOutput").ap()
    program(nc, aps, out)
    result = run_bass_kernel_spmd(nc, [arrays], core_ids=[0])
    return result.results[0]["out"]
```
